# Optimizing a Trainium2 kernel written in Bass

```python
import jax, jax.numpy as jnp
from jax import lax
import numpy as np

D_MODEL = 1024
BATCH = 1
SEQ = 128
DEPTH = 2
DEC_BATCH = 1
DEC_SEQ = 512
PAST_LEN = 128

GRID_W = 64
HGRN_HEADS = 8
HGRN_DK = 128
HGRN_DV = 128
HGRN_WIDTH = HGRN_HEADS * HGRN_DK
HGRN_CHUNK = 64
ATTN_HEADS = 16
KV_HEADS = 4
HEAD_DIM = 64
ATTN_WIDTH = ATTN_HEADS * HEAD_DIM
KV_WIDTH = KV_HEADS * HEAD_DIM
Q_BLOCK = 128
ATTN_SCALE = HEAD_DIM ** -0.5
ROPE_THETA = 10000.0
PEER_HEADS = 8
PEER_KEY_DIM = 256
PEER_HALF = PEER_KEY_DIM // 2
N_KEYS = 128
N_EXPERTS = N_KEYS * N_KEYS
PEER_TOPK = 16
PEER_BLOCK = 128
DEEPNORM_ALPHA = (2 * DEPTH) ** 0.25
DEEPNORM_BETA = (8 * DEPTH) ** -0.25
EPS = 1e-6
IN_SIZES = (HGRN_WIDTH, HGRN_WIDTH, HGRN_WIDTH, HGRN_WIDTH, HGRN_WIDTH, ATTN_WIDTH, KV_WIDTH, KV_WIDTH, D_MODEL, D_MODEL)
IN_COLS = sum(IN_SIZES)
IN_OFFSETS = tuple(np.cumsum(IN_SIZES)[:-1].tolist())

kernel_name = 'hybrid_hgrn2_gqa_peer_diffusion_step'

def layer_norm(x, g, b):
    xf = x.astype(jnp.float32)
    mu = jnp.mean(xf, axis=-1, keepdims=True)
    var = jnp.mean(jnp.square(xf - mu), axis=-1, keepdims=True)
    return ((xf - mu) * lax.rsqrt(var + EPS)).astype(x.dtype) * g + b

def rms_norm(x, g):
    xf = x.astype(jnp.float32)
    return (xf * lax.rsqrt(jnp.mean(xf * xf, axis=-1, keepdims=True) + EPS)).astype(g.dtype) * g

def axial_rope(x, rows):
    L = x.shape[1]
    row = jnp.broadcast_to(jnp.arange(rows, dtype=jnp.float32)[:, None], (rows, GRID_W)).reshape(L)
    col = jnp.broadcast_to(jnp.arange(GRID_W, dtype=jnp.float32)[None, :], (rows, GRID_W)).reshape(L)
    n_freq = HEAD_DIM // 4
    inv = jnp.power(ROPE_THETA, -jnp.arange(n_freq, dtype=jnp.float32) / n_freq)
    ang = jnp.concatenate([row[:, None] * inv, col[:, None] * inv], axis=-1)
    cos = jnp.cos(ang)[None, :, None, :].astype(x.dtype)
    sin = jnp.sin(ang)[None, :, None, :].astype(x.dtype)
    x1, x2 = x[..., :HEAD_DIM // 2], x[..., HEAD_DIM // 2:]
    return jnp.concatenate([x1 * cos - x2 * sin, x1 * sin + x2 * cos], axis=-1)

def gla_chunk_scan(q, k, v, logf, s0):
    B, L, H, _ = q.shape
    n = L // HGRN_CHUNK

    def chunks(t):
        return jnp.moveaxis(t.astype(jnp.float32).reshape(B, n, HGRN_CHUNK, H, t.shape[-1]), 1, 0)

    mask = jnp.tril(jnp.ones((HGRN_CHUNK, HGRN_CHUNK), dtype=bool))[None, :, :, None, None]

    def step(S, inp):
        qc, kc, vc, gc = inp
        b = jnp.cumsum(gc, axis=1)
        decay = jnp.exp(jnp.where(mask, b[:, :, None] - b[:, None, :], -jnp.inf))
        scores = jnp.einsum('bihd,bjhd,bijhd->bhij', qc, kc, decay)
        o = (jnp.einsum('bhij,bjhv->bihv', scores, vc)
             + jnp.einsum('bihd,bhdv->bihv', qc * jnp.exp(b), S))
        b_last = b[:, -1]
        S = (jnp.exp(b_last)[..., None] * S
             + jnp.einsum('bjhd,bjhv->bhdv', kc * jnp.exp(b_last[:, None] - b), vc))
        return S, o

    S, o = lax.scan(step, s0.astype(jnp.float32), (chunks(q), chunks(k), chunks(v), chunks(logf)))
    o = jnp.moveaxis(o, 0, 1).reshape(B, L, H, v.shape[-1])
    return o, S

def hgrn2_branch(hq, hf_fwd, hf_bwd, hi, hg, lb_fwd, lb_bwd, norm_g, s0_fwd, s0_bwd):
    B, L, _ = hq.shape

    def heads(t):
        return t.reshape(B, L, HGRN_HEADS, -1)

    q = heads(jax.nn.silu(hq))
    v = heads(hi)

    def gates(z, lb):
        z = heads(z).astype(jnp.float32)
        lb = lb.reshape(HGRN_HEADS, HGRN_DK)
        f = lb + (1.0 - lb) * jax.nn.sigmoid(z)
        k = (1.0 - lb) * jax.nn.sigmoid(-z)
        return jnp.log(f), k

    logf_f, k_f = gates(hf_fwd, lb_fwd)
    logf_b, k_b = gates(hf_bwd, lb_bwd)
    o_f, s_f = gla_chunk_scan(q, k_f, v, logf_f, s0_fwd)

    def flip(t):
        return jnp.flip(t, axis=1)

    o_b, s_b = gla_chunk_scan(flip(q), flip(k_b), flip(v), flip(logf_b), s0_bwd)
    o = (o_f + flip(o_b)).astype(hq.dtype)
    o = rms_norm(o, norm_g) * heads(jax.nn.silu(hg))
    return o.reshape(B, L, HGRN_WIDTH), s_f, s_b

def attend(q, k, v):
    B, L, H, hd = q.shape
    nb = L // Q_BLOCK
    G = H // KV_HEADS
    qb = jnp.moveaxis(q.reshape(B, nb, Q_BLOCK, KV_HEADS, G, hd), 1, 0)

    def block(qi):
        s = jnp.einsum('bqkgd,bskd->bkgqs', qi, k).astype(jnp.float32) * ATTN_SCALE
        p = jax.nn.softmax(s, axis=-1).astype(v.dtype)
        return jnp.einsum('bkgqs,bskd->bqkgd', p, v)

    o = lax.map(block, qb)
    return jnp.moveaxis(o, 0, 1).reshape(B, L, H * hd)

def peer_mixer(h, w_query, sub_keys, u_tab, v_tab):
    B, L, D = h.shape
    T = B * L
    x = h.reshape(T, D)
    q = (x @ w_query).reshape(T, PEER_HEADS, 2, PEER_HALF)
    s = jnp.einsum('thpd,hpnd->thpn', q, sub_keys).astype(jnp.float32)
    s_top, i_top = lax.top_k(s, PEER_TOPK)
    cand_s = (s_top[:, :, 0, :, None] + s_top[:, :, 1, None, :]).reshape(T, PEER_HEADS, PEER_TOPK * PEER_TOPK)
    cand_i = (i_top[:, :, 0, :, None] * N_KEYS + i_top[:, :, 1, None, :]).reshape(T, PEER_HEADS, PEER_TOPK * PEER_TOPK)
    best_s, best_pos = lax.top_k(cand_s, PEER_TOPK)
    expert = jnp.take_along_axis(cand_i, best_pos, axis=-1)
    gate = jax.nn.softmax(best_s, axis=-1).astype(h.dtype)
    nb = T // PEER_BLOCK

    def block(args):
        xb, eb, gb = args
        a = jax.nn.gelu(jnp.einsum('td,thkd->thk', xb, u_tab[eb]), approximate=False)
        return jnp.einsum('thk,thkd->td', gb * a, v_tab[eb])

    out = lax.map(block, (x.reshape(nb, PEER_BLOCK, D),
                          expert.reshape(nb, PEER_BLOCK, PEER_HEADS, PEER_TOPK),
                          gate.reshape(nb, PEER_BLOCK, PEER_HEADS, PEER_TOPK)))
    return out.reshape(B, L, D)

def trunk_layer(x, mod, w_in, lb_fwd, lb_bwd, hgrn_norm_g, q_norm_g, k_norm_g, w_branch_rec, w_branch_att,
                w_out, ln1_g, ln1_b, ln2_g, ln2_b, peer_w_query, peer_sub_keys, peer_u, peer_v,
                s0_fwd, s0_bwd, ctx_k, ctx_v):
    B, L, _ = x.shape
    sh1, sc1, g1, sh2, sc2, g2 = jnp.split(mod[:, None, :], 6, axis=-1)
    h = x * (1.0 + sc1) + sh1
    hq, hff, hfb, hi, hg, aq, ak, av, ga, gb = jnp.split(h @ w_in, IN_OFFSETS, axis=-1)
    o_rec, s_f, s_b = hgrn2_branch(hq, hff, hfb, hi, hg, lb_fwd, lb_bwd, hgrn_norm_g, s0_fwd, s0_bwd)
    q = rms_norm(aq.reshape(B, L, ATTN_HEADS, HEAD_DIM), q_norm_g)
    k = rms_norm(ak.reshape(B, L, KV_HEADS, HEAD_DIM), k_norm_g)
    v = av.reshape(B, L, KV_HEADS, HEAD_DIM)
    if ctx_k is None:
        o_att = attend(q, k, v)
    else:
        rows = L // GRID_W
        o_att = attend(axial_rope(q, rows),
                       jnp.concatenate([axial_rope(k, rows), ctx_k], axis=1),
                       jnp.concatenate([v, ctx_v], axis=1))
    y = jax.nn.sigmoid(ga) * (o_rec @ w_branch_rec) + jax.nn.sigmoid(gb) * (o_att @ w_branch_att)
    x = layer_norm(DEEPNORM_ALPHA * x + g1 * (y @ w_out), ln1_g, ln1_b)
    h2 = x * (1.0 + sc2) + sh2
    x = layer_norm(DEEPNORM_ALPHA * x + g2 * peer_mixer(h2, peer_w_query, peer_sub_keys, peer_u, peer_v), ln2_g, ln2_b)
    return x, k, v, jnp.stack([s_f, s_b], axis=1).astype(x.dtype)

def setup_inputs(seed: int = 0) -> dict:
    key = jax.random.key(seed)
    ks = jax.random.split(key, 26)

    def nrm(k, shape, s):
        return jax.random.normal(k, shape, jnp.float32) * s

    D = D_MODEL
    return {
        'x_prompt': nrm(ks[0], (BATCH, SEQ, D), 1.0),
        'x_sample': nrm(ks[1], (DEC_BATCH, DEC_SEQ, D), 1.0),
        'cache_attn_k': nrm(ks[2], (DEC_BATCH, DEPTH, PAST_LEN, KV_HEADS, HEAD_DIM), 1.0),
        'cache_attn_v': nrm(ks[3], (DEC_BATCH, DEPTH, PAST_LEN, KV_HEADS, HEAD_DIM), 1.0),
        'state_hgrn': nrm(ks[4], (DEC_BATCH, DEPTH, 2, HGRN_HEADS, HGRN_DK, HGRN_DV), 0.5),
        'c': nrm(ks[5], (DEC_BATCH, D), 1.0),
        'c_ctx': nrm(ks[6], (D,), 1.0),
        'w_mod': nrm(ks[7], (DEPTH, D, 6 * D), 0.5 * D ** -0.5),
        'b_mod': nrm(ks[8], (DEPTH, 6 * D), 0.02),
        'w_in': nrm(ks[9], (DEPTH, D, IN_COLS), D ** -0.5),
        'hgrn_lb_logits': nrm(ks[10], (2, DEPTH, HGRN_WIDTH), 0.1),
        'hgrn_norm_g': 1.0 + nrm(ks[11], (DEPTH, HGRN_DV), 0.02),
        'q_norm_g': 1.0 + nrm(ks[12], (DEPTH, HEAD_DIM), 0.02),
        'k_norm_g': 1.0 + nrm(ks[13], (DEPTH, HEAD_DIM), 0.02),
        'w_branch_rec': nrm(ks[14], (DEPTH, HGRN_WIDTH, D), HGRN_WIDTH ** -0.5),
        'w_branch_att': nrm(ks[15], (DEPTH, ATTN_WIDTH, D), ATTN_WIDTH ** -0.5),
        'w_out': nrm(ks[16], (DEPTH, D, D), DEEPNORM_BETA * D ** -0.5),
        'ln1_g': 1.0 + nrm(ks[17], (DEPTH, D), 0.02),
        'ln1_b': nrm(ks[18], (DEPTH, D), 0.02),
        'ln2_g': 1.0 + nrm(ks[19], (DEPTH, D), 0.02),
        'ln2_b': nrm(ks[20], (DEPTH, D), 0.02),
        'peer_w_query': nrm(ks[21], (DEPTH, D, PEER_HEADS * PEER_KEY_DIM), D ** -0.5),
        'peer_sub_keys': nrm(ks[22], (DEPTH, PEER_HEADS, 2, N_KEYS, PEER_HALF), PEER_HALF ** -0.5),
        'peer_u': nrm(ks[23], (DEPTH, N_EXPERTS, D), D ** -0.5),
        'peer_v': nrm(ks[24], (DEPTH, N_EXPERTS, D), DEEPNORM_BETA),
    }

def reference(x_prompt, x_sample, cache_attn_k, cache_attn_v, state_hgrn, c, c_ctx, w_mod, b_mod, w_in,
              hgrn_lb_logits, hgrn_norm_g, q_norm_g, k_norm_g, w_branch_rec, w_branch_att, w_out,
              ln1_g, ln1_b, ln2_g, ln2_b, peer_w_query, peer_sub_keys, peer_u, peer_v):
    lb = jnp.cumsum(jax.nn.softmax(hgrn_lb_logits.astype(jnp.float32), axis=1), axis=1)
    lb = lb - lb[:, :1]
    zero_state = jnp.zeros((x_prompt.shape[0], HGRN_HEADS, HGRN_DK, HGRN_DV), jnp.float32)
    silu_ctx = jax.nn.silu(c_ctx)[None, :]
    silu_c = jax.nn.silu(c)
    xp, xs = x_prompt, x_sample
    new_k, new_v, new_s = [], [], []
    for l in range(DEPTH):
        shared = (w_in[l], lb[0, l], lb[1, l], hgrn_norm_g[l], q_norm_g[l], k_norm_g[l], w_branch_rec[l],
                  w_branch_att[l], w_out[l], ln1_g[l], ln1_b[l], ln2_g[l], ln2_b[l], peer_w_query[l],
                  peer_sub_keys[l], peer_u[l], peer_v[l])
        xp, k_l, v_l, s_l = trunk_layer(xp, silu_ctx @ w_mod[l] + b_mod[l], *shared,
                                        zero_state, zero_state, None, None)
        new_k.append(k_l)
        new_v.append(v_l)
        new_s.append(s_l)
        xs, _, _, _ = trunk_layer(xs, silu_c @ w_mod[l] + b_mod[l], *shared,
                                  state_hgrn[:, l, 0], state_hgrn[:, l, 1],
                                  cache_attn_k[:, l], cache_attn_v[:, l])
    return (xp, xs, jnp.stack(new_k, axis=1), jnp.stack(new_v, axis=1), jnp.stack(new_s, axis=1))


_drawn_inputs = setup_inputs


def setup_inputs(seed=0):
    import zlib

    import numpy as np

    out = dict(_drawn_inputs(seed))
    spreads = {}
    factors = {'cache_attn_k': 8.0,
     'cache_attn_v': 8.0,
     'state_hgrn': 8.0,
     'hgrn_norm_g': 8.0,
     'q_norm_g': 8.0,
     'k_norm_g': 7.553}
    for name, (base, spread) in spreads.items():
        noise = np.random.default_rng([zlib.crc32(name.encode()), seed]).standard_normal(out[name].shape)
        drawn = base * np.exp(spread * noise) if base else spread * noise
        out[name] = __import__('jax').numpy.asarray(drawn.astype(out[name].dtype))
    for name, factor in factors.items():
        out[name] = (out[name] * factor).astype(out[name].dtype)
    return out
```

```python
from contextlib import ExitStack

import numpy as np

import concourse.bass as bass
from concourse import mybir

F32 = mybir.dt.float32
U32 = mybir.dt.uint32
U8 = mybir.dt.uint8
ALU = mybir.AluOpType
ACT = mybir.ActivationFunctionType
AX = mybir.AxisListType

P = 128
DEPTH = 2
D = 1024
KD = D // P
NT = 5
T = NT * P
LAT = T - P
HALF = T // 2
HEADS = 8
KV = 4
HD = 64
QH = 16
GROUP = QH // KV
GRID_W = 64
PEER_H = 8
TOPK = 16
SLOTS = PEER_H * TOPK
NKEYS = 128
N_EXPERTS = NKEYS * NKEYS
CB = 512
ALPHA = float((2 * DEPTH) ** 0.25)
EPS = 1e-6
SCALE = HD ** -0.5
LOG_FLOOR = 2.0 ** -62
LEVELS = [64, 32, 16, 8, 4, 2, 1]
NL = len(LEVELS)
ROWS = 8
TURNS = SLOTS // ROWS
TURNS_A = 5
ALL_ROWS = tuple(range(ROWS))
PE_ROWS = (0, 2, 4, 6)
DIAGS = 4
STAGED = 2
B_MOD, B_GATE, B_HEAD, B_KV, B_Q, B_MIX, B_OUT, B_SK, B_PQ = 0, 12, 14, 22, 23, 25, 33, 35, 36
NB = 40
SH1, SC1, G1, SH2, SC2, G2 = range(6)


def build(nc, ins, outs):
    with ExitStack() as ctx:
        def sb(name, shape, dt=F32):
            return ctx.enter_context(nc.sbuf_tensor(name, shape, dt))

        def sem(name):
            return ctx.enter_context(nc.semaphore(name))

        x = sb("x", [P, NT, D])
        ring = sb("ring", [P, 2, KD, CB])
        ident = sb("ident", [P, P])
        cos = sb("cos", [P, NT - 1, 32])
        sin = sb("sin", [P, NT - 1, 32])
        reset = sb("reset", [P, NT * 129])
        iota = sb("iota", [P, TOPK])
        masks = sb("masks", [P, 2 * NL + 1, P], U8)
        bmod = sb("bmod", [P, DEPTH, 48])
        modv = sb("modv", [P, 48, 2])
        cond = sb("cond", [P, KD, 2])
        rows_g = sb("rows_g", [P, DEPTH, P + 2 * HD])
        lbz = sb("lbz", [P, 2, DEPTH, HEADS])
        lbf = sb("lbf", [P, DEPTH * 2 * HEADS])
        omlb = sb("omlb", [P, DEPTH * 2 * HEADS])
        small = sb("small", [P, 256])
        layer_base = sb("layer_base", [P, 1])
        hT = sb("hT", [P, KD, T])
        late = sb("late", [P, 8192])
        arena = sb("arena", [P, 23552])
        banks = ctx.enter_context(nc.psum_tensor("banks", [P, 8, 512], F32))

        def pair(b, n=T):
            return banks[:, b:b + 2, :].rearrange("p a n -> p (a n)")[:, 0:n]

        def halves(b):
            return banks[:, b:b + 2, 0:HALF]

        class Region:
            def __init__(self, base, at=0):
                self.base, self.at = base, at

            def take(self, n):
                self.at += n
                assert self.at <= self.base.shape[1], (self.at, self.base.shape)
                return self.base[:, self.at - n:self.at]

        def r3(ap, b):
            return ap.rearrange("p (a b) -> p a b", b=b)

        sgate = r3(arena[:, 0:5120], D)
        orecT = r3(arena[:, 5120:10240], T)
        reg = Region(arena, 10240)
        hq, hv, hk0, hk1, ksum, sc = (reg.take(T) for _ in range(6))
        hk = [hk0, hk1]
        sig = [reg.take(T) for _ in range(2)]
        gl = [r3(reg.take(NT * 129), 129) for _ in range(2)]
        pre = [r3(reg.take(NT * 129), 129) for _ in range(2)]
        E = [reg.take(T) for _ in range(2)]
        X = [reg.take(T) for _ in range(2)]
        qdec = [reg.take(T) for _ in range(2)]
        reg2 = Region(late)
        kdT = [reg2.take(T) for _ in range(2)]
        S = [r3(reg2.take(4 * P), P) for _ in range(2)]
        hnew = r3(reg2.take(2 * P), P)
        o1 = reg2.take(T)
        osq = reg2.take(T)
        tot = r3(reg2.take(2 * NT), NT)
        oattT = r3(arena[:, 0:5120], T)
        reg = Region(arena, 10240)
        qkv = r3(reg.take(NT * 1536), 1536)
        KT = r3(reg.take(2 * 768), 768)
        kpast = reg.take(256)
        vpast = reg.take(256)
        qstage = r3(reg.take(T), P)
        qTs = reg.take(T)
        pr = [reg.take(T) for _ in range(2)]
        PTc = [reg.take(P) for _ in range(2)]
        reg2 = Region(late)
        PT = [r3(reg2.take(NT * LAT), LAT) for _ in range(2)]
        nt1 = reg2.take(1280)
        nt2 = reg2.take(1280)
        yT = r3(arena[:, 10240:15360], T)
        reg = Region(arena, 15360)
        sgA = [reg.take(HALF) for _ in range(2)]
        sgB = [reg.take(HALF) for _ in range(2)]
        y1 = reg.take(HALF)
        y2 = reg.take(HALF)
        lnrows = r3(late[:, 0:4096], D)
        bca = r3(late[:, 4096:6144], D)
        skT = r3(late[:, 6144:8192], P)
        bcb = r3(arena[:, 0:4096], D)
        outtmp = arena[:, 15360:15872]
        h2 = r3(arena[:, 15360:20480], D)
        scores = arena[:, 0:10240].rearrange("p (t u n) -> p t u n", t=NT, n=NKEYS)
        qT = r3(arena[:, 10240:10240 + 4 * T], T)
        stage = arena[:, 10240:12288]
        work = arena[:, 12288:14336]
        reg = Region(late, 6144)
        tv = r3(reg.take(256), TOPK)
        ti = r3(reg.take(256), TOPK)
        tif = r3(reg.take(256), TOPK)
        bs, bp, bq, paf, pbf, e1, e2, av, gate = (reg.take(SLOTS) for _ in range(9))
        wv = reg.take(SLOTS)
        gsum, idxs = small[:, 232:240], small[:, 240:248]
        diag = [arena[:, 256 + j * P:256 + (j + 1) * P] for j in range(DIAGS)]
        hTf = hT[:, :, :].rearrange("p k t -> p (k t)")
        grow = [hTf[:, j * D:(j + 1) * D] for j in range(5)] + \
               [arena[:, 20480 + j * D:20480 + (j + 1) * D] for j in range(3)]
        acc = arena[:, 14336:15360]

        init = sem("init")
        cond_ready = sem("cond_ready")
        lb_shifted, lb_exped, lb_ready = sem("lb_shifted"), sem("lb_exped"), sem("lb_ready")
        w_full = [sem(f"w_full{s}") for s in range(2)]
        w_free = [sem(f"w_free{s}") for s in range(2)]
        bank_free = [sem(f"bank_free{b}") for b in range(8)]
        to_act = [sem(f"to_act{b}") for b in range(8)]
        to_dve = [sem(f"to_dve{b}") for b in range(8)]
        left = {e: sem(f"left_{e}") for e in ("pe", "act", "dve")}
        enter = {e: sem(f"enter_{e}") for e in ("pe", "act", "dve")}
        heads_set = sem("heads_set")
        s0_full = sem("s0_full")
        kneg_ready, log_ready, pre_ready = sem("kneg_ready"), sem("log_ready"), sem("pre_ready")
        v_ready, ksum_ready, tot_ready = sem("v_ready"), sem("ksum_ready"), sem("tot_ready")
        dif_ready = [sem(f"dif_ready{b}") for b in range(2)]
        exp_ready = [sem(f"exp_ready{b}") for b in range(2)]
        e_free = [sem(f"e_free{b}") for b in range(2)]
        x_ready = [sem(f"x_ready{b}") for b in range(2)]
        kdt_ready, sc_ready, state_ready = sem("kdt_ready"), sem("sc_ready"), sem("state_ready")
        hnew_ready, hnew_sent = sem("hnew_ready"), sem("hnew_sent")
        osq_ready, ms_ready, rms_ready = sem("osq_ready"), sem("ms_ready"), sem("rms_ready")
        o1_ready = sem("o1_ready")
        qkv_ready, past_full = sem("qkv_ready"), sem("past_full")
        qkn_pool, qkn_pe, qkn_act = sem("qkn_pool"), sem("qkn_pe"), sem("qkn_act")
        kvnew_sent, kt_ready = sem("kvnew_sent"), sem("kt_ready")
        qst_ready, qst_free, qts_ready = sem("qst_ready"), sem("qst_free"), sem("qts_ready")
        max_ready = [sem(f"max_ready{b}") for b in range(2)]
        prob_raw = [sem(f"prob_raw{b}") for b in range(2)]
        prob_ready = [sem(f"prob_ready{b}") for b in range(2)]
        pt_ready = [sem(f"pt_ready{b}") for b in range(2)]
        pt_free = [sem(f"pt_free{b}") for b in range(2)]
        sg_ready = [sem(f"sg_ready{b}") for b in range(2)]
        sg_free = [sem(f"sg_free{b}") for b in range(2)]
        bc_ready, ln_full = sem("bc_ready"), sem("ln_full")
        var_ready, std_ready = sem("var_ready"), sem("std_ready")
        h2_ready, h2T_ready = sem("h2_ready"), sem("h2T_ready")
        sk_arrived, sk_ready, qt_ready = sem("sk_arrived"), sem("sk_ready"), sem("qt_ready")
        stage_ready, stage_free = sem("stage_ready"), sem("stage_free")
        softexp_ready = sem("softexp_ready")
        idx_ready, idx_staged = sem("idx_ready"), sem("idx_staged")
        row_full = [sem(f"row_full{j}") for j in range(ROWS)]
        row_free = [sem(f"row_free{j}") for j in range(ROWS)]
        dots_ready, gelu_ready, wv_ready = sem("dots_ready"), sem("gelu_ready"), sem("wv_ready")
        acc_zero, acc_seen, acc_done = sem("acc_zero"), sem("acc_seen"), sem("acc_done")
        acc_free = sem("acc_free")
        diag_ready, diag_used = sem("diag_ready"), sem("diag_used")
        done, stored = sem("done"), sem("stored")

        def phase_barrier(eng, me):
            if me == "pool":
                for other in left:
                    eng.wait_ge(left[other], 1)
                    eng.sem_inc(left[other], -1)
                for other in left:
                    eng.drain().then_inc(enter[other], 1)
            else:
                eng.drain().then_inc(left[me], 1)
                eng.wait_ge(enter[me], 1)
                eng.sem_inc(enter[me], -1)

        INIT = 16 * 14
        units = [(d, s) for s in LEVELS for d in range(2)]

        block = ctx.enter_context(nc.Block())

        @block.sync
        def _(sp):
            with sp.Fori(0, DEPTH * NB // 2) as i:
                for s in range(2):
                    sp.wait_ge(w_free[s], 1)
                    sp.sem_inc(w_free[s], -1)
                    sp.dma_start(ring[:, s].rearrange("p k n -> p (k n)"),
                                 ins["wblk"][bass.ds(2 * i + s, 1)].rearrange("a p n -> p (a n)")
                                 ).then_inc(w_full[s], 16)
            sp.wait_ge(done, 1)
            sp.dma_start(outs[0][0], x[:, 0, :]).then_inc(stored, 16)
            sp.dma_start(outs[1][0].rearrange("(t p) d -> p t d", p=P), x[:, 1:NT, :]
                         ).then_inc(stored, 16)
            sp.wait_ge(stored, 32)

        @block.gpsimd
        def _(pool):
            for s in w_free + e_free + pt_free + sg_free + row_free + bank_free \
                    + [qst_free, acc_free]:
                pool.sem_inc(s, 1)
            pool.sem_inc(hnew_sent, 32)
            pool.sem_inc(diag_used, DIAGS - 1)
            nc.gpsimd.memset(layer_base[:], 0.0)
            pool.wait_ge(init, INIT)
            with pool.Fori(0, DEPTH) as l:
                phase_barrier(pool, "pool")
                phase_barrier(pool, "pool")
                phase_barrier(pool, "pool")
                for d in range(2):
                    nc.gpsimd.memset(gl[d][:, :, 0:1], 0.0)
                pool.drain().then_inc(heads_set, 1)
                with pool.Fori(0, HEADS) as h:
                    pool.wait_ge(pre_ready, 2)
                    pool.sem_inc(pre_ready, -2)
                    for n, (d, s) in enumerate(units):
                        base = pre[d][:, :, 1 - d:129 - d]
                        base = base.rearrange("p t (b s) -> p t b s", s=2 * s)
                        ref = pre[d][:, :, 0:128].rearrange("p t (b s) -> p t b s", s=2 * s)[:, :, :, s:s + 1]
                        pool.wait_ge(e_free[n % 2], 1)
                        pool.sem_inc(e_free[n % 2], -1)
                        nc.gpsimd.tensor_tensor(
                            E[n % 2].rearrange("p (t b s) -> p t b s", t=NT, s=2 * s), base,
                            ref.to_broadcast([P, NT, P // (2 * s), 2 * s]), ALU.subtract
                        ).then_inc(dif_ready[n % 2], 1)
                    for n, (d, to_end) in enumerate([(0, 0), (0, 1), (1, 1), (1, 0)]):
                        base = pre[d][:, :, 1 - d:129 - d]
                        ref = pre[d][:, :, 128 * to_end:128 * to_end + 1].to_broadcast([P, NT, P])
                        pool.wait_ge(e_free[n % 2], 1)
                        pool.sem_inc(e_free[n % 2], -1)
                        nc.gpsimd.tensor_tensor(r3(E[n % 2], P), base, ref, ALU.subtract
                                                ).then_inc(dif_ready[n % 2], 1)
                phase_barrier(pool, "pool")
                pool.wait_ge(qkn_pool, 1)
                pool.sem_inc(qkn_pool, -1)
                for kp in range(2):
                    with pool.Fori(0, 4) as i:
                        pool.wait_ge(qst_free, 1)
                        pool.sem_inc(qst_free, -1)
                        nc.gpsimd.tensor_copy(qstage, qkv[:, :, bass.ds((kp * 4 + i) * P, P)]
                                              ).then_inc(qst_ready, 1)
                phase_barrier(pool, "pool")
                phase_barrier(pool, "pool")
                phase_barrier(pool, "pool")
                pool.wait_ge(sk_arrived, 1)
                pool.sem_inc(sk_arrived, -1)
                nc.gpsimd.tensor_copy(skT, ring[:, B_SK % 2].rearrange("p k (a n) -> p (k a) n", n=NKEYS)[:, 0:16])
                pool.drain().then_inc(sk_ready, 1)
                pool.drain().then_inc(w_free[B_SK % 2], 1)
                phase_barrier(pool, "pool")
                with pool.Fori(0, NT) as t:
                    pool.wait_ge(idx_ready, 1)
                    pool.sem_inc(idx_ready, -1)
                    for table in ("peer_u", "peer_v"):
                        with pool.Fori(0, SLOTS // ROWS) as i:
                            for r in range(0, ROWS, STAGED):
                                for j in range(r, r + STAGED):
                                    pool.wait_ge(row_free[j], 1)
                                    pool.sem_inc(row_free[j], -1)
                                nc.gpsimd.tensor_copy(
                                    idxs[:, r:r + STAGED].bitcast(U32),
                                    arena[:, bass.ds(t * 2048 + i * ROWS + r, STAGED)].bitcast(U32)
                                ).then_inc(idx_staged, 1)
                                pool.wait_ge(idx_staged, 1)
                                pool.sem_inc(idx_staged, -1)
                                for j in range(r, r + STAGED):
                                    nc.gpsimd.indirect_dma_start(
                                        grow[j], None, ins[table],
                                        bass.IndirectOffsetOnAxis(ap=idxs[:, j:j + 1].bitcast(U32), axis=0)
                                    ).then_inc(row_full[j], 16)
                phase_barrier(pool, "pool")
                phase_barrier(pool, "pool")

        @block.scalar
        def _(act):
            loads = [(x[:, 0, :], ins["x_prompt"]),
                     (x[:, 1:NT, :], ins["x_sample"].rearrange("(t p) d -> p t d", p=P)),
                     (cond[:], ins["cond"]), (bmod[:], ins["bmod"]), (lbz[:], ins["lbz"]),
                     (ident[:], ins["ident"]), (cos[:], ins["cos"]), (sin[:], ins["sin"]),
                     (iota[:], ins["iota"]), (arena[:, 0:(2 * NL + 1) * P], ins["masks"]), (reset[:], ins["reset"])]
            for dst, src in loads:
                act.dma_start(dst, src).then_inc(init, 16)
            for n, (a, b) in enumerate([(0, P), (P, P + HD), (P + HD, P + 2 * HD)]):
                act.dma_start(rows_g[:, :, a:b], ins[("hgrn_norm_g", "q_norm_g", "k_norm_g")[n]]
                              .partition_broadcast(P)).then_inc(init, 16)
            act.wait_ge(init, INIT)
            nc.scalar.activation(cond[:], cond[:], ACT.Silu).then_inc(cond_ready, 1)
            act.wait_ge(lb_shifted, 1)
            nc.scalar.activation(lbz[:], lbz[:], ACT.Exp).then_inc(lb_exped, 1)
            act.wait_ge(lb_ready, 1)

            def square_root(n):
                act.wait_ge(var_ready, 1)
                act.sem_inc(var_ready, -1)
                nc.scalar.activation(small[:, 0:n], small[:, 0:n], ACT.Sqrt).then_inc(std_ready, 1)

            with act.Fori(0, DEPTH) as l:
                phase_barrier(act, "act")
                for k in range(KD):
                    b = 4 + k % 4
                    act.wait_ge(to_act[b], 1)
                    act.sem_inc(to_act[b], -1)
                    nc.scalar.activation(hT[:, k, 0:P], banks[:, b, 0:P], ACT.Identity,
                                         bias=modv[:, SH1 * 8 + k, 0:1], scale=modv[:, SC1 * 8 + k, 0:1]
                                         ).then_inc(bank_free[b], 1)
                phase_barrier(act, "act")
                for g in range(2 * NT):
                    b = g % 8
                    act.wait_ge(to_act[b], 1)
                    act.sem_inc(to_act[b], -1)
                    nc.scalar.activation(sgate[:, g % NT, g // NT * CB:(g // NT + 1) * CB], banks[:, b, :],
                                         ACT.Silu).then_inc(bank_free[b], 1)
                phase_barrier(act, "act")
                act.wait_ge(heads_set, 1)
                act.sem_inc(heads_set, -1)
                with act.Fori(0, HEADS) as h:
                    for d in range(2):
                        act.dma_start(S[d][:, 3 * d, :], ins["state"][bass.ds((l * 2 + d) * HEADS + h, 1)]
                                      .rearrange("a p n -> p (a n)")).then_inc(s0_full, 16)
                    act.wait_ge(to_act[0], 1)
                    act.sem_inc(to_act[0], -1)
                    nc.scalar.activation(hq.rearrange("p (a n) -> p a n", a=2), halves(0), ACT.Silu
                                         ).then_inc(bank_free[0], 1)
                    for d in range(2):
                        b = 2 + 2 * d
                        act.wait_ge(to_act[b], 1)
                        act.sem_inc(to_act[b], -1)
                        nc.scalar.activation(hk[d].rearrange("p (a n) -> p a n", a=2), halves(b), ACT.Sigmoid,
                                             scale=-1.0).then_inc(kneg_ready, 1)
                        nc.scalar.activation(sig[d].rearrange("p (a n) -> p a n", a=2), halves(b), ACT.Sigmoid
                                             ).then_inc(bank_free[b], 1)
                    act.wait_ge(to_act[6], 1)
                    act.sem_inc(to_act[6], -1)
                    nc.scalar.copy(hv, pair(6)).then_inc(bank_free[6], 1)
                    act.drain().then_inc(v_ready, 1)
                    for d in range(2):
                        c = bass.ds((l * 2 + d) * HEADS + h, 1)
                        nc.scalar.activation(gl[d][:, :, 1:129], r3(sig[d], P), ACT.Ln,
                                             bias=lbf[:, c], scale=omlb[:, c]).then_inc(log_ready, 1)
                    for n, (d, s) in enumerate(units):
                        act.wait_ge(dif_ready[n % 2], 1)
                        act.sem_inc(dif_ready[n % 2], -1)
                        e = E[n % 2].rearrange("p (b s) -> p b s", s=2 * s)
                        nc.scalar.activation(e[:, :, 0:s], e[:, :, 0:s], ACT.Exp, scale=-1.0)
                        nc.scalar.activation(e[:, :, s:2 * s], e[:, :, s:2 * s], ACT.Exp
                                             ).then_inc(exp_ready[n % 2], 1)
                    for n, sign in enumerate([1.0, -1.0, -1.0, 1.0]):
                        act.wait_ge(dif_ready[n % 2], 1)
                        act.sem_inc(dif_ready[n % 2], -1)
                        nc.scalar.activation(E[n % 2], E[n % 2], ACT.Exp, scale=sign
                                             ).then_inc(exp_ready[n % 2], 1)
                    for d in range(2):
                        nc.scalar.activation(tot[:, d, :], pre[d][:, :, 128:129].rearrange("p t a -> p (t a)"),
                                             ACT.Exp).then_inc(tot_ready, 1)
                    for d in range(2):
                        act.wait_ge(to_act[4 + 2 * d], 1)
                        act.sem_inc(to_act[4 + 2 * d], -1)
                        nc.scalar.copy(kdT[d], pair(4 + 2 * d)).then_inc(bank_free[4 + 2 * d], 1)
                        act.drain().then_inc(kdt_ready, 1)
                    act.wait_ge(hnew_ready, 1)
                    act.sem_inc(hnew_ready, -1)
                    for d in range(2):
                        act.dma_start(outs[4][bass.ds((l * 2 + d) * HEADS + h, 1)].rearrange("a p n -> p (a n)"),
                                      hnew[:, d, :]).then_inc(hnew_sent, 16)
                    act.wait_ge(to_act[4], 1)
                    act.sem_inc(to_act[4], -1)
                    nc.scalar.activation(osq, pair(4), ACT.Square).then_inc(osq_ready, 1)
                    square_root(NT)
                    act.wait_ge(to_act[6], 1)
                    act.sem_inc(to_act[6], -1)
                    nc.scalar.copy(orecT[:, bass.ds(h, 1), :].rearrange("p a n -> p (a n)"), pair(6)
                                   ).then_inc(bank_free[6], 1)
                phase_barrier(act, "act")
                act.dma_start(kpast, ins["cache_k"][bass.ds(l, 1)].rearrange("a p n -> p (a n)")).then_inc(past_full, 16)
                act.dma_start(vpast, ins["cache_v"][bass.ds(l, 1)].rearrange("a p n -> p (a n)")).then_inc(past_full, 16)
                for g in range(3 * NT):
                    b = g % 8
                    c = (1024, 0, 512)[g // NT]
                    act.wait_ge(to_act[b], 1)
                    act.sem_inc(to_act[b], -1)
                    nc.scalar.copy(qkv[:, g % NT, c:c + CB], banks[:, b, :]).then_inc(bank_free[b], 1)
                act.drain().then_inc(qkv_ready, 1)
                square_root(NT * 20)
                act.wait_ge(qkn_act, 1)
                act.sem_inc(qkn_act, -1)
                for n in range(2):
                    act.dma_start(outs[2 + n][bass.ds(l, 1)].rearrange("a p n -> p (a n)"),
                                  qkv[:, 0, 1024 + 256 * n:1280 + 256 * n]).then_inc(kvnew_sent, 16)
                for kp in range(2):
                    act.wait_ge(to_act[2 * kp], 1)
                    act.sem_inc(to_act[2 * kp], -1)
                    nc.scalar.copy(KT[:, kp, :], pair(2 * kp, 768)).then_inc(bank_free[2 * kp], 1)
                    act.drain().then_inc(kt_ready, 1)
                for kp in range(2):
                    with act.Fori(0, 4) as i:
                        act.wait_ge(to_act[6], 1)
                        act.sem_inc(to_act[6], -1)
                        nc.scalar.copy(qTs, pair(6)).then_inc(bank_free[6], 1)
                        act.drain().then_inc(qts_ready, 1)

                        def probs(u):
                            n = P if u % NT == 0 else T
                            act.wait_ge(max_ready[u % 2], 1)
                            act.sem_inc(max_ready[u % 2], -1)
                            nc.scalar.activation(pr[u % 2][:, 0:n], pair(2 * (u % 2), n), ACT.Exp,
                                                 bias=small[:, 128 + u % 2:129 + u % 2], scale=SCALE,
                                                 accum_out=small[:, 130 + u % 2:131 + u % 2]
                                                 ).then_inc(prob_raw[u % 2], 1)
                            act.drain().then_inc(bank_free[2 * (u % 2)], 1)

                        def evacuate(u):
                            half, qt = divmod(u, NT)
                            act.wait_ge(to_act[4], 1)
                            act.sem_inc(to_act[4], -1)
                            if qt == 0:
                                act.wait_ge(pt_free[half], 1)
                                act.sem_inc(pt_free[half], -1)
                                nc.scalar.copy(PTc[half], banks[:, 4, 0:P]).then_inc(bank_free[4], 1)
                            else:
                                nc.scalar.copy(PT[half][:, :, (qt - 1) * P:qt * P], r3(pair(4), P)
                                               ).then_inc(bank_free[4], 1)
                            if qt == NT - 1:
                                act.drain().then_inc(pt_ready[half], 1)

                        for u in range(2 * NT):
                            probs(u)
                            if u:
                                evacuate(u - 1)
                        evacuate(2 * NT - 1)
                        act.wait_ge(to_act[6], 1)
                        act.sem_inc(to_act[6], -1)
                        nc.scalar.copy(oattT[:, bass.ds(kp * 4 + i, 1), 0:P].rearrange("p a n -> p (a n)"),
                                       banks[:, 7, 0:P])
                        nc.scalar.copy(oattT[:, bass.ds(kp * 4 + i, 1), P:T].rearrange("p a n -> p (a n)"),
                                       banks[:, 6, :]).then_inc(bank_free[6], 1)
                act.wait_ge(kvnew_sent, 32)
                act.sem_inc(kvnew_sent, -32)
                phase_barrier(act, "act")
                with act.Fori(0, KD):
                    for f in range(2):
                        act.wait_ge(sg_free[f], 1)
                        act.sem_inc(sg_free[f], -1)
                        act.wait_ge(to_act[4 * f], 1)
                        act.sem_inc(to_act[4 * f], -1)
                        nc.scalar.activation(sgA[f], banks[:, 4 * f, 0:HALF], ACT.Sigmoid
                                             ).then_inc(bank_free[4 * f], 1)
                        act.wait_ge(to_act[4 * f + 1], 1)
                        act.sem_inc(to_act[4 * f + 1], -1)
                        nc.scalar.activation(sgB[f], banks[:, 4 * f + 1, 0:HALF], ACT.Sigmoid
                                             ).then_inc(bank_free[4 * f + 1], 1)
                        act.drain().then_inc(sg_ready[f], 1)
                phase_barrier(act, "act")
                act.dma_start(lnrows, ins["lnrows"][bass.ds(l, 1)].rearrange("a r n -> (a r) n")
                              .partition_broadcast(P)).then_inc(ln_full, 16)
                for v, dst in enumerate([bca[:, 0], bca[:, 1], bcb[:, 0], bcb[:, 1], bcb[:, 2], bcb[:, 3]]):
                    b = 2 * (v % 4)
                    act.wait_ge(to_act[b], 1)
                    act.sem_inc(to_act[b], -1)
                    nc.scalar.copy(dst, pair(b, D)).then_inc(bank_free[b], 1)
                act.drain().then_inc(bc_ready, 1)
                square_root(NT)
                phase_barrier(act, "act")
                for t in range(NT):
                    b = 2 * (t % 4)
                    act.wait_ge(to_act[b], 1)
                    act.sem_inc(to_act[b], -1)
                    nc.scalar.copy(hT[:, :, t * P:(t + 1) * P], r3(pair(b, D), P)).then_inc(bank_free[b], 1)
                    act.drain().then_inc(h2T_ready, 1)
                with act.Fori(0, 4):
                    for u in range(4):
                        b = 2 * (u % 2)
                        act.wait_ge(to_act[b], 1)
                        act.sem_inc(to_act[b], -1)
                        nc.scalar.copy(qT[:, u, :].rearrange("p (a n) -> p a n", a=2), halves(b)
                                       ).then_inc(bank_free[b], 1)
                        act.drain().then_inc(qt_ready, 1)
                phase_barrier(act, "act")
                for c in range(2):
                    act.wait_ge(to_act[2 * c], 1)
                    act.sem_inc(to_act[2 * c], -1)
                    nc.scalar.copy(bca[:, c], pair(2 * c, D)).then_inc(bank_free[2 * c], 1)
                nc.scalar.copy(stage, arena[:, 0:2048]).then_inc(stage_ready, 1)

                def peer_act(t, more):
                    act.wait_ge(dots_ready, 1)
                    act.sem_inc(dots_ready, -1)
                    nc.scalar.activation(gate, gate, ACT.Exp).then_inc(softexp_ready, 1)
                    nc.scalar.activation(av, av, ACT.Gelu).then_inc(gelu_ready, 1)
                    if more:
                        act.wait_ge(stage_free, 1)
                        act.sem_inc(stage_free, -1)
                        nc.scalar.copy(stage, arena[:, bass.ds((t + 1) * 2048, 2048)]).then_inc(stage_ready, 1)
                    act.wait_ge(wv_ready, 1)
                    act.sem_inc(wv_ready, -1)
                    for first, count, mine in ((0, TURNS_A, ALL_ROWS), (TURNS_A, TURNS - TURNS_A, PE_ROWS)):
                        with act.Fori(0, count) as i:
                            for n, j in enumerate(mine):
                                act.wait_ge(diag_used, 1)
                                act.sem_inc(diag_used, -1)
                                nc.scalar.activation(diag[n % DIAGS], ident[:], ACT.Copy,
                                                     scale=wv[:, bass.ds((i + first) * ROWS + j, 1)]
                                                     ).then_inc(diag_ready, 1)
                    act.wait_ge(to_act[4], 1)
                    act.sem_inc(to_act[4], -1)
                    nc.scalar.copy(h2[:, bass.ds(t, 1), :].rearrange("p a n -> p (a n)"), pair(4, D)
                                   ).then_inc(bank_free[4], 1)

                with act.Fori(0, NT - 1) as t:
                    peer_act(t, True)
                peer_act(NT - 1, False)
                phase_barrier(act, "act")
                square_root(NT)
                phase_barrier(act, "act")

        @block.tensor
        def _(pe):
            def project(b, s, c, rhs):
                pe.wait_ge(bank_free[b], 1)
                pe.sem_inc(bank_free[b], -1)
                for f in range(2):
                    for k in range(KD):
                        last = nc.tensor.matmul(banks[:, b + f, 0:HALF], ring[:, s, k, c:c + P],
                                                rhs[:, k, f * HALF:(f + 1) * HALF], start=k == 0, stop=k == KD - 1)
                return last

            def tokenwise(b, s, lhs, t):
                pe.wait_ge(bank_free[b], 1)
                pe.sem_inc(bank_free[b], -1)
                for k in range(KD):
                    last = nc.tensor.matmul(banks[:, b, :], lhs[:, k, t * P:(t + 1) * P], ring[:, s, k, :],
                                            start=k == 0, stop=k == KD - 1)
                return last

            def at(b, t):
                return banks[:, b + t // 4, t % 4 * P:(t % 4 + 1) * P]

            def spread(b, part, c):
                pe.wait_ge(bank_free[b], 1)
                pe.sem_inc(bank_free[b], -1)
                for k in range(KD):
                    last = nc.tensor.matmul(at(b, k), modv[:, part * 8 + k, c:c + 1].to_broadcast([P, P]),
                                            ident[:], start=True, stop=True)
                last.then_inc(to_act[b], 1)

            pe.wait_ge(init, INIT)
            pe.wait_ge(cond_ready, 1)
            with pe.Fori(0, DEPTH) as l:
                with pe.Fori(0, B_GATE // 2):
                    for s in range(2):
                        pe.wait_ge(w_full[s], 16)
                        pe.sem_inc(w_full[s], -16)
                        pe.wait_ge(bank_free[s], 1)
                        pe.sem_inc(bank_free[s], -1)
                        for c in range(4):
                            for k in range(KD):
                                last = nc.tensor.matmul(banks[:, s, 2 * c:2 * c + 2], ring[:, s, k, c * P:(c + 1) * P],
                                                        cond[:, k, :], start=k == 0, stop=k == KD - 1)
                        last.then_inc(to_dve[s], 1)
                        pe.drain().then_inc(w_free[s], 1)
                phase_barrier(pe, "pe")
                for k in range(KD):
                    b = k % 4
                    pe.wait_ge(bank_free[4 + b], 1)
                    pe.sem_inc(bank_free[4 + b], -1)
                    nc.tensor.transpose(banks[:, 4 + b, 0:P], x[:, 0, k * P:(k + 1) * P], ident[:]
                                        ).then_inc(to_act[4 + b], 1)
                    pe.wait_ge(bank_free[b], 1)
                    pe.sem_inc(bank_free[b], -1)
                    for t in range(1, NT):
                        last = nc.tensor.transpose(banks[:, b, (t - 1) * P:t * P], x[:, t, k * P:(k + 1) * P], ident[:])
                    last.then_inc(to_dve[b], 1)
                phase_barrier(pe, "pe")
                for g in range(2 * NT):
                    s = (B_GATE + g // NT) % 2
                    if g % NT == 0:
                        pe.wait_ge(w_full[s], 16)
                        pe.sem_inc(w_full[s], -16)
                    tokenwise(g % 8, s, hT, g % NT).then_inc(to_act[g % 8], 1)
                    if g % NT == NT - 1:
                        pe.drain().then_inc(w_free[s], 1)
                phase_barrier(pe, "pe")
                with pe.Fori(0, HEADS // 2):
                    for s in range(2):
                        pe.wait_ge(w_full[s], 16)
                        pe.sem_inc(w_full[s], -16)
                        for c in range(3):
                            project(2 * c, s, c * P, hT).then_inc(to_act[2 * c], 1)
                        pe.wait_ge(bank_free[6], 1)
                        pe.sem_inc(bank_free[6], -1)
                        for t in range(NT):
                            for k in range(KD):
                                last = nc.tensor.matmul(at(6, t), hT[:, k, t * P:(t + 1) * P], ring[:, s, k, 3 * P:4 * P],
                                                        start=k == 0, stop=k == KD - 1)
                        last.then_inc(to_act[6], 1)
                        pe.drain().then_inc(w_free[s], 1)
                        for n in range(2 * NL):
                            b = 2 * (n % 2)
                            pe.wait_ge(x_ready[n % 2], 1)
                            pe.sem_inc(x_ready[n % 2], -1)
                            pe.wait_ge(bank_free[b], 1)
                            pe.sem_inc(bank_free[b], -1)
                            for t in range(NT):
                                xt = X[n % 2][:, t * P:(t + 1) * P]
                                last = nc.tensor.matmul(at(b, t), xt, xt, start=True, stop=True)
                            last.then_inc(to_dve[b], 1)
                        pe.wait_ge(ksum_ready, 1)
                        pe.sem_inc(ksum_ready, -1)
                        pe.wait_ge(bank_free[0], 1)
                        pe.sem_inc(bank_free[0], -1)
                        for t in range(NT):
                            last = nc.tensor.matmul(at(0, t), ksum[:, t * P:(t + 1) * P], hq[:, t * P:(t + 1) * P],
                                                    start=True, stop=True)
                        last.then_inc(to_dve[0], 1)
                        for d in range(2):
                            pe.wait_ge(x_ready[d], 1)
                            pe.sem_inc(x_ready[d], -1)
                            pe.wait_ge(bank_free[4 + 2 * d], 1)
                            pe.sem_inc(bank_free[4 + 2 * d], -1)
                            for t in range(NT):
                                last = nc.tensor.transpose(at(4 + 2 * d, t), X[d][:, t * P:(t + 1) * P], ident[:])
                            last.then_inc(to_act[4 + 2 * d], 1)
                        pe.wait_ge(v_ready, 1)
                        pe.sem_inc(v_ready, -1)
                        for d in range(2):
                            pe.wait_ge(kdt_ready, 1)
                            pe.sem_inc(kdt_ready, -1)
                            pe.wait_ge(bank_free[2 * d], 1)
                            pe.sem_inc(bank_free[2 * d], -1)
                            for t in range(NT):
                                last = nc.tensor.matmul(at(2 * d, t), kdT[d][:, t * P:(t + 1) * P],
                                                        hv[:, t * P:(t + 1) * P], start=True, stop=True)
                            last.then_inc(to_dve[2 * d], 1)
                        pe.wait_ge(sc_ready, 1)
                        pe.sem_inc(sc_ready, -1)
                        pe.wait_ge(state_ready, 1)
                        pe.sem_inc(state_ready, -1)
                        pe.wait_ge(bank_free[4], 1)
                        pe.sem_inc(bank_free[4], -1)
                        for t in range(NT):
                            tt = slice(t * P, (t + 1) * P)
                            last = nc.tensor.matmul(at(4, t), sc[:, tt], hv[:, tt], start=True, stop=t == 0)
                            for d in range(2 * (t > 0)):
                                last = nc.tensor.matmul(at(4, t), qdec[d][:, tt], S[d][:, t - 1, :],
                                                        start=False, stop=d == 1)
                        last.then_inc(to_act[4], 1)
                        pe.wait_ge(o1_ready, 1)
                        pe.sem_inc(o1_ready, -1)
                        pe.wait_ge(bank_free[6], 1)
                        pe.sem_inc(bank_free[6], -1)
                        for t in range(NT):
                            last = nc.tensor.transpose(at(6, t), o1[:, t * P:(t + 1) * P], ident[:])
                        last.then_inc(to_act[6], 1)
                phase_barrier(pe, "pe")
                for g in range(3 * NT):
                    s = (B_KV + g // NT) % 2
                    if g % NT == 0:
                        pe.wait_ge(w_full[s], 16)
                        pe.sem_inc(w_full[s], -16)
                    tokenwise(g % 8, s, hT, g % NT).then_inc(to_act[g % 8], 1)
                    if g % NT == NT - 1:
                        pe.drain().then_inc(w_free[s], 1)
                pe.wait_ge(past_full, 32)
                pe.sem_inc(past_full, -32)
                pe.wait_ge(qkn_pe, 1)
                pe.sem_inc(qkn_pe, -1)
                for kp in range(2):
                    pe.wait_ge(bank_free[2 * kp], 1)
                    pe.sem_inc(bank_free[2 * kp], -1)
                    for t in range(NT + 1):
                        src = qkv[:, t, 1024 + kp * P:1024 + (kp + 1) * P] if t < NT else kpast[:, kp * P:(kp + 1) * P]
                        last = nc.tensor.transpose(at(2 * kp, t), src, ident[:])
                    last.then_inc(to_act[2 * kp], 1)
                pe.wait_ge(kt_ready, 2)
                pe.sem_inc(kt_ready, -2)
                for kp in range(2):
                    with pe.Fori(0, 4):
                        pe.wait_ge(qst_ready, 1)
                        pe.sem_inc(qst_ready, -1)
                        pe.wait_ge(bank_free[6], 1)
                        pe.sem_inc(bank_free[6], -1)
                        for t in range(NT):
                            last = nc.tensor.transpose(at(6, t), qstage[:, t, :], ident[:])
                        last.then_inc(to_act[6], 1)
                        pe.drain().then_inc(qst_free, 1)
                        pe.wait_ge(qts_ready, 1)
                        pe.sem_inc(qts_ready, -1)

                        def score(u):
                            half, qt = divmod(u, NT)
                            rows = slice(64 * half, 64 * half + 64)
                            b = 2 * (u % 2)
                            pe.wait_ge(bank_free[b], 1)
                            pe.sem_inc(bank_free[b], -1)
                            lhs = qTs[rows, qt * P:(qt + 1) * P]
                            if qt == 0:
                                last = nc.tensor.matmul(banks[:, b, 0:P], lhs, KT[rows, kp, 0:P], start=True, stop=True)
                            else:
                                nc.tensor.matmul(banks[:, b, :], lhs, KT[rows, kp, P:T], start=True, stop=True)
                                last = nc.tensor.matmul(banks[:, b + 1, 0:P], lhs, KT[rows, kp, T:T + P],
                                                        start=True, stop=True)
                            last.then_inc(to_dve[b], 1)

                        def turn(u):
                            pe.wait_ge(prob_ready[u % 2], 1)
                            pe.sem_inc(prob_ready[u % 2], -1)
                            pe.wait_ge(bank_free[4], 1)
                            pe.sem_inc(bank_free[4], -1)
                            for j in range(1 if u % NT == 0 else NT):
                                last = nc.tensor.transpose(at(4, j), pr[u % 2][:, j * P:(j + 1) * P], ident[:])
                            last.then_inc(to_act[4], 1)

                        def weigh(half):
                            rows = slice(64 * half, 64 * half + 64)
                            c = 1280 + (2 * kp + half) * HD
                            pe.wait_ge(pt_ready[half], 1)
                            pe.sem_inc(pt_ready[half], -1)
                            if half == 0:
                                pe.wait_ge(bank_free[6], 1)
                                pe.sem_inc(bank_free[6], -1)
                            nc.tensor.matmul(banks[rows, 7, 0:P], qkv[:, 0, c:c + HD], PTc[half], start=True, stop=True)
                            for j in range(NT):
                                lhs = qkv[:, j + 1, c:c + HD] if j < NT - 1 else vpast[:, c - 1280:c - 1280 + HD]
                                last = nc.tensor.matmul(banks[rows, 6, :], lhs, PT[half][:, j, :],
                                                        start=j == 0, stop=j == NT - 1)
                            last.then_inc(pt_free[half], 1)

                        score(0)
                        for u in range(2 * NT):
                            if u + 1 < 2 * NT:
                                score(u + 1)
                            turn(u)
                            if u == NT + 1:
                                weigh(0)
                        weigh(1)
                        pe.drain().then_inc(to_act[6], 1)
                phase_barrier(pe, "pe")
                with pe.Fori(0, KD // 2):
                    for n in range(2):
                        s = (B_MIX + n) % 2
                        pe.wait_ge(w_full[s], 16)
                        pe.sem_inc(w_full[s], -16)
                        for f in range(2):
                            for c, rhs in enumerate([hT, hT, orecT, oattT]):
                                b = 4 * f + c
                                pe.wait_ge(bank_free[b], 1)
                                pe.sem_inc(bank_free[b], -1)
                                for k in range(KD):
                                    last = nc.tensor.matmul(banks[:, b, 0:HALF], ring[:, s, k, c * P:(c + 1) * P],
                                                            rhs[:, k, f * HALF:(f + 1) * HALF],
                                                            start=k == 0, stop=k == KD - 1)
                                last.then_inc((to_act if c < 2 else to_dve)[b], 1)
                        pe.drain().then_inc(w_free[s], 1)
                phase_barrier(pe, "pe")
                for v, (part, c) in enumerate([(G1, 0), (G1, 1), (SC2, 0), (SH2, 0), (SC2, 1), (SH2, 1)]):
                    spread(2 * (v % 4), part, c)
                for b in range(0, 8, 2):
                    pe.wait_ge(bank_free[b], 1)
                    pe.sem_inc(bank_free[b], -1)
                    pe.sem_inc(bank_free[b], 1)
                for g in range(2 * NT):
                    s = (B_OUT + g // NT) % 2
                    if g % NT == 0:
                        pe.wait_ge(w_full[s], 16)
                        pe.sem_inc(w_full[s], -16)
                    tokenwise(g % 8, s, yT, g % NT).then_inc(to_dve[g % 8], 1)
                    if g % NT == NT - 1:
                        pe.drain().then_inc(w_free[s], 1)
                phase_barrier(pe, "pe")
                pe.wait_ge(w_full[B_SK % 2], 16)
                pe.sem_inc(w_full[B_SK % 2], -16)
                pe.sem_inc(sk_arrived, 1)
                for t in range(NT):
                    b = 2 * (t % 4)
                    pe.wait_ge(h2_ready, 1)
                    pe.sem_inc(h2_ready, -1)
                    pe.wait_ge(bank_free[b], 1)
                    pe.sem_inc(bank_free[b], -1)
                    for k in range(KD):
                        last = nc.tensor.transpose(at(b, k), h2[:, t, k * P:(k + 1) * P], ident[:])
                    last.then_inc(to_act[b], 1)
                pe.wait_ge(h2T_ready, NT)
                pe.sem_inc(h2T_ready, -NT)
                pe.wait_ge(sk_ready, 1)
                pe.sem_inc(sk_ready, -1)
                with pe.Fori(0, 2) as i:
                    for s in range(2):
                        def match(u):
                            b = 4 + 2 * (u % 2)
                            pe.wait_ge(qt_ready, 1)
                            pe.sem_inc(qt_ready, -1)
                            pe.wait_ge(bank_free[b], 1)
                            pe.sem_inc(bank_free[b], -1)
                            for t in range(NT):
                                last = nc.tensor.matmul(
                                    at(b, t), qT[:, u, t * P:(t + 1) * P],
                                    skT[:, bass.ds((2 * i + s) * 4 + u, 1), :].rearrange("p a n -> p (a n)"),
                                    start=True, stop=True)
                            last.then_inc(to_dve[b], 1)

                        pe.wait_ge(w_full[s], 16)
                        pe.sem_inc(w_full[s], -16)
                        for u in range(4):
                            project(2 * (u % 2), s, u * P, hT).then_inc(to_act[2 * (u % 2)], 1)
                            if u:
                                match(u - 1)
                        match(3)
                        pe.drain().then_inc(w_free[s], 1)
                phase_barrier(pe, "pe")
                for c in range(2):
                    spread(2 * c, G2, c)
                with pe.Fori(0, NT) as t:
                    pe.wait_ge(acc_zero, 1)
                    pe.sem_inc(acc_zero, -1)
                    pe.wait_ge(bank_free[4], 1)
                    pe.sem_inc(bank_free[4], -1)
                    for c in range(2):
                        last = nc.tensor.matmul(banks[:, 4 + c, :], ident[:], acc[:, c * CB:(c + 1) * CB],
                                                start=True, stop=False, skip_group_check=True)
                    last.then_inc(acc_seen, 1)
                    for first, count, mine in ((0, TURNS_A, ALL_ROWS), (TURNS_A, TURNS - TURNS_A, PE_ROWS)):
                        with pe.Fori(0, count) as i:
                            for n, j in enumerate(mine):
                                pe.wait_ge(diag_ready, 1)
                                pe.sem_inc(diag_ready, -1)
                                pe.wait_ge(row_full[j], (((l * NT + t) * 2 + 1) * TURNS + first + i + 1) * 16)
                                nc.tensor.matmul(banks[:, 4, :], diag[n % DIAGS], grow[j][:, 0:CB], start=False,
                                                 stop=False, skip_group_check=True
                                                 ).then_inc(diag_used, 1)
                                nc.tensor.matmul(banks[:, 5, :], diag[n % DIAGS], grow[j][:, CB:D], start=False,
                                                 stop=False, skip_group_check=True).then_inc(row_free[j], 1)
                    pe.wait_ge(acc_done, 1)
                    pe.sem_inc(acc_done, -1)
                    for c in range(2):
                        last = nc.tensor.matmul(banks[:, 4 + c, :], ident[:], acc[:, c * CB:(c + 1) * CB],
                                                start=False, stop=True, skip_group_check=True)
                    last.then_inc(to_act[4], 1)
                    pe.drain().then_inc(acc_free, 1)
                phase_barrier(pe, "pe")
                phase_barrier(pe, "pe")

        @block.vector
        def _(dve):
            V = nc.vector
            dve.wait_ge(init, INIT)
            z = [lbz[:, :, j, :] for j in range(DEPTH)]
            m = r3(small[:, 0:16], 8)
            V.tensor_tensor(m, z[0], z[1], ALU.max)
            dve.drain()
            for j in range(DEPTH):
                V.tensor_tensor(z[j], z[j], m, ALU.subtract).then_inc(lb_shifted, j)                    if j else V.tensor_tensor(z[j], z[j], m, ALU.subtract)
            dve.wait_ge(lb_exped, 1)
            V.tensor_tensor(m, z[0], z[1], ALU.add)
            V.memset(lbf[:, 0:16], LOG_FLOOR)
            V.tensor_copy(masks[:].rearrange("p n i -> p (n i)"), arena[:, 0:(2 * NL + 1) * P])
            V.memset(omlb[:, 0:16], 1.0)
            dve.drain()
            V.reciprocal(small[:, 0:16], small[:, 0:16])
            dve.drain()
            V.tensor_tensor(r3(lbf[:, 16:32], 8), z[1], m, ALU.mult)
            dve.drain()
            V.tensor_scalar(omlb[:, 16:32], lbf[:, 16:32], -1.0, 1.0, ALU.mult, ALU.add)
            dve.drain()
            V.tensor_scalar(lbf[:, 16:32], lbf[:, 16:32], LOG_FLOOR, None, ALU.add).then_inc(lb_ready, 1)
            dve.drain()

            def inverse_root(n):
                dve.drain().then_inc(var_ready, 1)
                dve.wait_ge(std_ready, 1)
                dve.sem_inc(std_ready, -1)
                V.reciprocal(small[:, 0:n], small[:, 0:n])
                dve.drain()

            def layer_norm(gain, shift):
                stats = small[:, 64:64 + NT * 12].rearrange("p (t c s) -> p t c s", t=NT, c=2)
                mv = r3(small[:, 128:128 + 2 * NT], 2)
                for t in range(NT):
                    for c in range(2):
                        V.bn_stats(stats[:, t, c, :], x[:, t, c * 512:(c + 1) * 512])
                dve.drain()
                for t in range(NT):
                    V.bn_aggr(mv[:, t, :], stats[:, t, :, :])
                dve.drain()
                V.tensor_scalar(small[:, 0:NT], mv[:, :, 1:2].rearrange("p t a -> p (t a)"), EPS, None, ALU.add)
                inverse_root(NT)
                for t in range(NT):
                    V.tensor_scalar(x[:, t, :], x[:, t, :], mv[:, t, 0:1], small[:, t:t + 1], ALU.subtract, ALU.mult)
                dve.drain()
                for t in range(NT):
                    V.tensor_tensor(x[:, t, :], x[:, t, :], lnrows[:, gain, :], ALU.mult)
                dve.drain()
                for t in range(NT):
                    V.tensor_tensor(x[:, t, :], x[:, t, :], lnrows[:, shift, :], ALU.add)
                dve.drain()

            def top16(values, indices, source, spare, n, count):
                src, alt = r3(source, n), r3(spare, n)
                for u in range(count):
                    V.max(values[:, u, 0:8], src[:, u, :])
                dve.drain()
                for u in range(count):
                    V.max_index(indices[:, u, 0:8], values[:, u, 0:8], src[:, u, :])
                for u in range(count):
                    V.match_replace(alt[:, u, :], values[:, u, 0:8], src[:, u, :], -3.0e38)
                dve.drain()
                for u in range(count):
                    V.max(values[:, u, 8:16], alt[:, u, :])
                dve.drain()
                for u in range(count):
                    V.max_index(indices[:, u, 8:16], values[:, u, 8:16], alt[:, u, :])
                dve.drain()

            with dve.Fori(0, DEPTH) as l:
                with dve.Fori(0, B_GATE // 2) as i:
                    for s in range(2):
                        dve.wait_ge(to_dve[s], 1)
                        dve.sem_inc(to_dve[s], -1)
                        V.tensor_tensor(
                            modv[:, bass.ds((2 * i + s) * 4, 4), :], r3(banks[:, s, 0:8], 2),
                            bmod[:].rearrange("p l m -> p (l m)")[:, bass.ds(l * 48 + (2 * i + s) * 4, 4)]
                            .unsqueeze(2).to_broadcast([P, 4, 2]), ALU.add).then_inc(bank_free[s], 1)
                dve.drain()
                for part in (SC1, SC2):
                    V.tensor_scalar(modv[:, part * 8:part * 8 + 8, :], modv[:, part * 8:part * 8 + 8, :],
                                    1.0, None, ALU.add)
                phase_barrier(dve, "dve")
                for k in range(KD):
                    b = k % 4
                    dve.wait_ge(to_dve[b], 1)
                    dve.sem_inc(to_dve[b], -1)
                    V.tensor_scalar(hT[:, k, P:T], banks[:, b, :], modv[:, SC1 * 8 + k, 1:2],
                                    modv[:, SH1 * 8 + k, 1:2], ALU.mult, ALU.add).then_inc(bank_free[b], 1)
                phase_barrier(dve, "dve")
                phase_barrier(dve, "dve")
                with dve.Fori(0, HEADS) as h:
                    for d in range(2):
                        dve.wait_ge(kneg_ready, 1)
                        dve.sem_inc(kneg_ready, -1)
                        V.tensor_scalar(hk[d], hk[d], omlb[:, bass.ds((l * 2 + d) * HEADS + h, 1)], None, ALU.mult)
                    dve.drain()
                    V.tensor_tensor(ksum, hk[0], hk[1], ALU.add).then_inc(ksum_ready, 1)
                    for d in range(2):
                        dve.wait_ge(log_ready, 1)
                        dve.sem_inc(log_ready, -1)
                        V.tensor_tensor_scan(pre[d].rearrange("p t n -> p (t n)"), reset[:],
                                             gl[d].rearrange("p t n -> p (t n)"), 0.0, ALU.mult, ALU.add
                                             ).then_inc(pre_ready, 1)

                    def place(n):
                        b = 2 * (n % 2)
                        dve.wait_ge(to_dve[b], 1)
                        dve.sem_inc(to_dve[b], -1)
                        V.copy_predicated(r3(sc, P), masks[:, n:n + 1, :].to_broadcast([P, NT, P]),
                                          r3(pair(b), P)).then_inc(bank_free[b], 1)

                    for n, (d, s) in enumerate(units):
                        lo, up = (hk[0], hq) if d == 0 else (hq, hk[1])
                        v = [y.rearrange("p (b s) -> p b s", s=2 * s) for y in (X[n % 2], E[n % 2], lo, up)]
                        dve.wait_ge(exp_ready[n % 2], 1)
                        dve.sem_inc(exp_ready[n % 2], -1)
                        V.tensor_tensor(v[0][:, :, 0:s], v[1][:, :, 0:s], v[2][:, :, 0:s], ALU.mult)
                        V.tensor_tensor(v[0][:, :, s:2 * s], v[1][:, :, s:2 * s], v[3][:, :, s:2 * s], ALU.mult
                                        ).then_inc(x_ready[n % 2], 1)
                        if n:
                            place(n - 1)
                        dve.drain().then_inc(e_free[n % 2], 1)
                    for n, (src, dst) in enumerate([(hq, qdec[0]), (hk[0], X[0]), (hq, qdec[1]), (hk[1], X[1])]):
                        dve.wait_ge(exp_ready[n % 2], 1)
                        dve.sem_inc(exp_ready[n % 2], -1)
                        V.tensor_tensor(dst, E[n % 2], src, ALU.mult).then_inc(e_free[n % 2], 1)
                        if n % 2:
                            dve.drain().then_inc(x_ready[n // 2], 1)
                        if n == 0:
                            place(2 * NL - 1)
                    dve.drain()
                    place(2 * NL)
                    dve.drain().then_inc(sc_ready, 1)
                    dve.wait_ge(tot_ready, 2)
                    dve.sem_inc(tot_ready, -2)
                    dve.wait_ge(s0_full, 32)
                    dve.sem_inc(s0_full, -32)
                    dve.wait_ge(hnew_sent, 32)
                    dve.sem_inc(hnew_sent, -32)
                    for d in range(2):
                        dve.wait_ge(to_dve[2 * d], 1)
                        dve.sem_inc(to_dve[2 * d], -1)
                        added = r3(pair(2 * d), P)
                        V.tensor_copy(hnew[:, d, :], added[:, 0, :])
                        for n in ([0, 1, 2], [3, 2, 1])[d]:
                            to = n + 1 - 2 * d
                            V.scalar_tensor_tensor(S[d][:, to, :], S[d][:, n, :], tot[:, d, n + 1:n + 2],
                                                   added[:, n + 1, :], ALU.mult, ALU.add)
                            dve.drain()
                        dve.drain().then_inc(bank_free[2 * d], 1)
                    dve.drain().then_inc(state_ready, 1)
                    dve.drain().then_inc(hnew_ready, 1)
                    dve.wait_ge(osq_ready, 1)
                    dve.sem_inc(osq_ready, -1)
                    V.tensor_reduce(small[:, 0:NT], r3(osq, P), AX.X, ALU.add)
                    dve.drain()
                    V.tensor_scalar(small[:, 0:NT], small[:, 0:NT], 1.0 / P, EPS, ALU.mult, ALU.add)
                    inverse_root(NT)
                    V.tensor_tensor(r3(o1, P), r3(pair(4), P), small[:, 0:NT].unsqueeze(2).to_broadcast([P, NT, P]),
                                    ALU.mult).then_inc(bank_free[4], 1)
                    dve.drain()
                    V.tensor_tensor(r3(o1, P), r3(o1, P), rows_g[:, bass.ds(l, 1), 0:P].to_broadcast([P, NT, P]),
                                    ALU.mult)
                    dve.drain()
                    V.tensor_tensor(r3(o1, P), r3(o1, P), sgate[:, :, bass.ds(h * P, P)], ALU.mult
                                    ).then_inc(o1_ready, 1)
                phase_barrier(dve, "dve")
                dve.wait_ge(qkv_ready, 1)
                dve.sem_inc(qkv_ready, -1)
                for t in range(NT):
                    V.tensor_tensor(nt1, qkv[:, t, 0:1280], qkv[:, t, 0:1280], ALU.mult)
                    dve.drain()
                    V.tensor_reduce(small[:, 20 * t:20 * t + 20], r3(nt1, HD), AX.X, ALU.add)
                    dve.drain()
                V.tensor_scalar(small[:, 0:100], small[:, 0:100], 1.0 / HD, EPS, ALU.mult, ALU.add)
                inverse_root(100)
                for t in range(NT):
                    v = r3(qkv[:, t, 0:1280], HD)
                    V.tensor_tensor(v, v, small[:, 20 * t:20 * t + 20].unsqueeze(2).to_broadcast([P, 20, HD]), ALU.mult)
                    dve.drain()
                    V.tensor_tensor(v[:, 0:QH], v[:, 0:QH],
                                    rows_g[:, bass.ds(l, 1), P:P + HD].to_broadcast([P, QH, HD]), ALU.mult)
                    V.tensor_tensor(v[:, QH:20], v[:, QH:20],
                                    rows_g[:, bass.ds(l, 1), P + HD:P + 2 * HD].to_broadcast([P, KV, HD]), ALU.mult)
                    dve.drain()
                    if t:
                        c, s = (y[:, t - 1:t, :].to_broadcast([P, 20, 32]) for y in (cos, sin))
                        a, b = r3(nt1, HD), r3(nt2, HD)
                        V.tensor_tensor(a[:, :, 0:32], v[:, :, 0:32], c, ALU.mult)
                        V.tensor_tensor(a[:, :, 32:64], v[:, :, 0:32], s, ALU.mult)
                        V.tensor_tensor(b[:, :, 0:32], v[:, :, 32:64], s, ALU.mult)
                        V.tensor_tensor(b[:, :, 32:64], v[:, :, 32:64], c, ALU.mult)
                        dve.drain()
                        V.tensor_tensor(v[:, :, 0:32], a[:, :, 0:32], b[:, :, 0:32], ALU.subtract)
                        V.tensor_tensor(v[:, :, 32:64], a[:, :, 32:64], b[:, :, 32:64], ALU.add)
                for s in (qkn_pool, qkn_pe, qkn_act):
                    dve.drain().then_inc(s, 1)
                for kp in range(2):
                    with dve.Fori(0, 4):
                        def highest(u):
                            b = 2 * (u % 2)
                            dve.wait_ge(to_dve[b], 1)
                            dve.sem_inc(to_dve[b], -1)
                            c = small[:, 128 + u % 2:129 + u % 2]
                            V.reduce_max(c, pair(b, P if u % NT == 0 else T), AX.X)
                            dve.drain()
                            V.tensor_scalar(c, c, -SCALE, None, ALU.mult).then_inc(max_ready[u % 2], 1)

                        def normalise(u):
                            n = P if u % NT == 0 else T
                            dve.wait_ge(prob_raw[u % 2], 1)
                            dve.sem_inc(prob_raw[u % 2], -1)
                            c = small[:, 130 + u % 2:131 + u % 2]
                            V.reciprocal(c, c)
                            dve.drain()
                            V.tensor_scalar(pr[u % 2][:, 0:n], pr[u % 2][:, 0:n], c, None, ALU.mult
                                            ).then_inc(prob_ready[u % 2], 1)

                        for u in range(2 * NT):
                            highest(u)
                            if u:
                                normalise(u - 1)
                        normalise(2 * NT - 1)
                phase_barrier(dve, "dve")
                with dve.Fori(0, KD) as n:
                    for f in range(2):
                        dve.wait_ge(sg_ready[f], 1)
                        dve.sem_inc(sg_ready[f], -1)
                        dve.wait_ge(to_dve[4 * f + 2], 1)
                        dve.sem_inc(to_dve[4 * f + 2], -1)
                        V.tensor_tensor(y1, banks[:, 4 * f + 2, 0:HALF], sgA[f], ALU.mult
                                        ).then_inc(bank_free[4 * f + 2], 1)
                        dve.wait_ge(to_dve[4 * f + 3], 1)
                        dve.sem_inc(to_dve[4 * f + 3], -1)
                        V.tensor_tensor(y2, banks[:, 4 * f + 3, 0:HALF], sgB[f], ALU.mult
                                        ).then_inc(bank_free[4 * f + 3], 1)
                        dve.drain().then_inc(sg_free[f], 1)
                        V.tensor_tensor(yT[:, bass.ds(n, 1), f * HALF:(f + 1) * HALF].rearrange("p a n -> p (a n)"),
                                        y1, y2, ALU.add)
                        dve.drain()
                phase_barrier(dve, "dve")
                dve.wait_ge(bc_ready, 1)
                dve.sem_inc(bc_ready, -1)
                for g in range(2 * NT):
                    t, c = g % NT, slice(g // NT * CB, (g // NT + 1) * CB)
                    dve.wait_ge(to_dve[g % 8], 1)
                    dve.sem_inc(to_dve[g % 8], -1)
                    V.tensor_tensor(outtmp, banks[:, g % 8, :], bca[:, min(t, 1), c], ALU.mult
                                    ).then_inc(bank_free[g % 8], 1)
                    dve.drain()
                    V.scalar_tensor_tensor(x[:, t, c], x[:, t, c], ALPHA, outtmp, ALU.mult, ALU.add)
                    dve.drain()
                dve.wait_ge(ln_full, 16)
                dve.sem_inc(ln_full, -16)
                layer_norm(0, 1)
                phase_barrier(dve, "dve")
                for t in range(NT):
                    c = 2 * min(t, 1)
                    V.tensor_tensor(h2[:, t, :], x[:, t, :], bcb[:, c, :], ALU.mult)
                    dve.drain()
                    V.tensor_tensor(h2[:, t, :], h2[:, t, :], bcb[:, c + 1, :], ALU.add).then_inc(h2_ready, 1)
                with dve.Fori(0, 4) as i:
                    for u in range(4):
                        b = 4 + 2 * (u % 2)
                        dve.wait_ge(to_dve[b], 1)
                        dve.sem_inc(to_dve[b], -1)
                        V.tensor_copy(r3(arena[:, 0:10240], 2048)[:, :, bass.ds((i * 4 + u) * NKEYS, NKEYS)],
                                      r3(pair(b), P)).then_inc(bank_free[b], 1)
                phase_barrier(dve, "dve")
                def choose_experts(t):
                    dve.wait_ge(stage_ready, 1)
                    dve.sem_inc(stage_ready, -1)
                    top16(tv, ti.bitcast(U32), stage, work, NKEYS, 2 * PEER_H)
                    V.tensor_copy(tif, ti.bitcast(U32))
                    halves_v = tv.rearrange("p (h a) k -> p h a k", a=2)
                    V.tensor_tensor(stage.rearrange("p (h a b) -> p h a b", h=PEER_H, a=TOPK),
                                    halves_v[:, :, 0, :].unsqueeze(3).to_broadcast([P, PEER_H, TOPK, TOPK]),
                                    halves_v[:, :, 1, :].unsqueeze(2).to_broadcast([P, PEER_H, TOPK, TOPK]), ALU.add)
                    dve.drain()
                    top16(r3(bs, TOPK), r3(bp, TOPK).bitcast(U32), stage, work, TOPK * TOPK, PEER_H)
                    V.tensor_tensor(r3(gate, TOPK), r3(bs, TOPK), r3(bs, TOPK)[:, :, 0:1]
                                    .to_broadcast([P, PEER_H, TOPK]), ALU.subtract)
                    V.tensor_scalar(bq.bitcast(U32), bp.bitcast(U32), 4, None, ALU.logical_shift_right)
                    V.tensor_scalar(bp.bitcast(U32), bp.bitcast(U32), 15, None, ALU.bitwise_and)
                    dve.drain()
                    V.tensor_copy(paf, bq.bitcast(U32))
                    V.tensor_copy(pbf, bp.bitcast(U32))
                    dve.drain()
                    halves_i = tif.rearrange("p (h a) k -> p h a k", a=2)
                    for a, (pos, found) in enumerate([(paf, e1), (pbf, e2)]):
                        V.tensor_tensor(r3(stage, TOPK), pos.unsqueeze(2).to_broadcast([P, SLOTS, TOPK]),
                                        iota[:].unsqueeze(1).to_broadcast([P, SLOTS, TOPK]), ALU.is_equal)
                        dve.drain()
                        one = stage.rearrange("p (h s k) -> p h s k", h=PEER_H, s=TOPK)
                        V.tensor_tensor(one, one, halves_i[:, :, a, :].unsqueeze(2)
                                        .to_broadcast([P, PEER_H, TOPK, TOPK]), ALU.mult)
                        dve.drain()
                        V.tensor_reduce(found, r3(stage, TOPK), AX.X, ALU.add)
                        dve.drain()
                    dve.drain().then_inc(stage_free, 1)
                    V.scalar_tensor_tensor(e1, e1, float(NKEYS), e2, ALU.mult, ALU.add)
                    dve.drain()
                    V.tensor_scalar(arena[:, bass.ds(t * 2048, SLOTS)].bitcast(U32), e1, layer_base[:], None,
                                    ALU.add).then_inc(idx_ready, 1)

                def peer_dve(t, more):
                    ht = h2[:, bass.ds(t, 1), :].rearrange("p a n -> p (a n)")
                    with dve.Fori(0, TURNS) as i:
                        for j in range(ROWS):
                            dve.wait_ge(row_full[j], (((l * NT + t) * 2) * TURNS + i + 1) * 16)
                            V.scalar_tensor_tensor(grow[j], grow[j], 1.0, ht, ALU.mult, ALU.mult,
                                                   accum_out=av[:, bass.ds(i * ROWS + j, 1)]
                                                   ).then_inc(row_free[j], 1)
                    dve.drain().then_inc(dots_ready, 1)
                    dve.wait_ge(acc_free, 1)
                    dve.sem_inc(acc_free, -1)
                    V.memset(acc, 0.0).then_inc(acc_zero, 1)
                    dve.wait_ge(softexp_ready, 1)
                    dve.sem_inc(softexp_ready, -1)
                    V.tensor_reduce(gsum, r3(gate, TOPK), AX.X, ALU.add)
                    dve.drain()
                    V.reciprocal(gsum, gsum)
                    dve.drain()
                    V.tensor_tensor(r3(gate, TOPK), r3(gate, TOPK), gsum.unsqueeze(2)
                                    .to_broadcast([P, PEER_H, TOPK]), ALU.mult)
                    dve.drain()
                    dve.wait_ge(gelu_ready, 1)
                    dve.sem_inc(gelu_ready, -1)
                    V.tensor_tensor(wv, av, gate, ALU.mult).then_inc(wv_ready, 1)
                    dve.drain()
                    if more:
                        choose_experts(t + 1)
                    dve.wait_ge(acc_seen, 1)
                    dve.sem_inc(acc_seen, -1)
                    with dve.Fori(0, TURNS - TURNS_A) as i:
                        for j in sorted(set(ALL_ROWS) - set(PE_ROWS)):
                            dve.wait_ge(row_full[j], (((l * NT + t) * 2 + 1) * TURNS + TURNS_A + i + 1) * 16)
                            V.scalar_tensor_tensor(acc, grow[j], wv[:, bass.ds((i + TURNS_A) * ROWS + j, 1)], acc,
                                                   ALU.mult, ALU.add).then_inc(row_free[j], 1)
                            dve.drain()
                    dve.drain().then_inc(acc_done, 1)

                choose_experts(0)
                with dve.Fori(0, NT - 1) as t:
                    peer_dve(t, True)
                peer_dve(NT - 1, False)
                phase_barrier(dve, "dve")
                for t in range(NT):
                    V.tensor_tensor(h2[:, t, :], h2[:, t, :], bca[:, min(t, 1), :], ALU.mult)
                dve.drain()
                for t in range(NT):
                    V.scalar_tensor_tensor(x[:, t, :], x[:, t, :], ALPHA, h2[:, t, :], ALU.mult, ALU.add)
                V.tensor_scalar(layer_base[:], layer_base[:], float(N_EXPERTS), None, ALU.add)
                dve.drain()
                layer_norm(2, 3)
                phase_barrier(dve, "dve")
            dve.wait_ge(hnew_sent, 32)
            dve.drain().then_inc(done, 1)


def level_masks():
    j, i = np.meshgrid(np.arange(P), np.arange(P), indexing="ij")
    out = np.zeros((P, 2 * NL + 1, P), np.float32)
    for n, s in enumerate(LEVELS):
        same = (i // (2 * s)) == (j // (2 * s))
        out[:, 2 * n] = same & (i // s % 2 == 1) & (j // s % 2 == 0)
        out[:, 2 * n + 1] = same & (i // s % 2 == 0) & (j // s % 2 == 1)
    out[:, 2 * NL] = i == j
    return out.reshape(P, (2 * NL + 1) * P)


def rotary_tables():
    t = np.arange(LAT, dtype=np.float32)
    inv = (np.float32(10000.0) ** (-np.arange(HD // 4, dtype=np.float32) / np.float32(HD // 4))).astype(np.float32)
    ang = np.concatenate([np.floor(t / GRID_W)[:, None] * inv, (t % GRID_W)[:, None] * inv], axis=1).astype(np.float32)
    return [np.ascontiguousarray(f(ang).astype(np.float32).reshape(NT - 1, P, 32).transpose(1, 0, 2))
            for f in (np.cos, np.sin)]


def layout(inputs):
    a = {k: np.asarray(v) for k, v in inputs.items()}
    w_in = a["w_in"]
    off = np.cumsum([0, 1024, 1024, 1024, 1024, 1024, 1024, 256, 256, 1024, 1024])
    hq, hff, hfb, hi, hg, aq, ak, av, ga, gb = (w_in[:, :, off[n]:off[n + 1]] for n in range(10))
    order = [h for kp in range(2) for i in range(4) for h in (8 * kp + i, 8 * kp + 4 + i)]
    aq = aq.reshape(DEPTH, D, QH, HD)[:, :, order].reshape(DEPTH, D, D)
    watt = a["w_branch_att"].reshape(DEPTH, QH, HD, D)[:, order].reshape(DEPTH, D, D)
    sk = a["peer_sub_keys"].transpose(0, 4, 1, 2, 3).reshape(DEPTH, P, 2048)

    def block(w):
        return w.reshape(KD, P, CB).transpose(1, 0, 2).reshape(P, KD * CB)

    wblk = np.zeros((DEPTH * NB, P, KD * CB), np.float32)
    for l in range(DEPTH):
        blocks = [a["w_mod"][l][:, j * CB:(j + 1) * CB] for j in range(12)]
        blocks += [hg[l][:, j * CB:(j + 1) * CB] for j in range(2)]
        blocks += [np.concatenate([w[l][:, h * P:(h + 1) * P] for w in (hq, hff, hfb, hi)], 1) for h in range(HEADS)]
        blocks += [np.concatenate([ak[l], av[l]], 1), aq[l][:, 0:CB], aq[l][:, CB:]]
        blocks += [np.concatenate([w[l][:, n * P:(n + 1) * P] for w in (ga, gb, a["w_branch_rec"], watt)], 1)
                   for n in range(KD)]
        blocks += [a["w_out"][l][:, j * CB:(j + 1) * CB] for j in range(2)]
        blocks += [None] + [a["peer_w_query"][l][:, j * CB:(j + 1) * CB] for j in range(4)]
        for n, w in enumerate(blocks):
            if w is None:
                wblk[l * NB + n, :, 0:2048] = sk[l]
            else:
                wblk[l * NB + n] = block(w)
    cos, sin = rotary_tables()
    reset = np.ones((P, NT, 129), np.float32)
    reset[:, :, 0] = 0.0
    return {
        "x_prompt": a["x_prompt"][0], "x_sample": a["x_sample"][0],
        "cond": np.stack([a["c_ctx"], a["c"][0]]).reshape(2, KD, P).transpose(2, 1, 0),
        "bmod": a["b_mod"].reshape(DEPTH, 48, P).transpose(2, 0, 1),
        "lbz": a["hgrn_lb_logits"].reshape(2, DEPTH, HEADS, P).transpose(3, 0, 1, 2),
        "ident": np.eye(P, dtype=np.float32), "cos": cos, "sin": sin,
        "iota": np.tile(np.arange(TOPK, dtype=np.float32), (P, 1)),
        "masks": level_masks(), "reset": reset.reshape(P, NT * 129),
        "hgrn_norm_g": a["hgrn_norm_g"], "q_norm_g": a["q_norm_g"], "k_norm_g": a["k_norm_g"],
        "state": a["state_hgrn"].reshape(DEPTH * 2 * HEADS, P, P),
        "cache_k": a["cache_attn_k"].reshape(DEPTH, P, KV * HD),
        "cache_v": a["cache_attn_v"].reshape(DEPTH, P, KV * HD),
        "lnrows": np.stack([a[n] for n in ("ln1_g", "ln1_b", "ln2_g", "ln2_b")], axis=1),
        "peer_u": a["peer_u"].reshape(DEPTH * N_EXPERTS, D), "peer_v": a["peer_v"].reshape(DEPTH * N_EXPERTS, D),
        "wblk": wblk,
    }


def kernel(**inputs):
    import concourse.bacc as bacc
    from concourse.bass_utils import run_bass_kernel_spmd

    nc = bacc.Bacc("TRN2", target_bir_lowering=False, num_devices=1)
    arrays, ins = {}, {}
    for name, a in layout(inputs).items():
        a = np.ascontiguousarray(a)
        arrays[f"in_{name}"] = a
        ins[name] = nc.dram_tensor(f"in_{name}", a.shape, mybir.dt.from_np(a.dtype), kind="ExternalInput").ap()
    shapes = [(1, P, D), (1, LAT, D), (DEPTH, P, KV * HD), (DEPTH, P, KV * HD), (DEPTH * 2 * HEADS, P, P)]
    outs = [nc.dram_tensor(f"out_{i}", s, F32, kind="ExternalOutput").ap() for i, s in enumerate(shapes)]
    build(nc, ins, outs)
    r = run_bass_kernel_spmd(nc, [arrays], core_ids=[0])
    got = [r.results[0][f"out_{i}"] for i in range(len(shapes))]
    return (got[0], got[1], got[2].reshape(1, DEPTH, P, KV, HD), got[3].reshape(1, DEPTH, P, KV, HD),
            got[4].reshape(1, DEPTH, 2, HEADS, P, P))
```

```python
from contextlib import ExitStack

import numpy as np

import concourse.bass as bass
from concourse import mybir

F32 = mybir.dt.float32
U32 = mybir.dt.uint32
U8 = mybir.dt.uint8
ALU = mybir.AluOpType
ACT = mybir.ActivationFunctionType
AX = mybir.AxisListType

P = 128
DEPTH = 2
D = 1024
KD = D // P
NT = 5
T = NT * P
LAT = T - P
HALF = T // 2
HEADS = 8
KV = 4
HD = 64
QH = 16
GROUP = QH // KV
GRID_W = 64
PEER_H = 8
TOPK = 16
SLOTS = PEER_H * TOPK
NKEYS = 128
N_EXPERTS = NKEYS * NKEYS
CB = 512
ALPHA = float((2 * DEPTH) ** 0.25)
EPS = 1e-6
SCALE = HD ** -0.5
LOG_FLOOR = 2.0 ** -62
LEVELS = [64, 32, 16, 8, 4, 2, 1]
NL = len(LEVELS)
ROWS = 8
TURNS = SLOTS // ROWS
TURNS_A = 5
ALL_ROWS = tuple(range(ROWS))
PE_ROWS = (0, 2, 4, 6)
DIAGS = 4
STAGED = 2
B_MOD, B_GATE, B_HEAD, B_KV, B_Q, B_MIX, B_OUT, B_SK, B_PQ = 0, 12, 14, 22, 23, 25, 33, 35, 36
NB = 40
SH1, SC1, G1, SH2, SC2, G2 = range(6)


def build(nc, ins, outs):
    with ExitStack() as ctx:
        def sb(name, shape, dt=F32):
            return ctx.enter_context(nc.sbuf_tensor(name, shape, dt))

        def sem(name):
            return ctx.enter_context(nc.semaphore(name))

        x = sb("x", [P, NT, D])
        ring = sb("ring", [P, 2, KD, CB])
        ident = sb("ident", [P, P])
        cos = sb("cos", [P, NT - 1, 32])
        sin = sb("sin", [P, NT - 1, 32])
        reset = sb("reset", [P, NT * 129])
        iota = sb("iota", [P, TOPK])
        masks = sb("masks", [P, 2 * NL + 1, P], U8)
        bmod = sb("bmod", [P, DEPTH, 48])
        modv = sb("modv", [P, 48, 2])
        cond = sb("cond", [P, KD, 2])
        rows_g = sb("rows_g", [P, DEPTH, P + 2 * HD])
        lbz = sb("lbz", [P, 2, DEPTH, HEADS])
        lbf = sb("lbf", [P, DEPTH * 2 * HEADS])
        omlb = sb("omlb", [P, DEPTH * 2 * HEADS])
        small = sb("small", [P, 256])
        layer_base = sb("layer_base", [P, 1])
        hT = sb("hT", [P, KD, T])
        late = sb("late", [P, 8192])
        arena = sb("arena", [P, 23552])
        banks = ctx.enter_context(nc.psum_tensor("banks", [P, 8, 512], F32))

        def pair(b, n=T):
            return banks[:, b:b + 2, :].rearrange("p a n -> p (a n)")[:, 0:n]

        def halves(b):
            return banks[:, b:b + 2, 0:HALF]

        class Region:
            def __init__(self, base, at=0):
                self.base, self.at = base, at

            def take(self, n):
                self.at += n
                assert self.at <= self.base.shape[1], (self.at, self.base.shape)
                return self.base[:, self.at - n:self.at]

        def r3(ap, b):
            return ap.rearrange("p (a b) -> p a b", b=b)

        modrows = arena[0:2, 0:6 * D]
        sgate = r3(arena[:, 0:5120], D)
        orecT = r3(arena[:, 5120:10240], T)
        reg = Region(arena, 10240)
        hq, hv, hk0, hk1, ksum, sc = (reg.take(T) for _ in range(6))
        hk = [hk0, hk1]
        sig = [reg.take(T) for _ in range(2)]
        gl = [r3(reg.take(NT * 129), 129) for _ in range(2)]
        pre = [r3(reg.take(NT * 129), 129) for _ in range(2)]
        E = [reg.take(T) for _ in range(2)]
        X = [reg.take(T) for _ in range(2)]
        qdec = [reg.take(T) for _ in range(2)]
        reg2 = Region(late)
        kdT = [reg2.take(T) for _ in range(2)]
        S = [r3(reg2.take(4 * P), P) for _ in range(2)]
        o1 = reg2.take(T)
        osq = reg2.take(T)
        tot = r3(reg2.take(2 * NT), NT)
        hnew = r3(late[:, 7936:8192], P)
        oattT = r3(arena[:, 0:5120], T)
        reg = Region(arena, 10240)
        qkv = r3(reg.take(NT * 1536), 1536)
        KT = r3(reg.take(2 * 768), 768)
        kpast = reg.take(256)
        vpast = reg.take(256)
        qTs = [reg.take(T) for _ in range(2)]
        pr = [reg.take(T) for _ in range(2)]
        reg2 = Region(late)
        PT = [r3(reg2.take(T), P) for _ in range(2)]
        onorm = reg2.take(T)
        qstage = [r3(reg2.take(T), P) for _ in range(2)]
        nt1 = reg2.take(NT * CB)
        nt2 = arena[:, 0:NT * CB]
        low = [small[:, 128 + 10 * b:138 + 10 * b] for b in range(2)]
        psum = [small[:, 148 + 10 * b:158 + 10 * b] for b in range(2)]
        yT = r3(arena[:, 10240:15360], T)
        reg = Region(arena, 15360)
        sgA = [reg.take(HALF) for _ in range(2)]
        sgB = [reg.take(HALF) for _ in range(2)]
        y1 = reg.take(HALF)
        y2 = reg.take(HALF)
        lnrows = r3(late[:, 0:4096], D)
        bca = r3(late[:, 4096:6144], D)
        skT = r3(late[:, 6144:8192], P)
        bcb = r3(arena[:, 0:4096], D)
        outtmp = arena[:, 15360:15872]
        h2 = r3(arena[:, 15360:20480], D)
        scores = arena[:, 0:10240].rearrange("p (t u n) -> p t u n", t=NT, n=NKEYS)
        qT = r3(arena[:, 10240:10240 + 4 * T], T)
        stage = arena[:, 10240:12288]
        work = arena[:, 12288:14336]
        reg = Region(late, 6144)
        tv = r3(reg.take(256), TOPK)
        ti = r3(reg.take(256), TOPK)
        tif = r3(reg.take(256), TOPK)
        bs, bp, bq, paf, pbf, e1, e2, av, gate = (reg.take(SLOTS) for _ in range(9))
        wv = reg.take(SLOTS)
        gsum, idxs = small[:, 232:240], small[:, 240:248]
        diag = [arena[:, 256 + j * P:256 + (j + 1) * P] for j in range(DIAGS)]
        hTf = hT[:, :, :].rearrange("p k t -> p (k t)")
        grow = [hTf[:, j * D:(j + 1) * D] for j in range(5)] + \
               [arena[:, 20480 + j * D:20480 + (j + 1) * D] for j in range(3)]
        acc = arena[:, 14336:15360]

        init = sem("init")
        cond_ready = sem("cond_ready")
        lb_shifted, lb_exped, lb_ready = sem("lb_shifted"), sem("lb_exped"), sem("lb_ready")
        w_full = [sem(f"w_full{s}") for s in range(2)]
        w_free = [sem(f"w_free{s}") for s in range(2)]
        bank_free = [sem(f"bank_free{b}") for b in range(8)]
        to_act = [sem(f"to_act{b}") for b in range(8)]
        to_dve = [sem(f"to_dve{b}") for b in range(8)]
        left = {e: sem(f"left_{e}") for e in ("pe", "act", "dve")}
        enter = {e: sem(f"enter_{e}") for e in ("pe", "act", "dve")}
        modrows_ready = sem("modrows_ready")
        heads_set = sem("heads_set")
        s0_full = sem("s0_full")
        kneg_ready, log_ready, pre_ready = sem("kneg_ready"), sem("log_ready"), sem("pre_ready")
        v_ready, ksum_ready, tot_ready = sem("v_ready"), sem("ksum_ready"), sem("tot_ready")
        dif_ready = [sem(f"dif_ready{b}") for b in range(2)]
        exp_ready = [sem(f"exp_ready{b}") for b in range(2)]
        e_free = [sem(f"e_free{b}") for b in range(2)]
        x_ready = [sem(f"x_ready{b}") for b in range(2)]
        kdt_ready, sc_ready, state_ready = sem("kdt_ready"), sem("sc_ready"), sem("state_ready")
        hnew_ready, hnew_sent = sem("hnew_ready"), sem("hnew_sent")
        osq_ready, ms_ready, rms_ready = sem("osq_ready"), sem("ms_ready"), sem("rms_ready")
        o1_ready = sem("o1_ready")
        qkv_ready, past_full = sem("qkv_ready"), sem("past_full")
        qkn_pool, kn_pe, kn_act = sem("qkn_pool"), sem("kn_pe"), sem("kn_act")
        kvnew_sent, kt_ready = sem("kvnew_sent"), sem("kt_ready")
        qst_ready = [sem(f"qst_ready{b}") for b in range(2)]
        qst_free = [sem(f"qst_free{b}") for b in range(2)]
        low_ready = [sem(f"low_ready{b}") for b in range(2)]
        prob_ready = [sem(f"prob_ready{b}") for b in range(2)]
        pt_ready = [sem(f"pt_ready{b}") for b in range(2)]
        onorm_ready = sem("onorm_ready")
        sg_ready = [sem(f"sg_ready{b}") for b in range(2)]
        sg_free = [sem(f"sg_free{b}") for b in range(2)]
        bc_ready, ln_full = sem("bc_ready"), sem("ln_full")
        var_ready, std_ready = sem("var_ready"), sem("std_ready")
        h2_ready, h2T_ready = sem("h2_ready"), sem("h2T_ready")
        sk_arrived, sk_ready, qt_ready = sem("sk_arrived"), sem("sk_ready"), sem("qt_ready")
        stage_ready, stage_free = sem("stage_ready"), sem("stage_free")
        softexp_ready = sem("softexp_ready")
        idx_ready, idx_staged = sem("idx_ready"), sem("idx_staged")
        row_full = [sem(f"row_full{j}") for j in range(ROWS)]
        row_free = [sem(f"row_free{j}") for j in range(ROWS)]
        dots_ready, gelu_ready, wv_ready = sem("dots_ready"), sem("gelu_ready"), sem("wv_ready")
        acc_zero, acc_seen, acc_done = sem("acc_zero"), sem("acc_seen"), sem("acc_done")
        acc_free = sem("acc_free")
        diag_ready, diag_used = sem("diag_ready"), sem("diag_used")
        done, stored = sem("done"), sem("stored")

        def phase_barrier(eng, me):
            if me == "pool":
                for other in left:
                    eng.wait_ge(left[other], 1)
                    eng.sem_inc(left[other], -1)
                for other in left:
                    eng.drain().then_inc(enter[other], 1)
            else:
                eng.drain().then_inc(left[me], 1)
                eng.wait_ge(enter[me], 1)
                eng.sem_inc(enter[me], -1)

        INIT = 16 * 14
        units = [(d, s) for s in LEVELS for d in range(2)]

        block = ctx.enter_context(nc.Block())

        @block.sync
        def _(sp):
            with sp.Fori(0, DEPTH * NB // 2) as i:
                for s in range(2):
                    sp.wait_ge(w_free[s], 1)
                    sp.sem_inc(w_free[s], -1)
                    sp.dma_start(ring[:, s].rearrange("p k n -> p (k n)"),
                                 ins["wblk"][bass.ds(2 * i + s, 1)].rearrange("a p n -> p (a n)")
                                 ).then_inc(w_full[s], 16)
            sp.wait_ge(done, 1)
            sp.dma_start(outs[0][0], x[:, 0, :]).then_inc(stored, 16)
            sp.dma_start(outs[1][0].rearrange("(t p) d -> p t d", p=P), x[:, 1:NT, :]
                         ).then_inc(stored, 16)
            sp.wait_ge(stored, 32)

        @block.gpsimd
        def _(pool):
            for s in w_free + e_free + qst_free + sg_free + row_free + bank_free \
                    + [acc_free]:
                pool.sem_inc(s, 1)
            pool.sem_inc(hnew_sent, 32)
            pool.sem_inc(diag_used, DIAGS - 1)
            nc.gpsimd.memset(layer_base[:], 0.0)
            pool.wait_ge(init, INIT)
            with pool.Fori(0, DEPTH) as l:
                phase_barrier(pool, "pool")
                phase_barrier(pool, "pool")
                phase_barrier(pool, "pool")
                for d in range(2):
                    nc.gpsimd.memset(gl[d][:, :, 0:1], 0.0)
                pool.drain().then_inc(heads_set, 1)
                with pool.Fori(0, HEADS) as h:
                    pool.wait_ge(pre_ready, 2)
                    pool.sem_inc(pre_ready, -2)
                    for n, (d, s) in enumerate(units):
                        base = pre[d][:, :, 1 - d:129 - d]
                        base = base.rearrange("p t (b s) -> p t b s", s=2 * s)
                        ref = pre[d][:, :, 0:128].rearrange("p t (b s) -> p t b s", s=2 * s)[:, :, :, s:s + 1]
                        pool.wait_ge(e_free[n % 2], 1)
                        pool.sem_inc(e_free[n % 2], -1)
                        nc.gpsimd.tensor_tensor(
                            E[n % 2].rearrange("p (t b s) -> p t b s", t=NT, s=2 * s), base,
                            ref.to_broadcast([P, NT, P // (2 * s), 2 * s]), ALU.subtract
                        ).then_inc(dif_ready[n % 2], 1)
                    for n, (d, to_end) in enumerate([(0, 0), (0, 1), (1, 1), (1, 0)]):
                        base = pre[d][:, :, 1 - d:129 - d]
                        ref = pre[d][:, :, 128 * to_end:128 * to_end + 1].to_broadcast([P, NT, P])
                        pool.wait_ge(e_free[n % 2], 1)
                        pool.sem_inc(e_free[n % 2], -1)
                        nc.gpsimd.tensor_tensor(r3(E[n % 2], P), base, ref, ALU.subtract
                                                ).then_inc(dif_ready[n % 2], 1)
                phase_barrier(pool, "pool")
                pool.wait_ge(qkn_pool, 1)
                pool.sem_inc(qkn_pool, -1)
                with pool.Fori(0, QH // 4) as i:
                    for b in range(2):
                        pool.wait_ge(qst_free[b], 1)
                        pool.sem_inc(qst_free[b], -1)
                        nc.gpsimd.tensor_copy(qstage[b], qkv[:, :, bass.ds((2 * i + b) * P, P)]
                                              ).then_inc(qst_ready[b], 1)
                phase_barrier(pool, "pool")
                phase_barrier(pool, "pool")
                phase_barrier(pool, "pool")
                pool.wait_ge(sk_arrived, 1)
                pool.sem_inc(sk_arrived, -1)
                nc.gpsimd.tensor_copy(skT, ring[:, B_SK % 2].rearrange("p k (a n) -> p (k a) n", n=NKEYS)[:, 0:16])
                pool.drain().then_inc(sk_ready, 1)
                pool.drain().then_inc(w_free[B_SK % 2], 1)
                phase_barrier(pool, "pool")
                with pool.Fori(0, NT) as t:
                    pool.wait_ge(idx_ready, 1)
                    pool.sem_inc(idx_ready, -1)
                    for table in ("peer_u", "peer_v"):
                        with pool.Fori(0, SLOTS // ROWS) as i:
                            for r in range(0, ROWS, STAGED):
                                for j in range(r, r + STAGED):
                                    pool.wait_ge(row_free[j], 1)
                                    pool.sem_inc(row_free[j], -1)
                                nc.gpsimd.tensor_copy(
                                    idxs[:, r:r + STAGED].bitcast(U32),
                                    arena[:, bass.ds(t * 2048 + i * ROWS + r, STAGED)].bitcast(U32)
                                ).then_inc(idx_staged, 1)
                                pool.wait_ge(idx_staged, 1)
                                pool.sem_inc(idx_staged, -1)
                                for j in range(r, r + STAGED):
                                    nc.gpsimd.indirect_dma_start(
                                        grow[j], None, ins[table],
                                        bass.IndirectOffsetOnAxis(ap=idxs[:, j:j + 1].bitcast(U32), axis=0)
                                    ).then_inc(row_full[j], 16)
                phase_barrier(pool, "pool")
                phase_barrier(pool, "pool")

        @block.scalar
        def _(act):
            loads = [(x[:, 0, :], ins["x_prompt"]),
                     (x[:, 1:NT, :], ins["x_sample"].rearrange("(t p) d -> p t d", p=P)),
                     (cond[:], ins["cond"]), (bmod[:], ins["bmod"]), (lbz[:], ins["lbz"]),
                     (ident[:], ins["ident"]), (cos[:], ins["cos"]), (sin[:], ins["sin"]),
                     (iota[:], ins["iota"]), (arena[:, 0:(2 * NL + 1) * P], ins["masks"]), (reset[:], ins["reset"])]
            for dst, src in loads:
                act.dma_start(dst, src).then_inc(init, 16)
            for n, (a, b) in enumerate([(0, P), (P, P + HD), (P + HD, P + 2 * HD)]):
                act.dma_start(rows_g[:, :, a:b], ins[("hgrn_norm_g", "q_norm_g", "k_norm_g")[n]]
                              .partition_broadcast(P)).then_inc(init, 16)
            act.wait_ge(init, INIT)
            nc.scalar.activation(cond[:], cond[:], ACT.Silu).then_inc(cond_ready, 1)
            act.wait_ge(lb_shifted, 1)
            nc.scalar.activation(lbz[:], lbz[:], ACT.Exp).then_inc(lb_exped, 1)
            act.wait_ge(lb_ready, 1)

            def square_root(n):
                act.wait_ge(var_ready, 1)
                act.sem_inc(var_ready, -1)
                nc.scalar.activation(small[:, 0:n], small[:, 0:n], ACT.Sqrt).then_inc(std_ready, 1)

            with act.Fori(0, DEPTH) as l:
                phase_barrier(act, "act")
                for k in range(KD):
                    b = 4 + k % 4
                    act.wait_ge(to_act[b], 1)
                    act.sem_inc(to_act[b], -1)
                    nc.scalar.activation(hT[:, k, 0:P], banks[:, b, 0:P], ACT.Identity,
                                         bias=modv[:, SH1 * 8 + k, 0:1], scale=modv[:, SC1 * 8 + k, 0:1]
                                         ).then_inc(bank_free[b], 1)
                phase_barrier(act, "act")
                for g in range(2 * NT):
                    b = g % 8
                    act.wait_ge(to_act[b], 1)
                    act.sem_inc(to_act[b], -1)
                    nc.scalar.activation(sgate[:, g % NT, g // NT * CB:(g // NT + 1) * CB], banks[:, b, :],
                                         ACT.Silu).then_inc(bank_free[b], 1)
                phase_barrier(act, "act")
                act.wait_ge(heads_set, 1)
                act.sem_inc(heads_set, -1)
                with act.Fori(0, HEADS) as h:
                    for d in range(2):
                        act.dma_start(S[d][:, 3 * d, :], ins["state"][bass.ds((l * 2 + d) * HEADS + h, 1)]
                                      .rearrange("a p n -> p (a n)")).then_inc(s0_full, 16)
                    act.wait_ge(to_act[0], 1)
                    act.sem_inc(to_act[0], -1)
                    nc.scalar.activation(hq.rearrange("p (a n) -> p a n", a=2), halves(0), ACT.Silu
                                         ).then_inc(bank_free[0], 1)
                    for d in range(2):
                        b = 2 + 2 * d
                        act.wait_ge(to_act[b], 1)
                        act.sem_inc(to_act[b], -1)
                        nc.scalar.activation(hk[d].rearrange("p (a n) -> p a n", a=2), halves(b), ACT.Sigmoid,
                                             scale=-1.0).then_inc(kneg_ready, 1)
                        nc.scalar.activation(sig[d].rearrange("p (a n) -> p a n", a=2), halves(b), ACT.Sigmoid
                                             ).then_inc(bank_free[b], 1)
                    act.wait_ge(to_act[6], 1)
                    act.sem_inc(to_act[6], -1)
                    nc.scalar.copy(hv, pair(6)).then_inc(bank_free[6], 1)
                    act.drain().then_inc(v_ready, 1)
                    for d in range(2):
                        c = bass.ds((l * 2 + d) * HEADS + h, 1)
                        nc.scalar.activation(gl[d][:, :, 1:129], r3(sig[d], P), ACT.Ln,
                                             bias=lbf[:, c], scale=omlb[:, c]).then_inc(log_ready, 1)
                    for n, (d, s) in enumerate(units):
                        act.wait_ge(dif_ready[n % 2], 1)
                        act.sem_inc(dif_ready[n % 2], -1)
                        e = E[n % 2].rearrange("p (b s) -> p b s", s=2 * s)
                        nc.scalar.activation(e[:, :, 0:s], e[:, :, 0:s], ACT.Exp, scale=-1.0)
                        nc.scalar.activation(e[:, :, s:2 * s], e[:, :, s:2 * s], ACT.Exp
                                             ).then_inc(exp_ready[n % 2], 1)
                    for n, sign in enumerate([1.0, -1.0, -1.0, 1.0]):
                        act.wait_ge(dif_ready[n % 2], 1)
                        act.sem_inc(dif_ready[n % 2], -1)
                        nc.scalar.activation(E[n % 2], E[n % 2], ACT.Exp, scale=sign
                                             ).then_inc(exp_ready[n % 2], 1)
                    for d in range(2):
                        nc.scalar.activation(tot[:, d, :], pre[d][:, :, 128:129].rearrange("p t a -> p (t a)"),
                                             ACT.Exp).then_inc(tot_ready, 1)
                    for d in range(2):
                        act.wait_ge(to_act[4 + 2 * d], 1)
                        act.sem_inc(to_act[4 + 2 * d], -1)
                        nc.scalar.copy(kdT[d], pair(4 + 2 * d)).then_inc(bank_free[4 + 2 * d], 1)
                        act.drain().then_inc(kdt_ready, 1)
                    act.wait_ge(hnew_ready, 1)
                    act.sem_inc(hnew_ready, -1)
                    for d in range(2):
                        act.dma_start(outs[4][bass.ds((l * 2 + d) * HEADS + h, 1)].rearrange("a p n -> p (a n)"),
                                      hnew[:, d, :]).then_inc(hnew_sent, 16)
                    act.wait_ge(to_act[4], 1)
                    act.sem_inc(to_act[4], -1)
                    nc.scalar.activation(osq, pair(4), ACT.Square).then_inc(osq_ready, 1)
                    square_root(NT)
                    act.wait_ge(to_act[6], 1)
                    act.sem_inc(to_act[6], -1)
                    nc.scalar.copy(orecT[:, bass.ds(h, 1), :].rearrange("p a n -> p (a n)"), pair(6)
                                   ).then_inc(bank_free[6], 1)
                phase_barrier(act, "act")
                act.dma_start(kpast, ins["cache_k"][bass.ds(l, 1)].rearrange("a p n -> p (a n)")).then_inc(past_full, 16)
                act.dma_start(vpast, ins["cache_v"][bass.ds(l, 1)].rearrange("a p n -> p (a n)")).then_inc(past_full, 16)
                for g in range(3 * NT):
                    b = g % 8
                    c = (1024, 0, 512)[g // NT]
                    act.wait_ge(to_act[b], 1)
                    act.sem_inc(to_act[b], -1)
                    nc.scalar.copy(qkv[:, g % NT, c:c + CB], banks[:, b, :]).then_inc(bank_free[b], 1)
                    if g % NT == NT - 1:
                        act.drain().then_inc(qkv_ready, 1)
                    if g == NT + 1:
                        square_root(NT * KV)
                    if g == 2 * NT + 1:
                        square_root(NT * 8)
                square_root(NT * 8)
                act.wait_ge(kn_act, 1)
                act.sem_inc(kn_act, -1)
                for n in range(2):
                    act.dma_start(outs[2 + n][bass.ds(l, 1)].rearrange("a p n -> p (a n)"),
                                  qkv[:, 0, 1024 + 256 * n:1280 + 256 * n]).then_inc(kvnew_sent, 16)
                for kp in range(2):
                    act.wait_ge(to_act[2 * kp], 1)
                    act.sem_inc(to_act[2 * kp], -1)
                    nc.scalar.copy(KT[:, kp, :], pair(2 * kp, 768)).then_inc(bank_free[2 * kp], 1)
                    act.drain().then_inc(kt_ready, 1)

                def queries(b):
                    act.wait_ge(to_act[4], 1)
                    act.sem_inc(to_act[4], -1)
                    nc.scalar.copy(qTs[b], pair(4)).then_inc(bank_free[4], 1)
                    act.sem_inc(qst_free[b], 1)

                def exponentials(b, u):
                    n = P if u % NT == 0 else T
                    act.wait_ge(low_ready[u % 2], 1)
                    act.sem_inc(low_ready[u % 2], -1)
                    nc.scalar.activation(pr[u % 2][:, 0:n], pair(2 * (u % 2), n), ACT.Exp,
                                         bias=low[b][:, u:u + 1], scale=-1.0, accum_out=psum[b][:, u:u + 1]
                                         ).then_inc(prob_ready[u % 2], 1)

                def deliver(p):
                    act.wait_ge(to_act[4], 1)
                    act.sem_inc(to_act[4], -1)
                    nc.scalar.copy(oattT[:, bass.ds(p, 1), :].rearrange("p a n -> p (a n)"), pair(4)
                                   ).then_inc(bank_free[4], 1)

                def att_pair(b, before, more):
                    for u in range(2 * NT):
                        if u % 2 == 0:
                            act.wait_ge(to_act[4], 1)
                            act.sem_inc(to_act[4], -1)
                            n = 1 if u % NT == 0 else NT
                            nc.scalar.copy(PT[0][:, 0:n, :], r3(pair(4, n * P), P)).then_inc(bank_free[4], 1)
                            act.drain().then_inc(pt_ready[0], 1)
                        if u + 2 < 2 * NT:
                            exponentials(b, u + 2)
                        elif more:
                            exponentials(1 - b, u + 2 - 2 * NT)
                        if u == 1 and before is not None:
                            deliver(before)
                        if u == 5 and more:
                            queries(1 - b)

                queries(0)
                for u in range(2):
                    exponentials(0, u)
                att_pair(0, None, True)
                with act.Fori(0, QH // 4 - 1) as i:
                    att_pair(1, 2 * i, True)
                    att_pair(0, 2 * i + 1, True)
                att_pair(1, QH // 2 - 2, False)
                deliver(QH // 2 - 1)
                act.wait_ge(kvnew_sent, 32)
                act.sem_inc(kvnew_sent, -32)
                phase_barrier(act, "act")
                with act.Fori(0, KD):
                    for f in range(2):
                        act.wait_ge(sg_free[f], 1)
                        act.sem_inc(sg_free[f], -1)
                        act.wait_ge(to_act[4 * f], 1)
                        act.sem_inc(to_act[4 * f], -1)
                        nc.scalar.activation(sgA[f], banks[:, 4 * f, 0:HALF], ACT.Sigmoid
                                             ).then_inc(bank_free[4 * f], 1)
                        act.wait_ge(to_act[4 * f + 1], 1)
                        act.sem_inc(to_act[4 * f + 1], -1)
                        nc.scalar.activation(sgB[f], banks[:, 4 * f + 1, 0:HALF], ACT.Sigmoid
                                             ).then_inc(bank_free[4 * f + 1], 1)
                        act.drain().then_inc(sg_ready[f], 1)
                phase_barrier(act, "act")
                act.dma_start(lnrows, ins["lnrows"][bass.ds(l, 1)].rearrange("a r n -> (a r) n")
                              .partition_broadcast(P)).then_inc(ln_full, 16)
                for v, dst in enumerate([bca[:, 0], bca[:, 1], bcb[:, 0], bcb[:, 1], bcb[:, 2], bcb[:, 3]]):
                    b = 2 * (v % 4)
                    act.wait_ge(to_act[b], 1)
                    act.sem_inc(to_act[b], -1)
                    nc.scalar.copy(dst, pair(b, D)).then_inc(bank_free[b], 1)
                act.drain().then_inc(bc_ready, 1)
                square_root(NT)
                phase_barrier(act, "act")
                for t in range(NT):
                    b = 2 * (t % 4)
                    act.wait_ge(to_act[b], 1)
                    act.sem_inc(to_act[b], -1)
                    nc.scalar.copy(hT[:, :, t * P:(t + 1) * P], r3(pair(b, D), P)).then_inc(bank_free[b], 1)
                    act.drain().then_inc(h2T_ready, 1)
                with act.Fori(0, 4):
                    for u in range(4):
                        b = 2 * (u % 2)
                        act.wait_ge(to_act[b], 1)
                        act.sem_inc(to_act[b], -1)
                        nc.scalar.copy(qT[:, u, :].rearrange("p (a n) -> p a n", a=2), halves(b)
                                       ).then_inc(bank_free[b], 1)
                        act.drain().then_inc(qt_ready, 1)
                phase_barrier(act, "act")
                for c in range(2):
                    act.wait_ge(to_act[2 * c], 1)
                    act.sem_inc(to_act[2 * c], -1)
                    nc.scalar.copy(bca[:, c], pair(2 * c, D)).then_inc(bank_free[2 * c], 1)
                nc.scalar.copy(stage, arena[:, 0:2048]).then_inc(stage_ready, 1)

                def peer_act(t, more):
                    act.wait_ge(dots_ready, 1)
                    act.sem_inc(dots_ready, -1)
                    nc.scalar.activation(gate, gate, ACT.Exp).then_inc(softexp_ready, 1)
                    nc.scalar.activation(av, av, ACT.Gelu).then_inc(gelu_ready, 1)
                    if more:
                        act.wait_ge(stage_free, 1)
                        act.sem_inc(stage_free, -1)
                        nc.scalar.copy(stage, arena[:, bass.ds((t + 1) * 2048, 2048)]).then_inc(stage_ready, 1)
                    act.wait_ge(wv_ready, 1)
                    act.sem_inc(wv_ready, -1)
                    for first, count, mine in ((0, TURNS_A, ALL_ROWS), (TURNS_A, TURNS - TURNS_A, PE_ROWS)):
                        with act.Fori(0, count) as i:
                            for n, j in enumerate(mine):
                                act.wait_ge(diag_used, 1)
                                act.sem_inc(diag_used, -1)
                                nc.scalar.activation(diag[n % DIAGS], ident[:], ACT.Copy,
                                                     scale=wv[:, bass.ds((i + first) * ROWS + j, 1)]
                                                     ).then_inc(diag_ready, 1)
                    act.wait_ge(to_act[4], 1)
                    act.sem_inc(to_act[4], -1)
                    nc.scalar.copy(h2[:, bass.ds(t, 1), :].rearrange("p a n -> p (a n)"), pair(4, D)
                                   ).then_inc(bank_free[4], 1)

                with act.Fori(0, NT - 1) as t:
                    peer_act(t, True)
                peer_act(NT - 1, False)
                phase_barrier(act, "act")
                square_root(NT)
                phase_barrier(act, "act")

        @block.tensor
        def _(pe):
            def project(b, s, c, rhs):
                pe.wait_ge(bank_free[b], 1)
                pe.sem_inc(bank_free[b], -1)
                for f in range(2):
                    for k in range(KD):
                        last = nc.tensor.matmul(banks[:, b + f, 0:HALF], ring[:, s, k, c:c + P],
                                                rhs[:, k, f * HALF:(f + 1) * HALF], start=k == 0, stop=k == KD - 1)
                return last

            def tokenwise(b, s, lhs, t):
                pe.wait_ge(bank_free[b], 1)
                pe.sem_inc(bank_free[b], -1)
                for k in range(KD):
                    last = nc.tensor.matmul(banks[:, b, :], lhs[:, k, t * P:(t + 1) * P], ring[:, s, k, :],
                                            start=k == 0, stop=k == KD - 1)
                return last

            def at(b, t):
                return banks[:, b + t // 4, t % 4 * P:(t % 4 + 1) * P]

            def spread(b, part, c):
                pe.wait_ge(bank_free[b], 1)
                pe.sem_inc(bank_free[b], -1)
                for k in range(KD):
                    last = nc.tensor.matmul(at(b, k), modv[:, part * 8 + k, c:c + 1].to_broadcast([P, P]),
                                            ident[:], start=True, stop=True)
                last.then_inc(to_act[b], 1)

            pe.wait_ge(init, INIT)
            pe.wait_ge(cond_ready, 1)
            with pe.Fori(0, DEPTH) as l:
                with pe.Fori(0, B_GATE // 2):
                    for s in range(2):
                        pe.wait_ge(w_full[s], 16)
                        pe.sem_inc(w_full[s], -16)
                        pe.wait_ge(bank_free[s], 1)
                        pe.sem_inc(bank_free[s], -1)
                        for k in range(KD):
                            last = nc.tensor.matmul(banks[0:2, s, :], cond[:, k, :], ring[:, s, k, :],
                                                    start=k == 0, stop=k == KD - 1)
                        last.then_inc(to_dve[s], 1)
                        pe.drain().then_inc(w_free[s], 1)
                pe.wait_ge(modrows_ready, 1)
                pe.sem_inc(modrows_ready, -1)
                pe.wait_ge(bank_free[2], 1)
                pe.sem_inc(bank_free[2], -1)
                for m in range(48):
                    last = nc.tensor.transpose(banks[:, 2, 2 * m:2 * m + 2], modrows[:, m * P:(m + 1) * P],
                                               ident[0:2, 0:2])
                last.then_inc(to_dve[2], 1)
                phase_barrier(pe, "pe")
                for k in range(KD):
                    b = k % 4
                    pe.wait_ge(bank_free[4 + b], 1)
                    pe.sem_inc(bank_free[4 + b], -1)
                    nc.tensor.transpose(banks[:, 4 + b, 0:P], x[:, 0, k * P:(k + 1) * P], ident[:]
                                        ).then_inc(to_act[4 + b], 1)
                    pe.wait_ge(bank_free[b], 1)
                    pe.sem_inc(bank_free[b], -1)
                    for t in range(1, NT):
                        last = nc.tensor.transpose(banks[:, b, (t - 1) * P:t * P], x[:, t, k * P:(k + 1) * P], ident[:])
                    last.then_inc(to_dve[b], 1)
                phase_barrier(pe, "pe")
                for g in range(2 * NT):
                    s = (B_GATE + g // NT) % 2
                    if g % NT == 0:
                        pe.wait_ge(w_full[s], 16)
                        pe.sem_inc(w_full[s], -16)
                    tokenwise(g % 8, s, hT, g % NT).then_inc(to_act[g % 8], 1)
                    if g % NT == NT - 1:
                        pe.drain().then_inc(w_free[s], 1)
                phase_barrier(pe, "pe")
                with pe.Fori(0, HEADS // 2):
                    for s in range(2):
                        pe.wait_ge(w_full[s], 16)
                        pe.sem_inc(w_full[s], -16)
                        for c in range(3):
                            project(2 * c, s, c * P, hT).then_inc(to_act[2 * c], 1)
                        pe.wait_ge(bank_free[6], 1)
                        pe.sem_inc(bank_free[6], -1)
                        for t in range(NT):
                            for k in range(KD):
                                last = nc.tensor.matmul(at(6, t), hT[:, k, t * P:(t + 1) * P], ring[:, s, k, 3 * P:4 * P],
                                                        start=k == 0, stop=k == KD - 1)
                        last.then_inc(to_act[6], 1)
                        pe.drain().then_inc(w_free[s], 1)
                        for n in range(2 * NL):
                            b = 2 * (n % 2)
                            pe.wait_ge(x_ready[n % 2], 1)
                            pe.sem_inc(x_ready[n % 2], -1)
                            pe.wait_ge(bank_free[b], 1)
                            pe.sem_inc(bank_free[b], -1)
                            for t in range(NT):
                                xt = X[n % 2][:, t * P:(t + 1) * P]
                                last = nc.tensor.matmul(at(b, t), xt, xt, start=True, stop=True)
                            last.then_inc(to_dve[b], 1)
                        pe.wait_ge(ksum_ready, 1)
                        pe.sem_inc(ksum_ready, -1)
                        pe.wait_ge(bank_free[0], 1)
                        pe.sem_inc(bank_free[0], -1)
                        for t in range(NT):
                            last = nc.tensor.matmul(at(0, t), ksum[:, t * P:(t + 1) * P], hq[:, t * P:(t + 1) * P],
                                                    start=True, stop=True)
                        last.then_inc(to_dve[0], 1)
                        for d in range(2):
                            pe.wait_ge(x_ready[d], 1)
                            pe.sem_inc(x_ready[d], -1)
                            pe.wait_ge(bank_free[4 + 2 * d], 1)
                            pe.sem_inc(bank_free[4 + 2 * d], -1)
                            for t in range(NT):
                                last = nc.tensor.transpose(at(4 + 2 * d, t), X[d][:, t * P:(t + 1) * P], ident[:])
                            last.then_inc(to_act[4 + 2 * d], 1)
                        pe.wait_ge(v_ready, 1)
                        pe.sem_inc(v_ready, -1)
                        for d in range(2):
                            pe.wait_ge(kdt_ready, 1)
                            pe.sem_inc(kdt_ready, -1)
                            pe.wait_ge(bank_free[2 * d], 1)
                            pe.sem_inc(bank_free[2 * d], -1)
                            for t in range(NT):
                                last = nc.tensor.matmul(at(2 * d, t), kdT[d][:, t * P:(t + 1) * P],
                                                        hv[:, t * P:(t + 1) * P], start=True, stop=True)
                            last.then_inc(to_dve[2 * d], 1)
                        pe.wait_ge(sc_ready, 1)
                        pe.sem_inc(sc_ready, -1)
                        pe.wait_ge(state_ready, 1)
                        pe.sem_inc(state_ready, -1)
                        pe.wait_ge(bank_free[4], 1)
                        pe.sem_inc(bank_free[4], -1)
                        for t in range(NT):
                            tt = slice(t * P, (t + 1) * P)
                            last = nc.tensor.matmul(at(4, t), sc[:, tt], hv[:, tt], start=True, stop=t == 0)
                            for d in range(2 * (t > 0)):
                                last = nc.tensor.matmul(at(4, t), qdec[d][:, tt], S[d][:, t - 1, :],
                                                        start=False, stop=d == 1)
                        last.then_inc(to_act[4], 1)
                        pe.wait_ge(o1_ready, 1)
                        pe.sem_inc(o1_ready, -1)
                        pe.wait_ge(bank_free[6], 1)
                        pe.sem_inc(bank_free[6], -1)
                        for t in range(NT):
                            last = nc.tensor.transpose(at(6, t), o1[:, t * P:(t + 1) * P], ident[:])
                        last.then_inc(to_act[6], 1)
                phase_barrier(pe, "pe")
                for g in range(3 * NT):
                    s = (B_KV + g // NT) % 2
                    if g % NT == 0:
                        pe.wait_ge(w_full[s], 16)
                        pe.sem_inc(w_full[s], -16)
                    tokenwise(g % 8, s, hT, g % NT).then_inc(to_act[g % 8], 1)
                    if g % NT == NT - 1:
                        pe.drain().then_inc(w_free[s], 1)
                pe.wait_ge(past_full, 32)
                pe.sem_inc(past_full, -32)
                pe.wait_ge(kn_pe, 1)
                pe.sem_inc(kn_pe, -1)
                for b in (1, 3):
                    pe.wait_ge(bank_free[b], 1)
                    pe.sem_inc(bank_free[b], -1)
                    pe.sem_inc(bank_free[b], 1)
                for kp in range(2):
                    pe.wait_ge(bank_free[2 * kp], 1)
                    pe.sem_inc(bank_free[2 * kp], -1)
                    for t in range(NT + 1):
                        src = qkv[:, t, 1024 + kp * P:1024 + (kp + 1) * P] if t < NT else kpast[:, kp * P:(kp + 1) * P]
                        last = nc.tensor.transpose(at(2 * kp, t), src, ident[:])
                    last.then_inc(to_act[2 * kp], 1)
                pe.wait_ge(kt_ready, 2)
                pe.sem_inc(kt_ready, -2)

                def queries(b):
                    pe.wait_ge(qst_ready[b], 1)
                    pe.sem_inc(qst_ready[b], -1)
                    pe.wait_ge(bank_free[4], 1)
                    pe.sem_inc(bank_free[4], -1)
                    for t in range(NT):
                        last = nc.tensor.transpose(at(4, t), qstage[b][:, t, :], ident[:])
                    last.then_inc(to_act[4], 1)

                def score(b, u):
                    half, qt = divmod(u, NT)
                    rows = slice(64 * half, 64 * half + 64)
                    c = 2 * (u % 2)
                    lhs = qTs[b][rows, qt * P:(qt + 1) * P]
                    if qt == 0:
                        last = nc.tensor.matmul(banks[:, c, 0:P], lhs, KT[rows, b, 0:P], start=True, stop=True)
                    else:
                        nc.tensor.matmul(banks[:, c, :], lhs, KT[rows, b, P:T], start=True, stop=True)
                        last = nc.tensor.matmul(banks[:, c + 1, 0:P], lhs, KT[rows, b, T:T + P], start=True, stop=True)
                    last.then_inc(to_dve[c], 1)

                def turn(u):
                    pe.wait_ge(prob_ready[u % 2], 1)
                    pe.sem_inc(prob_ready[u % 2], -1)
                    pe.wait_ge(bank_free[4], 1)
                    pe.sem_inc(bank_free[4], -1)
                    for j in range(1 if u % NT == 0 else NT):
                        last = nc.tensor.transpose(at(4, j), pr[u % 2][:, j * P:(j + 1) * P], ident[:])
                    last.then_inc((to_act, to_dve)[u % 2][4], 1)

                def weigh(b, u):
                    half, qt = divmod(u, NT)
                    pe.wait_ge(pt_ready[u % 2], 1)
                    pe.sem_inc(pt_ready[u % 2], -1)
                    out = at(6, qt)[:, half * HD:(half + 1) * HD]
                    c = 1280 + (2 * b + half) * HD
                    if qt == 0:
                        last = nc.tensor.matmul(out, PT[u % 2][:, 0, :], qkv[:, 0, c:c + HD], start=True, stop=True)
                    for j in range(NT if qt else 0):
                        v = qkv[:, j + 1, c:c + HD] if j < NT - 1 else vpast[:, c - 1280:c - 1280 + HD]
                        last = nc.tensor.matmul(out, PT[u % 2][:, j, :], v, start=j == 0, stop=j == NT - 1)
                    if u == 2 * NT - 1:
                        last.then_inc(to_dve[6], 1)

                def output():
                    pe.wait_ge(bank_free[4], 1)
                    pe.sem_inc(bank_free[4], -1)
                    for t in range(NT):
                        last = nc.tensor.transpose(at(4, t), onorm[:, t * P:(t + 1) * P], ident[:])
                    last.then_inc(to_act[4], 1)

                def att_pair(b, before, more):
                    for u in range(2 * NT):
                        turn(u)
                        if u + 2 < 2 * NT:
                            score(b, u + 2)
                        elif more:
                            score(1 - b, u + 2 - 2 * NT)
                        if u == 1 and before:
                            pe.wait_ge(onorm_ready, 1)
                            pe.sem_inc(onorm_ready, -1)
                            output()
                        if u == 5 and more:
                            queries(1 - b)
                        if u:
                            weigh(b, u - 1)
                        elif before:
                            weigh(1 - b, 2 * NT - 1)

                for b in (0, 2, 6):
                    pe.wait_ge(bank_free[b], 1)
                    pe.sem_inc(bank_free[b], -1)
                queries(0)
                pe.wait_ge(bank_free[4], 1)
                pe.sem_inc(bank_free[4], -1)
                pe.sem_inc(bank_free[4], 1)
                for u in range(2):
                    score(0, u)
                att_pair(0, False, True)
                with pe.Fori(0, QH // 4 - 1):
                    att_pair(1, True, True)
                    att_pair(0, True, True)
                att_pair(1, True, False)
                weigh(1, 2 * NT - 1)
                pe.wait_ge(onorm_ready, 1)
                pe.sem_inc(onorm_ready, -1)
                output()
                for b in (0, 2, 6):
                    pe.sem_inc(bank_free[b], 1)
                phase_barrier(pe, "pe")
                with pe.Fori(0, KD // 2):
                    for n in range(2):
                        s = (B_MIX + n) % 2
                        pe.wait_ge(w_full[s], 16)
                        pe.sem_inc(w_full[s], -16)
                        for f in range(2):
                            for c, rhs in enumerate([hT, hT, orecT, oattT]):
                                b = 4 * f + c
                                pe.wait_ge(bank_free[b], 1)
                                pe.sem_inc(bank_free[b], -1)
                                for k in range(KD):
                                    last = nc.tensor.matmul(banks[:, b, 0:HALF], ring[:, s, k, c * P:(c + 1) * P],
                                                            rhs[:, k, f * HALF:(f + 1) * HALF],
                                                            start=k == 0, stop=k == KD - 1)
                                last.then_inc((to_act if c < 2 else to_dve)[b], 1)
                        pe.drain().then_inc(w_free[s], 1)
                phase_barrier(pe, "pe")
                for v, (part, c) in enumerate([(G1, 0), (G1, 1), (SC2, 0), (SH2, 0), (SC2, 1), (SH2, 1)]):
                    spread(2 * (v % 4), part, c)
                for b in range(0, 8, 2):
                    pe.wait_ge(bank_free[b], 1)
                    pe.sem_inc(bank_free[b], -1)
                    pe.sem_inc(bank_free[b], 1)
                for g in range(2 * NT):
                    s = (B_OUT + g // NT) % 2
                    if g % NT == 0:
                        pe.wait_ge(w_full[s], 16)
                        pe.sem_inc(w_full[s], -16)
                    tokenwise(g % 8, s, yT, g % NT).then_inc(to_dve[g % 8], 1)
                    if g % NT == NT - 1:
                        pe.drain().then_inc(w_free[s], 1)
                phase_barrier(pe, "pe")
                pe.wait_ge(w_full[B_SK % 2], 16)
                pe.sem_inc(w_full[B_SK % 2], -16)
                pe.sem_inc(sk_arrived, 1)
                for t in range(NT):
                    b = 2 * (t % 4)
                    pe.wait_ge(h2_ready, 1)
                    pe.sem_inc(h2_ready, -1)
                    pe.wait_ge(bank_free[b], 1)
                    pe.sem_inc(bank_free[b], -1)
                    for k in range(KD):
                        last = nc.tensor.transpose(at(b, k), h2[:, t, k * P:(k + 1) * P], ident[:])
                    last.then_inc(to_act[b], 1)
                pe.wait_ge(h2T_ready, NT)
                pe.sem_inc(h2T_ready, -NT)
                pe.wait_ge(sk_ready, 1)
                pe.sem_inc(sk_ready, -1)
                with pe.Fori(0, 2) as i:
                    for s in range(2):
                        def match(u):
                            b = 4 + 2 * (u % 2)
                            pe.wait_ge(qt_ready, 1)
                            pe.sem_inc(qt_ready, -1)
                            pe.wait_ge(bank_free[b], 1)
                            pe.sem_inc(bank_free[b], -1)
                            for t in range(NT):
                                last = nc.tensor.matmul(
                                    at(b, t), qT[:, u, t * P:(t + 1) * P],
                                    skT[:, bass.ds((2 * i + s) * 4 + u, 1), :].rearrange("p a n -> p (a n)"),
                                    start=True, stop=True)
                            last.then_inc(to_dve[b], 1)

                        pe.wait_ge(w_full[s], 16)
                        pe.sem_inc(w_full[s], -16)
                        for u in range(4):
                            project(2 * (u % 2), s, u * P, hT).then_inc(to_act[2 * (u % 2)], 1)
                            if u:
                                match(u - 1)
                        match(3)
                        pe.drain().then_inc(w_free[s], 1)
                phase_barrier(pe, "pe")
                for c in range(2):
                    spread(2 * c, G2, c)
                with pe.Fori(0, NT) as t:
                    pe.wait_ge(acc_zero, 1)
                    pe.sem_inc(acc_zero, -1)
                    pe.wait_ge(bank_free[4], 1)
                    pe.sem_inc(bank_free[4], -1)
                    for c in range(2):
                        last = nc.tensor.matmul(banks[:, 4 + c, :], ident[:], acc[:, c * CB:(c + 1) * CB],
                                                start=True, stop=False, skip_group_check=True)
                    last.then_inc(acc_seen, 1)
                    for first, count, mine in ((0, TURNS_A, ALL_ROWS), (TURNS_A, TURNS - TURNS_A, PE_ROWS)):
                        with pe.Fori(0, count) as i:
                            for n, j in enumerate(mine):
                                pe.wait_ge(diag_ready, 1)
                                pe.sem_inc(diag_ready, -1)
                                pe.wait_ge(row_full[j], (((l * NT + t) * 2 + 1) * TURNS + first + i + 1) * 16)
                                nc.tensor.matmul(banks[:, 4, :], diag[n % DIAGS], grow[j][:, 0:CB], start=False,
                                                 stop=False, skip_group_check=True
                                                 ).then_inc(diag_used, 1)
                                nc.tensor.matmul(banks[:, 5, :], diag[n % DIAGS], grow[j][:, CB:D], start=False,
                                                 stop=False, skip_group_check=True).then_inc(row_free[j], 1)
                    pe.wait_ge(acc_done, 1)
                    pe.sem_inc(acc_done, -1)
                    for c in range(2):
                        last = nc.tensor.matmul(banks[:, 4 + c, :], ident[:], acc[:, c * CB:(c + 1) * CB],
                                                start=False, stop=True, skip_group_check=True)
                    last.then_inc(to_act[4], 1)
                    pe.drain().then_inc(acc_free, 1)
                phase_barrier(pe, "pe")
                phase_barrier(pe, "pe")

        @block.vector
        def _(dve):
            V = nc.vector
            dve.wait_ge(init, INIT)
            z = [lbz[:, :, j, :] for j in range(DEPTH)]
            m = r3(small[:, 0:16], 8)
            V.tensor_tensor(m, z[0], z[1], ALU.max)
            dve.drain()
            for j in range(DEPTH):
                V.tensor_tensor(z[j], z[j], m, ALU.subtract).then_inc(lb_shifted, j)                    if j else V.tensor_tensor(z[j], z[j], m, ALU.subtract)
            V.tensor_scalar(rows_g[:, :, P:P + HD], rows_g[:, :, P:P + HD], -SCALE, None, ALU.mult)
            dve.wait_ge(lb_exped, 1)
            V.tensor_tensor(m, z[0], z[1], ALU.add)
            V.memset(lbf[:, 0:16], LOG_FLOOR)
            V.tensor_copy(masks[:].rearrange("p n i -> p (n i)"), arena[:, 0:(2 * NL + 1) * P])
            V.memset(omlb[:, 0:16], 1.0)
            dve.drain()
            V.reciprocal(small[:, 0:16], small[:, 0:16])
            dve.drain()
            V.tensor_tensor(r3(lbf[:, 16:32], 8), z[1], m, ALU.mult)
            dve.drain()
            V.tensor_scalar(omlb[:, 16:32], lbf[:, 16:32], -1.0, 1.0, ALU.mult, ALU.add)
            dve.drain()
            V.tensor_scalar(lbf[:, 16:32], lbf[:, 16:32], LOG_FLOOR, None, ALU.add).then_inc(lb_ready, 1)
            dve.drain()

            def inverse_root(n):
                dve.drain().then_inc(var_ready, 1)
                dve.wait_ge(std_ready, 1)
                dve.sem_inc(std_ready, -1)
                V.reciprocal(small[:, 0:n], small[:, 0:n])
                dve.drain()

            def layer_norm(gain, shift):
                stats = small[:, 64:64 + NT * 12].rearrange("p (t c s) -> p t c s", t=NT, c=2)
                mv = r3(small[:, 128:128 + 2 * NT], 2)
                for t in range(NT):
                    for c in range(2):
                        V.bn_stats(stats[:, t, c, :], x[:, t, c * 512:(c + 1) * 512])
                dve.drain()
                for t in range(NT):
                    V.bn_aggr(mv[:, t, :], stats[:, t, :, :])
                dve.drain()
                V.tensor_scalar(small[:, 0:NT], mv[:, :, 1:2].rearrange("p t a -> p (t a)"), EPS, None, ALU.add)
                inverse_root(NT)
                for t in range(NT):
                    V.tensor_scalar(x[:, t, :], x[:, t, :], mv[:, t, 0:1], small[:, t:t + 1], ALU.subtract, ALU.mult)
                dve.drain()
                for t in range(NT):
                    V.tensor_tensor(x[:, t, :], x[:, t, :], lnrows[:, gain, :], ALU.mult)
                dve.drain()
                for t in range(NT):
                    V.tensor_tensor(x[:, t, :], x[:, t, :], lnrows[:, shift, :], ALU.add)
                dve.drain()

            def top16(values, indices, source, spare, n, count):
                src, alt = r3(source, n), r3(spare, n)
                for u in range(count):
                    V.max(values[:, u, 0:8], src[:, u, :])
                dve.drain()
                for u in range(count):
                    V.max_index(indices[:, u, 0:8], values[:, u, 0:8], src[:, u, :])
                for u in range(count):
                    V.match_replace(alt[:, u, :], values[:, u, 0:8], src[:, u, :], -3.0e38)
                dve.drain()
                for u in range(count):
                    V.max(values[:, u, 8:16], alt[:, u, :])
                dve.drain()
                for u in range(count):
                    V.max_index(indices[:, u, 8:16], values[:, u, 8:16], alt[:, u, :])
                dve.drain()

            with dve.Fori(0, DEPTH) as l:
                with dve.Fori(0, B_GATE // 2) as i:
                    for s in range(2):
                        dve.wait_ge(to_dve[s], 1)
                        dve.sem_inc(to_dve[s], -1)
                        V.tensor_copy(modrows[:, bass.ds((2 * i + s) * CB, CB)], banks[0:2, s, :]
                                      ).then_inc(bank_free[s], 1)
                dve.drain().then_inc(modrows_ready, 1)
                dve.wait_ge(to_dve[2], 1)
                dve.sem_inc(to_dve[2], -1)
                V.tensor_tensor(modv[:], r3(banks[:, 2, 0:96], 2),
                                bmod[:, bass.ds(l, 1), :].rearrange("p a m -> p (a m)").unsqueeze(2)
                                .to_broadcast([P, 48, 2]), ALU.add).then_inc(bank_free[2], 1)
                dve.drain()
                for part in (SC1, SC2):
                    V.tensor_scalar(modv[:, part * 8:part * 8 + 8, :], modv[:, part * 8:part * 8 + 8, :],
                                    1.0, None, ALU.add)
                phase_barrier(dve, "dve")
                for k in range(KD):
                    b = k % 4
                    dve.wait_ge(to_dve[b], 1)
                    dve.sem_inc(to_dve[b], -1)
                    V.tensor_scalar(hT[:, k, P:T], banks[:, b, :], modv[:, SC1 * 8 + k, 1:2],
                                    modv[:, SH1 * 8 + k, 1:2], ALU.mult, ALU.add).then_inc(bank_free[b], 1)
                phase_barrier(dve, "dve")
                phase_barrier(dve, "dve")
                with dve.Fori(0, HEADS) as h:
                    for d in range(2):
                        dve.wait_ge(kneg_ready, 1)
                        dve.sem_inc(kneg_ready, -1)
                        V.tensor_scalar(hk[d], hk[d], omlb[:, bass.ds((l * 2 + d) * HEADS + h, 1)], None, ALU.mult)
                    dve.drain()
                    V.tensor_tensor(ksum, hk[0], hk[1], ALU.add).then_inc(ksum_ready, 1)
                    for d in range(2):
                        dve.wait_ge(log_ready, 1)
                        dve.sem_inc(log_ready, -1)
                        V.tensor_tensor_scan(pre[d].rearrange("p t n -> p (t n)"), reset[:],
                                             gl[d].rearrange("p t n -> p (t n)"), 0.0, ALU.mult, ALU.add
                                             ).then_inc(pre_ready, 1)

                    def place(n):
                        b = 2 * (n % 2)
                        dve.wait_ge(to_dve[b], 1)
                        dve.sem_inc(to_dve[b], -1)
                        V.copy_predicated(r3(sc, P), masks[:, n:n + 1, :].to_broadcast([P, NT, P]),
                                          r3(pair(b), P)).then_inc(bank_free[b], 1)

                    for n, (d, s) in enumerate(units):
                        lo, up = (hk[0], hq) if d == 0 else (hq, hk[1])
                        v = [y.rearrange("p (b s) -> p b s", s=2 * s) for y in (X[n % 2], E[n % 2], lo, up)]
                        dve.wait_ge(exp_ready[n % 2], 1)
                        dve.sem_inc(exp_ready[n % 2], -1)
                        V.tensor_tensor(v[0][:, :, 0:s], v[1][:, :, 0:s], v[2][:, :, 0:s], ALU.mult)
                        V.tensor_tensor(v[0][:, :, s:2 * s], v[1][:, :, s:2 * s], v[3][:, :, s:2 * s], ALU.mult
                                        ).then_inc(x_ready[n % 2], 1)
                        if n:
                            place(n - 1)
                        dve.drain().then_inc(e_free[n % 2], 1)
                    for n, (src, dst) in enumerate([(hq, qdec[0]), (hk[0], X[0]), (hq, qdec[1]), (hk[1], X[1])]):
                        dve.wait_ge(exp_ready[n % 2], 1)
                        dve.sem_inc(exp_ready[n % 2], -1)
                        V.tensor_tensor(dst, E[n % 2], src, ALU.mult).then_inc(e_free[n % 2], 1)
                        if n % 2:
                            dve.drain().then_inc(x_ready[n // 2], 1)
                        if n == 0:
                            place(2 * NL - 1)
                    dve.drain()
                    place(2 * NL)
                    dve.drain().then_inc(sc_ready, 1)
                    dve.wait_ge(tot_ready, 2)
                    dve.sem_inc(tot_ready, -2)
                    dve.wait_ge(s0_full, 32)
                    dve.sem_inc(s0_full, -32)
                    dve.wait_ge(hnew_sent, 32)
                    dve.sem_inc(hnew_sent, -32)
                    for d in range(2):
                        dve.wait_ge(to_dve[2 * d], 1)
                        dve.sem_inc(to_dve[2 * d], -1)
                        added = r3(pair(2 * d), P)
                        V.tensor_copy(hnew[:, d, :], added[:, 0, :])
                        for n in ([0, 1, 2], [3, 2, 1])[d]:
                            to = n + 1 - 2 * d
                            V.scalar_tensor_tensor(S[d][:, to, :], S[d][:, n, :], tot[:, d, n + 1:n + 2],
                                                   added[:, n + 1, :], ALU.mult, ALU.add)
                            dve.drain()
                        dve.drain().then_inc(bank_free[2 * d], 1)
                    dve.drain().then_inc(state_ready, 1)
                    dve.drain().then_inc(hnew_ready, 1)
                    dve.wait_ge(osq_ready, 1)
                    dve.sem_inc(osq_ready, -1)
                    V.tensor_reduce(small[:, 0:NT], r3(osq, P), AX.X, ALU.add)
                    dve.drain()
                    V.tensor_scalar(small[:, 0:NT], small[:, 0:NT], 1.0 / P, EPS, ALU.mult, ALU.add)
                    inverse_root(NT)
                    V.tensor_tensor(r3(o1, P), r3(pair(4), P), small[:, 0:NT].unsqueeze(2).to_broadcast([P, NT, P]),
                                    ALU.mult).then_inc(bank_free[4], 1)
                    dve.drain()
                    V.tensor_tensor(r3(o1, P), r3(o1, P), rows_g[:, bass.ds(l, 1), 0:P].to_broadcast([P, NT, P]),
                                    ALU.mult)
                    dve.drain()
                    V.tensor_tensor(r3(o1, P), r3(o1, P), sgate[:, :, bass.ds(h * P, P)], ALU.mult
                                    ).then_inc(o1_ready, 1)
                phase_barrier(dve, "dve")
                for c, heads, gain in ((1024, KV, P + HD), (0, 8, P), (512, 8, P)):
                    n = heads * HD
                    dve.wait_ge(qkv_ready, 1)
                    dve.sem_inc(qkv_ready, -1)
                    v = qkv[:, :, c:c + n].rearrange("p t (h d) -> p t h d", d=HD)
                    a, b = (y[:, 0:NT * n].rearrange("p (t h d) -> p t h d", t=NT, d=HD) for y in (nt1, nt2))
                    V.tensor_tensor(a, v, v, ALU.mult)
                    dve.drain()
                    V.tensor_reduce(small[:, 0:NT * heads], r3(nt1[:, 0:NT * n], HD), AX.X, ALU.add)
                    dve.drain()
                    V.tensor_scalar(small[:, 0:NT * heads], small[:, 0:NT * heads], 1.0 / HD, EPS, ALU.mult, ALU.add)
                    inverse_root(NT * heads)
                    V.tensor_tensor(v, v, r3(small[:, 0:NT * heads], heads).unsqueeze(3)
                                    .to_broadcast([P, NT, heads, HD]), ALU.mult)
                    dve.drain()
                    V.tensor_tensor(v, v, rows_g[:, bass.ds(l, 1), gain:gain + HD].unsqueeze(2)
                                    .to_broadcast([P, NT, heads, HD]), ALU.mult)
                    dve.drain()
                    lat = v[:, 1:NT]
                    cs, sn = (y[:].unsqueeze(2).to_broadcast([P, NT - 1, heads, 32]) for y in (cos, sin))
                    V.tensor_tensor(a[:, 1:NT, :, 0:32], lat[:, :, :, 0:32], cs, ALU.mult)
                    V.tensor_tensor(a[:, 1:NT, :, 32:64], lat[:, :, :, 0:32], sn, ALU.mult)
                    V.tensor_tensor(b[:, 1:NT, :, 0:32], lat[:, :, :, 32:64], sn, ALU.mult)
                    V.tensor_tensor(b[:, 1:NT, :, 32:64], lat[:, :, :, 32:64], cs, ALU.mult)
                    dve.drain()
                    V.tensor_tensor(lat[:, :, :, 0:32], a[:, 1:NT, :, 0:32], b[:, 1:NT, :, 0:32], ALU.subtract)
                    V.tensor_tensor(lat[:, :, :, 32:64], a[:, 1:NT, :, 32:64], b[:, 1:NT, :, 32:64], ALU.add)
                    dve.drain()
                    if c == 1024:
                        dve.drain().then_inc(kn_pe, 1)
                        dve.drain().then_inc(kn_act, 1)
                dve.drain().then_inc(qkn_pool, 1)

                def lowest(b, u):
                    c = 2 * (u % 2)
                    dve.wait_ge(to_dve[c], 1)
                    dve.sem_inc(to_dve[c], -1)
                    V.tensor_reduce(low[b][:, u:u + 1], pair(c, P if u % NT == 0 else T), AX.X, ALU.min
                                    ).then_inc(low_ready[u % 2], 1)

                def normalise(b):
                    dve.wait_ge(to_dve[6], 1)
                    dve.sem_inc(to_dve[6], -1)
                    V.reciprocal(psum[b], psum[b])
                    dve.drain()
                    V.tensor_tensor(onorm.rearrange("p (t h d) -> p t h d", t=NT, d=HD),
                                    pair(6).rearrange("p (t h d) -> p t h d", t=NT, d=HD),
                                    psum[b].rearrange("p (h t) -> p t h", h=2).unsqueeze(3)
                                    .to_broadcast([P, NT, 2, HD]), ALU.mult).then_inc(onorm_ready, 1)

                def att_pair(b, before, more):
                    for u in range(2 * NT):
                        if u % 2:
                            dve.wait_ge(to_dve[4], 1)
                            dve.sem_inc(to_dve[4], -1)
                            n = 1 if u % NT == 0 else NT
                            V.tensor_copy(PT[1][:, 0:n, :], r3(pair(4, n * P), P)).then_inc(bank_free[4], 1)
                            dve.drain().then_inc(pt_ready[1], 1)
                        if u + 2 < 2 * NT:
                            lowest(b, u + 2)
                        elif more:
                            lowest(1 - b, u + 2 - 2 * NT)
                        if u == 0 and before:
                            normalise(1 - b)

                for u in range(2):
                    lowest(0, u)
                att_pair(0, False, True)
                with dve.Fori(0, QH // 4 - 1):
                    att_pair(1, True, True)
                    att_pair(0, True, True)
                att_pair(1, True, False)
                normalise(1)
                phase_barrier(dve, "dve")
                with dve.Fori(0, KD) as n:
                    for f in range(2):
                        dve.wait_ge(sg_ready[f], 1)
                        dve.sem_inc(sg_ready[f], -1)
                        dve.wait_ge(to_dve[4 * f + 2], 1)
                        dve.sem_inc(to_dve[4 * f + 2], -1)
                        V.tensor_tensor(y1, banks[:, 4 * f + 2, 0:HALF], sgA[f], ALU.mult
                                        ).then_inc(bank_free[4 * f + 2], 1)
                        dve.wait_ge(to_dve[4 * f + 3], 1)
                        dve.sem_inc(to_dve[4 * f + 3], -1)
                        V.tensor_tensor(y2, banks[:, 4 * f + 3, 0:HALF], sgB[f], ALU.mult
                                        ).then_inc(bank_free[4 * f + 3], 1)
                        dve.drain().then_inc(sg_free[f], 1)
                        V.tensor_tensor(yT[:, bass.ds(n, 1), f * HALF:(f + 1) * HALF].rearrange("p a n -> p (a n)"),
                                        y1, y2, ALU.add)
                        dve.drain()
                phase_barrier(dve, "dve")
                dve.wait_ge(bc_ready, 1)
                dve.sem_inc(bc_ready, -1)
                for g in range(2 * NT):
                    t, c = g % NT, slice(g // NT * CB, (g // NT + 1) * CB)
                    dve.wait_ge(to_dve[g % 8], 1)
                    dve.sem_inc(to_dve[g % 8], -1)
                    V.tensor_tensor(outtmp, banks[:, g % 8, :], bca[:, min(t, 1), c], ALU.mult
                                    ).then_inc(bank_free[g % 8], 1)
                    dve.drain()
                    V.scalar_tensor_tensor(x[:, t, c], x[:, t, c], ALPHA, outtmp, ALU.mult, ALU.add)
                    dve.drain()
                dve.wait_ge(ln_full, 16)
                dve.sem_inc(ln_full, -16)
                layer_norm(0, 1)
                phase_barrier(dve, "dve")
                for t in range(NT):
                    c = 2 * min(t, 1)
                    V.tensor_tensor(h2[:, t, :], x[:, t, :], bcb[:, c, :], ALU.mult)
                    dve.drain()
                    V.tensor_tensor(h2[:, t, :], h2[:, t, :], bcb[:, c + 1, :], ALU.add).then_inc(h2_ready, 1)
                with dve.Fori(0, 4) as i:
                    for u in range(4):
                        b = 4 + 2 * (u % 2)
                        dve.wait_ge(to_dve[b], 1)
                        dve.sem_inc(to_dve[b], -1)
                        V.tensor_copy(r3(arena[:, 0:10240], 2048)[:, :, bass.ds((i * 4 + u) * NKEYS, NKEYS)],
                                      r3(pair(b), P)).then_inc(bank_free[b], 1)
                phase_barrier(dve, "dve")
                def choose_experts(t):
                    dve.wait_ge(stage_ready, 1)
                    dve.sem_inc(stage_ready, -1)
                    top16(tv, ti.bitcast(U32), stage, work, NKEYS, 2 * PEER_H)
                    V.tensor_copy(tif, ti.bitcast(U32))
                    halves_v = tv.rearrange("p (h a) k -> p h a k", a=2)
                    V.tensor_tensor(stage.rearrange("p (h a b) -> p h a b", h=PEER_H, a=TOPK),
                                    halves_v[:, :, 0, :].unsqueeze(3).to_broadcast([P, PEER_H, TOPK, TOPK]),
                                    halves_v[:, :, 1, :].unsqueeze(2).to_broadcast([P, PEER_H, TOPK, TOPK]), ALU.add)
                    dve.drain()
                    top16(r3(bs, TOPK), r3(bp, TOPK).bitcast(U32), stage, work, TOPK * TOPK, PEER_H)
                    V.tensor_tensor(r3(gate, TOPK), r3(bs, TOPK), r3(bs, TOPK)[:, :, 0:1]
                                    .to_broadcast([P, PEER_H, TOPK]), ALU.subtract)
                    V.tensor_scalar(bq.bitcast(U32), bp.bitcast(U32), 4, None, ALU.logical_shift_right)
                    V.tensor_scalar(bp.bitcast(U32), bp.bitcast(U32), 15, None, ALU.bitwise_and)
                    dve.drain()
                    V.tensor_copy(paf, bq.bitcast(U32))
                    V.tensor_copy(pbf, bp.bitcast(U32))
                    dve.drain()
                    halves_i = tif.rearrange("p (h a) k -> p h a k", a=2)
                    for a, (pos, found) in enumerate([(paf, e1), (pbf, e2)]):
                        V.tensor_tensor(r3(stage, TOPK), pos.unsqueeze(2).to_broadcast([P, SLOTS, TOPK]),
                                        iota[:].unsqueeze(1).to_broadcast([P, SLOTS, TOPK]), ALU.is_equal)
                        dve.drain()
                        one = stage.rearrange("p (h s k) -> p h s k", h=PEER_H, s=TOPK)
                        V.tensor_tensor(one, one, halves_i[:, :, a, :].unsqueeze(2)
                                        .to_broadcast([P, PEER_H, TOPK, TOPK]), ALU.mult)
                        dve.drain()
                        V.tensor_reduce(found, r3(stage, TOPK), AX.X, ALU.add)
                        dve.drain()
                    dve.drain().then_inc(stage_free, 1)
                    V.scalar_tensor_tensor(e1, e1, float(NKEYS), e2, ALU.mult, ALU.add)
                    dve.drain()
                    V.tensor_scalar(arena[:, bass.ds(t * 2048, SLOTS)].bitcast(U32), e1, layer_base[:], None,
                                    ALU.add).then_inc(idx_ready, 1)

                def peer_dve(t, more):
                    ht = h2[:, bass.ds(t, 1), :].rearrange("p a n -> p (a n)")
                    with dve.Fori(0, TURNS) as i:
                        for j in range(ROWS):
                            dve.wait_ge(row_full[j], (((l * NT + t) * 2) * TURNS + i + 1) * 16)
                            V.scalar_tensor_tensor(grow[j], grow[j], 1.0, ht, ALU.mult, ALU.mult,
                                                   accum_out=av[:, bass.ds(i * ROWS + j, 1)]
                                                   ).then_inc(row_free[j], 1)
                    dve.drain().then_inc(dots_ready, 1)
                    dve.wait_ge(acc_free, 1)
                    dve.sem_inc(acc_free, -1)
                    V.memset(acc, 0.0).then_inc(acc_zero, 1)
                    dve.wait_ge(softexp_ready, 1)
                    dve.sem_inc(softexp_ready, -1)
                    V.tensor_reduce(gsum, r3(gate, TOPK), AX.X, ALU.add)
                    dve.drain()
                    V.reciprocal(gsum, gsum)
                    dve.drain()
                    V.tensor_tensor(r3(gate, TOPK), r3(gate, TOPK), gsum.unsqueeze(2)
                                    .to_broadcast([P, PEER_H, TOPK]), ALU.mult)
                    dve.drain()
                    dve.wait_ge(gelu_ready, 1)
                    dve.sem_inc(gelu_ready, -1)
                    V.tensor_tensor(wv, av, gate, ALU.mult).then_inc(wv_ready, 1)
                    dve.drain()
                    if more:
                        choose_experts(t + 1)
                    dve.wait_ge(acc_seen, 1)
                    dve.sem_inc(acc_seen, -1)
                    with dve.Fori(0, TURNS - TURNS_A) as i:
                        for j in sorted(set(ALL_ROWS) - set(PE_ROWS)):
                            dve.wait_ge(row_full[j], (((l * NT + t) * 2 + 1) * TURNS + TURNS_A + i + 1) * 16)
                            V.scalar_tensor_tensor(acc, grow[j], wv[:, bass.ds((i + TURNS_A) * ROWS + j, 1)], acc,
                                                   ALU.mult, ALU.add).then_inc(row_free[j], 1)
                            dve.drain()
                    dve.drain().then_inc(acc_done, 1)

                choose_experts(0)
                with dve.Fori(0, NT - 1) as t:
                    peer_dve(t, True)
                peer_dve(NT - 1, False)
                phase_barrier(dve, "dve")
                for t in range(NT):
                    V.tensor_tensor(h2[:, t, :], h2[:, t, :], bca[:, min(t, 1), :], ALU.mult)
                dve.drain()
                for t in range(NT):
                    V.scalar_tensor_tensor(x[:, t, :], x[:, t, :], ALPHA, h2[:, t, :], ALU.mult, ALU.add)
                V.tensor_scalar(layer_base[:], layer_base[:], float(N_EXPERTS), None, ALU.add)
                dve.drain()
                layer_norm(2, 3)
                phase_barrier(dve, "dve")
            dve.wait_ge(hnew_sent, 32)
            dve.drain().then_inc(done, 1)


def level_masks():
    j, i = np.meshgrid(np.arange(P), np.arange(P), indexing="ij")
    out = np.zeros((P, 2 * NL + 1, P), np.float32)
    for n, s in enumerate(LEVELS):
        same = (i // (2 * s)) == (j // (2 * s))
        out[:, 2 * n] = same & (i // s % 2 == 1) & (j // s % 2 == 0)
        out[:, 2 * n + 1] = same & (i // s % 2 == 0) & (j // s % 2 == 1)
    out[:, 2 * NL] = i == j
    return out.reshape(P, (2 * NL + 1) * P)


def rotary_tables():
    t = np.arange(LAT, dtype=np.float32)
    inv = (np.float32(10000.0) ** (-np.arange(HD // 4, dtype=np.float32) / np.float32(HD // 4))).astype(np.float32)
    ang = np.concatenate([np.floor(t / GRID_W)[:, None] * inv, (t % GRID_W)[:, None] * inv], axis=1).astype(np.float32)
    return [np.ascontiguousarray(f(ang).astype(np.float32).reshape(NT - 1, P, 32).transpose(1, 0, 2))
            for f in (np.cos, np.sin)]


def layout(inputs):
    a = {k: np.asarray(v) for k, v in inputs.items()}
    w_in = a["w_in"]
    off = np.cumsum([0, 1024, 1024, 1024, 1024, 1024, 1024, 256, 256, 1024, 1024])
    hq, hff, hfb, hi, hg, aq, ak, av, ga, gb = (w_in[:, :, off[n]:off[n + 1]] for n in range(10))
    order = [h for i in range(4) for kp in range(2) for h in (8 * kp + i, 8 * kp + 4 + i)]
    aq = aq.reshape(DEPTH, D, QH, HD)[:, :, order].reshape(DEPTH, D, D)
    watt = a["w_branch_att"].reshape(DEPTH, QH, HD, D)[:, order].reshape(DEPTH, D, D)
    sk = a["peer_sub_keys"].transpose(0, 4, 1, 2, 3).reshape(DEPTH, P, 2048)

    def block(w):
        return w.reshape(KD, P, CB).transpose(1, 0, 2).reshape(P, KD * CB)

    wblk = np.zeros((DEPTH * NB, P, KD * CB), np.float32)
    for l in range(DEPTH):
        blocks = [a["w_mod"][l][:, j * CB:(j + 1) * CB] for j in range(12)]
        blocks += [hg[l][:, j * CB:(j + 1) * CB] for j in range(2)]
        blocks += [np.concatenate([w[l][:, h * P:(h + 1) * P] for w in (hq, hff, hfb, hi)], 1) for h in range(HEADS)]
        blocks += [np.concatenate([ak[l], av[l]], 1), aq[l][:, 0:CB], aq[l][:, CB:]]
        blocks += [np.concatenate([w[l][:, n * P:(n + 1) * P] for w in (ga, gb, a["w_branch_rec"], watt)], 1)
                   for n in range(KD)]
        blocks += [a["w_out"][l][:, j * CB:(j + 1) * CB] for j in range(2)]
        blocks += [None] + [a["peer_w_query"][l][:, j * CB:(j + 1) * CB] for j in range(4)]
        for n, w in enumerate(blocks):
            if w is None:
                wblk[l * NB + n, :, 0:2048] = sk[l]
            else:
                wblk[l * NB + n] = block(w)
    cos, sin = rotary_tables()
    reset = np.ones((P, NT, 129), np.float32)
    reset[:, :, 0] = 0.0
    return {
        "x_prompt": a["x_prompt"][0], "x_sample": a["x_sample"][0],
        "cond": np.stack([a["c_ctx"], a["c"][0]]).reshape(2, KD, P).transpose(2, 1, 0),
        "bmod": a["b_mod"].reshape(DEPTH, 48, P).transpose(2, 0, 1),
        "lbz": a["hgrn_lb_logits"].reshape(2, DEPTH, HEADS, P).transpose(3, 0, 1, 2),
        "ident": np.eye(P, dtype=np.float32), "cos": cos, "sin": sin,
        "iota": np.tile(np.arange(TOPK, dtype=np.float32), (P, 1)),
        "masks": level_masks(), "reset": reset.reshape(P, NT * 129),
        "hgrn_norm_g": a["hgrn_norm_g"], "q_norm_g": a["q_norm_g"], "k_norm_g": a["k_norm_g"],
        "state": a["state_hgrn"].reshape(DEPTH * 2 * HEADS, P, P),
        "cache_k": a["cache_attn_k"].reshape(DEPTH, P, KV * HD),
        "cache_v": a["cache_attn_v"].reshape(DEPTH, P, KV * HD),
        "lnrows": np.stack([a[n] for n in ("ln1_g", "ln1_b", "ln2_g", "ln2_b")], axis=1),
        "peer_u": a["peer_u"].reshape(DEPTH * N_EXPERTS, D), "peer_v": a["peer_v"].reshape(DEPTH * N_EXPERTS, D),
        "wblk": wblk,
    }


def kernel(**inputs):
    import concourse.bacc as bacc
    from concourse.bass_utils import run_bass_kernel_spmd

    nc = bacc.Bacc("TRN2", target_bir_lowering=False, num_devices=1)
    arrays, ins = {}, {}
    for name, a in layout(inputs).items():
        a = np.ascontiguousarray(a)
        arrays[f"in_{name}"] = a
        ins[name] = nc.dram_tensor(f"in_{name}", a.shape, mybir.dt.from_np(a.dtype), kind="ExternalInput").ap()
    shapes = [(1, P, D), (1, LAT, D), (DEPTH, P, KV * HD), (DEPTH, P, KV * HD), (DEPTH * 2 * HEADS, P, P)]
    outs = [nc.dram_tensor(f"out_{i}", s, F32, kind="ExternalOutput").ap() for i, s in enumerate(shapes)]
    build(nc, ins, outs)
    r = run_bass_kernel_spmd(nc, [arrays], core_ids=[0])
    got = [r.results[0][f"out_{i}"] for i in range(len(shapes))]
    return (got[0], got[1], got[2].reshape(1, DEPTH, P, KV, HD), got[3].reshape(1, DEPTH, P, KV, HD),
            got[4].reshape(1, DEPTH, 2, HEADS, P, P))
```

```python
from contextlib import ExitStack

import numpy as np

import concourse.bass as bass
from concourse import mybir

F32 = mybir.dt.float32
U32 = mybir.dt.uint32
U8 = mybir.dt.uint8
ALU = mybir.AluOpType
ACT = mybir.ActivationFunctionType
AX = mybir.AxisListType

P = 128
DEPTH = 2
D = 1024
KD = D // P
NT = 5
T = NT * P
LAT = T - P
HALF = T // 2
HEADS = 8
KV = 4
HD = 64
QH = 16
GROUP = QH // KV
GRID_W = 64
PEER_H = 8
TOPK = 16
SLOTS = PEER_H * TOPK
NKEYS = 128
N_EXPERTS = NKEYS * NKEYS
CB = 512
ALPHA = float((2 * DEPTH) ** 0.25)
EPS = 1e-6
SCALE = HD ** -0.5
LOG_FLOOR = 2.0 ** -62
LEVELS = [64, 32, 16, 8, 4, 2, 1]
NL = len(LEVELS)
ROWS = 8
TURNS = SLOTS // ROWS
TURNS_B = 9
TURNS_A = 4
ALL_ROWS = tuple(range(ROWS))
PE_ROWS = (0, 2, 4, 6)
DIAGS = 4
STAGED = 2
B_MOD, B_GATE, B_HEAD, B_KV, B_Q, B_MIX, B_OUT, B_SK, B_PQ = 0, 12, 14, 22, 23, 25, 33, 35, 36
NB = 40
SH1, SC1, G1, SH2, SC2, G2 = range(6)


def build(nc, ins, outs):
    with ExitStack() as ctx:
        def sb(name, shape, dt=F32):
            return ctx.enter_context(nc.sbuf_tensor(name, shape, dt))

        def sem(name):
            return ctx.enter_context(nc.semaphore(name))

        x = sb("x", [P, NT, D])
        ring = sb("ring", [P, 2, KD, CB])
        ident = sb("ident", [P, P])
        cos = sb("cos", [P, NT - 1, 32])
        sin = sb("sin", [P, NT - 1, 32])
        reset = sb("reset", [P, NT * 129])
        iota = sb("iota", [P, TOPK])
        masks = sb("masks", [P, 2 * NL + 1, P], U8)
        bmod = sb("bmod", [P, DEPTH, 48])
        modv = sb("modv", [P, 48, 2])
        cond = sb("cond", [P, KD, 2])
        rows_g = sb("rows_g", [P, DEPTH, P + 2 * HD])
        lbz = sb("lbz", [P, 2, DEPTH, HEADS])
        lbf = sb("lbf", [P, DEPTH * 2 * HEADS])
        omlb = sb("omlb", [P, DEPTH * 2 * HEADS])
        small = sb("small", [P, 256])
        layer_base = sb("layer_base", [P, 1])
        hT = sb("hT", [P, KD, T])
        late = sb("late", [P, 8192])
        arena = sb("arena", [P, 23552])
        banks = ctx.enter_context(nc.psum_tensor("banks", [P, 8, 512], F32))

        def pair(b, n=T):
            return banks[:, b:b + 2, :].rearrange("p a n -> p (a n)")[:, 0:n]

        def halves(b):
            return banks[:, b:b + 2, 0:HALF]

        class Region:
            def __init__(self, base, at=0):
                self.base, self.at = base, at

            def take(self, n):
                self.at += n
                assert self.at <= self.base.shape[1], (self.at, self.base.shape)
                return self.base[:, self.at - n:self.at]

        def r3(ap, b):
            return ap.rearrange("p (a b) -> p a b", b=b)

        modrows = arena[0:2, 0:6 * D]
        sgate = r3(arena[:, 0:5120], D)
        orecT = r3(arena[:, 5120:10240], T)
        reg = Region(arena, 10240)
        ksum, sc = reg.take(T), reg.take(T)
        reg2 = Region(late)
        hq, hv = ([r.take(T) for r in (reg, reg2)] for _ in range(2))
        hk = [[r.take(T), r.take(T)] for r in (reg, reg2)]
        sig = reg.take(T)
        gl = [r3(reg.take(NT * 129), 129) for _ in range(2)]
        pre = [r3(reg.take(NT * 129), 129) for _ in range(2)]
        E = [reg.take(T) for _ in range(2)]
        X = [reg.take(T) for _ in range(2)]
        qdec = [reg.take(T) for _ in range(2)]
        kdT = [reg2.take(T) for _ in range(2)]
        S = [r3(reg2.take(4 * P), P) for _ in range(2)]
        o1 = reg2.take(T)
        osq = reg2.take(T)
        tot = r3(reg2.take(2 * NT), NT)
        hnew = r3(late[:, 7936:8192], P)
        oattT = r3(arena[:, 0:5120], T)
        reg = Region(arena, 10240)
        qkv = r3(reg.take(NT * 1536), 1536)
        KT = r3(reg.take(2 * 768), 768)
        kpast = reg.take(256)
        vpast = reg.take(256)
        qTs = [reg.take(T) for _ in range(2)]
        pr = [reg.take(T) for _ in range(2)]
        reg2 = Region(late)
        PT = [r3(reg2.take(T), P) for _ in range(2)]
        onorm = reg2.take(T)
        qstage = [r3(reg2.take(T), P) for _ in range(2)]
        nt1 = reg2.take(NT * CB)
        nt2 = arena[:, 0:NT * CB]
        low = [small[:, 128 + 10 * b:138 + 10 * b] for b in range(2)]
        psum = [small[:, 148 + 10 * b:158 + 10 * b] for b in range(2)]
        yT = r3(arena[:, 10240:15360], T)
        reg = Region(arena, 15360)
        sgA = [reg.take(HALF) for _ in range(2)]
        sgB = [reg.take(HALF) for _ in range(2)]
        y1 = reg.take(HALF)
        y2 = reg.take(HALF)
        lnrows = r3(late[:, 0:4096], D)
        bca = r3(late[:, 4096:6144], D)
        skT = r3(late[:, 6144:8192], P)
        bcb = r3(arena[:, 0:4096], D)
        outtmp = arena[:, 15360:15872]
        h2 = r3(arena[:, 15360:20480], D)
        scores = arena[:, 0:10240].rearrange("p (t u n) -> p t u n", t=NT, n=NKEYS)
        qT = r3(arena[:, 10240:10240 + 4 * T], T)
        stage = arena[:, 10240:12288]
        work = arena[:, 12288:14336]
        reg = Region(late, 6144)
        tv = r3(reg.take(256), TOPK)
        ti = r3(reg.take(256), TOPK)
        tif = r3(reg.take(256), TOPK)
        bs, bp, bq, paf, pbf, e1, e2, av, gate = (reg.take(SLOTS) for _ in range(9))
        wv = reg.take(SLOTS)
        gsum, idxs = small[:, 232:240], small[:, 240:248]
        diag = [arena[:, 256 + j * P:256 + (j + 1) * P] for j in range(DIAGS)]
        hTf = hT[:, :, :].rearrange("p k t -> p (k t)")
        grow = [hTf[:, j * D:(j + 1) * D] for j in range(5)] + \
               [arena[:, 20480 + j * D:20480 + (j + 1) * D] for j in range(3)]
        acc = arena[:, 14336:15360]

        init = sem("init")
        cond_ready = sem("cond_ready")
        lb_shifted, lb_exped, lb_ready = sem("lb_shifted"), sem("lb_exped"), sem("lb_ready")
        w_full = [sem(f"w_full{s}") for s in range(2)]
        w_free = [sem(f"w_free{s}") for s in range(2)]
        bank_free = [sem(f"bank_free{b}") for b in range(8)]
        to_act = [sem(f"to_act{b}") for b in range(8)]
        to_dve = [sem(f"to_dve{b}") for b in range(8)]
        left = {e: sem(f"left_{e}") for e in ("pe", "act", "dve")}
        enter = {e: sem(f"enter_{e}") for e in ("pe", "act", "dve")}
        modrows_ready = sem("modrows_ready")
        heads_set = sem("heads_set")
        s0_full = sem("s0_full")
        kneg_ready, log_ready, pre_ready = sem("kneg_ready"), sem("log_ready"), sem("pre_ready")
        v_ready, ksum_ready, tot_ready = sem("v_ready"), sem("ksum_ready"), sem("tot_ready")
        dif_ready = [sem(f"dif_ready{b}") for b in range(2)]
        exp_ready = [sem(f"exp_ready{b}") for b in range(2)]
        e_free = [sem(f"e_free{b}") for b in range(2)]
        x_ready = [sem(f"x_ready{b}") for b in range(2)]
        kdt_ready, sc_ready, state_ready = sem("kdt_ready"), sem("sc_ready"), sem("state_ready")
        hnew_ready, hnew_sent = sem("hnew_ready"), sem("hnew_sent")
        osq_ready, ms_ready, rms_ready = sem("osq_ready"), sem("ms_ready"), sem("rms_ready")
        o1_ready = sem("o1_ready")
        qkv_ready, past_full = sem("qkv_ready"), sem("past_full")
        qkn_pool, kn_pe, kn_act = sem("qkn_pool"), sem("kn_pe"), sem("kn_act")
        kvnew_sent, kt_ready = sem("kvnew_sent"), sem("kt_ready")
        qst_ready = [sem(f"qst_ready{b}") for b in range(2)]
        qst_free = [sem(f"qst_free{b}") for b in range(2)]
        low_ready = [sem(f"low_ready{b}") for b in range(2)]
        prob_ready = [sem(f"prob_ready{b}") for b in range(2)]
        pt_ready = [sem(f"pt_ready{b}") for b in range(2)]
        onorm_ready = sem("onorm_ready")
        sg_ready = [sem(f"sg_ready{b}") for b in range(2)]
        sg_free = [sem(f"sg_free{b}") for b in range(2)]
        bc_ready, ln_full = sem("bc_ready"), sem("ln_full")
        var_ready, std_ready = sem("var_ready"), sem("std_ready")
        h2_ready, h2T_ready = sem("h2_ready"), sem("h2T_ready")
        sk_arrived, sk_ready, qt_ready = sem("sk_arrived"), sem("sk_ready"), sem("qt_ready")
        stage_ready, stage_free = sem("stage_ready"), sem("stage_free")
        softexp_ready = sem("softexp_ready")
        idx_ready, idx_staged = sem("idx_ready"), sem("idx_staged")
        row_full = [sem(f"row_full{j}") for j in range(ROWS)]
        row_free = [sem(f"row_free{j}") for j in range(ROWS)]
        dots_ready, gelu_ready, wv_ready = sem("dots_ready"), sem("gelu_ready"), sem("wv_ready")
        acc_zero, acc_seen, acc_done = sem("acc_zero"), sem("acc_seen"), sem("acc_done")
        acc_free = sem("acc_free")
        tile_summed = sem("tile_summed")
        diag_ready, diag_used = sem("diag_ready"), sem("diag_used")
        done, stored = sem("done"), sem("stored")

        def phase_barrier(eng, me):
            if me == "pool":
                for other in left:
                    eng.wait_ge(left[other], 1)
                    eng.sem_inc(left[other], -1)
                for other in left:
                    eng.drain().then_inc(enter[other], 1)
            else:
                eng.drain().then_inc(left[me], 1)
                eng.wait_ge(enter[me], 1)
                eng.sem_inc(enter[me], -1)

        INIT = 16 * 14
        units = [(d, s) for s in LEVELS for d in range(2)]

        block = ctx.enter_context(nc.Block())

        @block.sync
        def _(sp):
            with sp.Fori(0, DEPTH * NB // 2) as i:
                for s in range(2):
                    sp.wait_ge(w_free[s], 1)
                    sp.sem_inc(w_free[s], -1)
                    sp.dma_start(ring[:, s].rearrange("p k n -> p (k n)"),
                                 ins["wblk"][bass.ds(2 * i + s, 1)].rearrange("a p n -> p (a n)")
                                 ).then_inc(w_full[s], 16)
            sp.wait_ge(done, 1)
            sp.dma_start(outs[0][0], x[:, 0, :]).then_inc(stored, 16)
            sp.dma_start(outs[1][0].rearrange("(t p) d -> p t d", p=P), x[:, 1:NT, :]
                         ).then_inc(stored, 16)
            sp.wait_ge(stored, 32)

        @block.gpsimd
        def _(pool):
            for s in w_free + e_free + qst_free + sg_free + row_free + bank_free \
                    + [acc_free]:
                pool.sem_inc(s, 1)
            pool.sem_inc(hnew_sent, 32)
            pool.sem_inc(diag_used, DIAGS - 1)
            nc.gpsimd.memset(layer_base[:], 0.0)
            pool.wait_ge(init, INIT)
            with pool.Fori(0, DEPTH) as l:
                phase_barrier(pool, "pool")
                phase_barrier(pool, "pool")
                phase_barrier(pool, "pool")
                for d in range(2):
                    nc.gpsimd.memset(gl[d][:, :, 0:1], 0.0)
                pool.drain().then_inc(heads_set, 1)
                with pool.Fori(0, HEADS) as h:
                    pool.wait_ge(pre_ready, 2)
                    pool.sem_inc(pre_ready, -2)
                    for n, (d, s) in enumerate(units):
                        base = pre[d][:, :, 1 - d:129 - d]
                        base = base.rearrange("p t (b s) -> p t b s", s=2 * s)
                        ref = pre[d][:, :, 0:128].rearrange("p t (b s) -> p t b s", s=2 * s)[:, :, :, s:s + 1]
                        pool.wait_ge(e_free[n % 2], 1)
                        pool.sem_inc(e_free[n % 2], -1)
                        nc.gpsimd.tensor_tensor(
                            E[n % 2].rearrange("p (t b s) -> p t b s", t=NT, s=2 * s), base,
                            ref.to_broadcast([P, NT, P // (2 * s), 2 * s]), ALU.subtract
                        ).then_inc(dif_ready[n % 2], 1)
                    for n, (d, to_end) in enumerate([(0, 0), (0, 1), (1, 1), (1, 0)]):
                        base = pre[d][:, :, 1 - d:129 - d]
                        ref = pre[d][:, :, 128 * to_end:128 * to_end + 1].to_broadcast([P, NT, P])
                        pool.wait_ge(e_free[n % 2], 1)
                        pool.sem_inc(e_free[n % 2], -1)
                        nc.gpsimd.tensor_tensor(r3(E[n % 2], P), base, ref, ALU.subtract
                                                ).then_inc(dif_ready[n % 2], 1)
                phase_barrier(pool, "pool")
                pool.wait_ge(qkn_pool, 1)
                pool.sem_inc(qkn_pool, -1)
                with pool.Fori(0, QH // 4) as i:
                    for b in range(2):
                        pool.wait_ge(qst_free[b], 1)
                        pool.sem_inc(qst_free[b], -1)
                        nc.gpsimd.tensor_copy(qstage[b], qkv[:, :, bass.ds((2 * i + b) * P, P)]
                                              ).then_inc(qst_ready[b], 1)
                phase_barrier(pool, "pool")
                phase_barrier(pool, "pool")
                phase_barrier(pool, "pool")
                pool.wait_ge(sk_arrived, 1)
                pool.sem_inc(sk_arrived, -1)
                nc.gpsimd.tensor_copy(skT, ring[:, B_SK % 2].rearrange("p k (a n) -> p (k a) n", n=NKEYS)[:, 0:16])
                pool.drain().then_inc(sk_ready, 1)
                pool.drain().then_inc(w_free[B_SK % 2], 1)
                phase_barrier(pool, "pool")
                with pool.Fori(0, NT) as t:
                    pool.wait_ge(idx_ready, 1)
                    pool.sem_inc(idx_ready, -1)
                    for table in ("peer_u", "peer_v"):
                        with pool.Fori(0, SLOTS // ROWS) as i:
                            for r in range(0, ROWS, STAGED):
                                for j in range(r, r + STAGED):
                                    pool.wait_ge(row_free[j], 1)
                                    pool.sem_inc(row_free[j], -1)
                                nc.gpsimd.tensor_copy(
                                    idxs[:, r:r + STAGED].bitcast(U32),
                                    arena[:, bass.ds(t * 2048 + i * ROWS + r, STAGED)].bitcast(U32)
                                ).then_inc(idx_staged, 1)
                                pool.wait_ge(idx_staged, 1)
                                pool.sem_inc(idx_staged, -1)
                                for j in range(r, r + STAGED):
                                    nc.gpsimd.indirect_dma_start(
                                        grow[j], None, ins[table],
                                        bass.IndirectOffsetOnAxis(ap=idxs[:, j:j + 1].bitcast(U32), axis=0)
                                    ).then_inc(row_full[j], 16)
                phase_barrier(pool, "pool")

        @block.scalar
        def _(act):
            loads = [(x[:, 0, :], ins["x_prompt"]),
                     (x[:, 1:NT, :], ins["x_sample"].rearrange("(t p) d -> p t d", p=P)),
                     (cond[:], ins["cond"]), (bmod[:], ins["bmod"]), (lbz[:], ins["lbz"]),
                     (ident[:], ins["ident"]), (cos[:], ins["cos"]), (sin[:], ins["sin"]),
                     (iota[:], ins["iota"]), (arena[:, 0:(2 * NL + 1) * P], ins["masks"]), (reset[:], ins["reset"])]
            for dst, src in loads:
                act.dma_start(dst, src).then_inc(init, 16)
            for n, (a, b) in enumerate([(0, P), (P, P + HD), (P + HD, P + 2 * HD)]):
                act.dma_start(rows_g[:, :, a:b], ins[("hgrn_norm_g", "q_norm_g", "k_norm_g")[n]]
                              .partition_broadcast(P)).then_inc(init, 16)
            act.wait_ge(init, INIT)
            nc.scalar.activation(cond[:], cond[:], ACT.Silu).then_inc(cond_ready, 1)
            act.wait_ge(lb_shifted, 1)
            nc.scalar.activation(lbz[:], lbz[:], ACT.Exp).then_inc(lb_exped, 1)
            act.wait_ge(lb_ready, 1)

            def square_root(n):
                act.wait_ge(var_ready, 1)
                act.sem_inc(var_ready, -1)
                nc.scalar.activation(small[:, 0:n], small[:, 0:n], ACT.Sqrt).then_inc(std_ready, 1)

            with act.Fori(0, DEPTH) as l:
                phase_barrier(act, "act")
                for k in range(KD):
                    b = 4 + k % 4
                    act.wait_ge(to_act[b], 1)
                    act.sem_inc(to_act[b], -1)
                    nc.scalar.activation(hT[:, k, 0:P], banks[:, b, 0:P], ACT.Identity,
                                         bias=modv[:, SH1 * 8 + k, 0:1], scale=modv[:, SC1 * 8 + k, 0:1]
                                         ).then_inc(bank_free[b], 1)
                phase_barrier(act, "act")
                for g in range(2 * NT):
                    b = g % 8
                    act.wait_ge(to_act[b], 1)
                    act.sem_inc(to_act[b], -1)
                    nc.scalar.activation(sgate[:, g % NT, g // NT * CB:(g // NT + 1) * CB], banks[:, b, :],
                                         ACT.Silu).then_inc(bank_free[b], 1)
                phase_barrier(act, "act")
                act.wait_ge(heads_set, 1)
                act.sem_inc(heads_set, -1)

                def load_states(h):
                    for d in range(2):
                        act.dma_start(S[d][:, 3 * d, :], ins["state"][bass.ds((l * 2 + d) * HEADS + h, 1)]
                                      .rearrange("a p n -> p (a n)")).then_inc(s0_full, 16)

                def queries_in(b):
                    act.wait_ge(to_act[4], 1)
                    act.sem_inc(to_act[4], -1)
                    nc.scalar.activation(hq[b].rearrange("p (a n) -> p a n", a=2), halves(4), ACT.Silu).then_inc(bank_free[4], 1)

                def keys_in(b, h, d):
                    bank = 6 - 2 * d
                    act.wait_ge(to_act[bank], 1)
                    act.sem_inc(to_act[bank], -1)
                    nc.scalar.activation(hk[b][d].rearrange("p (a n) -> p a n", a=2), halves(bank), ACT.Sigmoid,
                                         scale=-1.0).then_inc(kneg_ready, 1)
                    nc.scalar.activation(sig.rearrange("p (a n) -> p a n", a=2), halves(bank), ACT.Sigmoid
                                         ).then_inc(bank_free[bank], 1)
                    act.drain()
                    c = bass.ds((l * 2 + d) * HEADS + h, 1)
                    nc.scalar.activation(gl[d][:, :, 1:129], r3(sig, P), ACT.Ln,
                                         bias=lbf[:, c], scale=omlb[:, c]).then_inc(log_ready, 1)
                    act.drain()

                def values_in(b):
                    act.wait_ge(to_act[6], 1)
                    act.sem_inc(to_act[6], -1)
                    nc.scalar.copy(hv[b], pair(6)).then_inc(bank_free[6], 1)
                    act.drain().then_inc(v_ready, 1)

                def output_in(h):
                    act.wait_ge(to_act[6], 1)
                    act.sem_inc(to_act[6], -1)
                    nc.scalar.copy(orecT[:, bass.ds(h, 1), :].rearrange("p a n -> p (a n)"), pair(6)
                                   ).then_inc(bank_free[6], 1)

                def head(b, h, first, more):
                    for n, (d, s) in enumerate(units):
                        act.wait_ge(dif_ready[n % 2], 1)
                        act.sem_inc(dif_ready[n % 2], -1)
                        e = E[n % 2].rearrange("p (b s) -> p b s", s=2 * s)
                        nc.scalar.activation(e[:, :, 0:s], e[:, :, 0:s], ACT.Exp, scale=-1.0)
                        nc.scalar.activation(e[:, :, s:2 * s], e[:, :, s:2 * s], ACT.Exp
                                             ).then_inc(exp_ready[n % 2], 1)
                        if n == 3 and not first:
                            output_in(h - 1)
                        if n == 6 and more:
                            queries_in(1 - b)
                        if n == 11 and more:
                            keys_in(1 - b, h + 1, 0)
                    for n, sign in enumerate([1.0, -1.0, -1.0, 1.0]):
                        act.wait_ge(dif_ready[n % 2], 1)
                        act.sem_inc(dif_ready[n % 2], -1)
                        nc.scalar.activation(E[n % 2], E[n % 2], ACT.Exp, scale=sign
                                             ).then_inc(exp_ready[n % 2], 1)
                    for d in range(2):
                        nc.scalar.activation(tot[:, d, :], pre[d][:, :, 128:129].rearrange("p t a -> p (t a)"),
                                             ACT.Exp).then_inc(tot_ready, 1)
                    for d in range(2):
                        act.wait_ge(to_act[2 - 2 * d], 1)
                        act.sem_inc(to_act[2 - 2 * d], -1)
                        nc.scalar.copy(kdT[d], pair(2 - 2 * d)).then_inc(bank_free[2 - 2 * d], 1)
                        act.drain().then_inc(kdt_ready, 1)
                    if more:
                        keys_in(1 - b, h + 1, 1)
                    act.wait_ge(hnew_ready, 1)
                    act.sem_inc(hnew_ready, -1)
                    for d in range(2):
                        act.dma_start(outs[4][bass.ds((l * 2 + d) * HEADS + h, 1)].rearrange("a p n -> p (a n)"),
                                      hnew[:, d, :]).then_inc(hnew_sent, 16)
                    act.wait_ge(to_act[2], 1)
                    act.sem_inc(to_act[2], -1)
                    nc.scalar.activation(osq, pair(2), ACT.Square).then_inc(osq_ready, 1)
                    if more:
                        load_states(h + 1)
                        values_in(1 - b)
                    square_root(NT)

                load_states(0)
                queries_in(0)
                keys_in(0, 0, 0)
                keys_in(0, 0, 1)
                values_in(0)
                head(0, 0, True, True)
                with act.Fori(0, HEADS // 2 - 1) as i:
                    head(1, 2 * i + 1, False, True)
                    head(0, 2 * i + 2, False, True)
                head(1, HEADS - 1, False, False)
                output_in(HEADS - 1)
                phase_barrier(act, "act")
                act.dma_start(kpast, ins["cache_k"][bass.ds(l, 1)].rearrange("a p n -> p (a n)")).then_inc(past_full, 16)
                act.dma_start(vpast, ins["cache_v"][bass.ds(l, 1)].rearrange("a p n -> p (a n)")).then_inc(past_full, 16)
                for g in range(3 * NT):
                    b = g % 8
                    c = (1024, 0, 512)[g // NT]
                    act.wait_ge(to_act[b], 1)
                    act.sem_inc(to_act[b], -1)
                    nc.scalar.copy(qkv[:, g % NT, c:c + CB], banks[:, b, :]).then_inc(bank_free[b], 1)
                    if g % NT == NT - 1:
                        act.drain().then_inc(qkv_ready, 1)
                    if g == NT + 1:
                        square_root(NT * KV)
                    if g == 2 * NT + 1:
                        square_root(NT * 8)
                square_root(NT * 8)
                act.wait_ge(kn_act, 1)
                act.sem_inc(kn_act, -1)
                for n in range(2):
                    act.dma_start(outs[2 + n][bass.ds(l, 1)].rearrange("a p n -> p (a n)"),
                                  qkv[:, 0, 1024 + 256 * n:1280 + 256 * n]).then_inc(kvnew_sent, 16)
                for kp in range(2):
                    act.wait_ge(to_act[2 * kp], 1)
                    act.sem_inc(to_act[2 * kp], -1)
                    nc.scalar.copy(KT[:, kp, :], pair(2 * kp, 768)).then_inc(bank_free[2 * kp], 1)
                    act.drain().then_inc(kt_ready, 1)

                def queries(b):
                    act.wait_ge(to_act[4], 1)
                    act.sem_inc(to_act[4], -1)
                    nc.scalar.copy(qTs[b], pair(4)).then_inc(bank_free[4], 1)
                    act.sem_inc(qst_free[b], 1)

                def exponentials(b, u):
                    n = P if u % NT == 0 else T
                    act.wait_ge(low_ready[u % 2], 1)
                    act.sem_inc(low_ready[u % 2], -1)
                    nc.scalar.activation(pr[u % 2][:, 0:n], pair(2 * (u % 2), n), ACT.Exp,
                                         bias=low[b][:, u:u + 1], scale=-1.0, accum_out=psum[b][:, u:u + 1]
                                         ).then_inc(prob_ready[u % 2], 1)

                def deliver(p):
                    act.wait_ge(to_act[4], 1)
                    act.sem_inc(to_act[4], -1)
                    nc.scalar.copy(oattT[:, bass.ds(p, 1), :].rearrange("p a n -> p (a n)"), pair(4)
                                   ).then_inc(bank_free[4], 1)

                def att_pair(b, before, more):
                    for u in range(2 * NT):
                        if u % 2 == 0:
                            act.wait_ge(to_act[4], 1)
                            act.sem_inc(to_act[4], -1)
                            n = 1 if u % NT == 0 else NT
                            nc.scalar.copy(PT[0][:, 0:n, :], r3(pair(4, n * P), P)).then_inc(bank_free[4], 1)
                            act.drain().then_inc(pt_ready[0], 1)
                        if u + 2 < 2 * NT:
                            exponentials(b, u + 2)
                        elif more:
                            exponentials(1 - b, u + 2 - 2 * NT)
                        if u == 1 and before is not None:
                            deliver(before)
                        if u == 5 and more:
                            queries(1 - b)

                queries(0)
                for u in range(2):
                    exponentials(0, u)
                att_pair(0, None, True)
                with act.Fori(0, QH // 4 - 1) as i:
                    att_pair(1, 2 * i, True)
                    att_pair(0, 2 * i + 1, True)
                att_pair(1, QH // 2 - 2, False)
                deliver(QH // 2 - 1)
                act.wait_ge(kvnew_sent, 32)
                act.sem_inc(kvnew_sent, -32)
                phase_barrier(act, "act")
                with act.Fori(0, KD):
                    for f in range(2):
                        act.wait_ge(sg_free[f], 1)
                        act.sem_inc(sg_free[f], -1)
                        act.wait_ge(to_act[4 * f], 1)
                        act.sem_inc(to_act[4 * f], -1)
                        nc.scalar.activation(sgA[f], banks[:, 4 * f, 0:HALF], ACT.Sigmoid
                                             ).then_inc(bank_free[4 * f], 1)
                        act.wait_ge(to_act[4 * f + 1], 1)
                        act.sem_inc(to_act[4 * f + 1], -1)
                        nc.scalar.activation(sgB[f], banks[:, 4 * f + 1, 0:HALF], ACT.Sigmoid
                                             ).then_inc(bank_free[4 * f + 1], 1)
                        act.drain().then_inc(sg_ready[f], 1)
                phase_barrier(act, "act")
                act.dma_start(lnrows, ins["lnrows"][bass.ds(l, 1)].rearrange("a r n -> (a r) n")
                              .partition_broadcast(P)).then_inc(ln_full, 16)
                for v, dst in enumerate([bca[:, 0], bca[:, 1], bcb[:, 0], bcb[:, 1], bcb[:, 2], bcb[:, 3]]):
                    b = 2 * (v % 4)
                    act.wait_ge(to_act[b], 1)
                    act.sem_inc(to_act[b], -1)
                    nc.scalar.copy(dst, pair(b, D)).then_inc(bank_free[b], 1)
                act.drain().then_inc(bc_ready, 1)
                square_root(NT)
                phase_barrier(act, "act")
                for t in range(NT):
                    b = 2 * (t % 4)
                    act.wait_ge(to_act[b], 1)
                    act.sem_inc(to_act[b], -1)
                    nc.scalar.copy(hT[:, :, t * P:(t + 1) * P], r3(pair(b, D), P)).then_inc(bank_free[b], 1)
                    act.drain().then_inc(h2T_ready, 1)
                with act.Fori(0, 4):
                    for u in range(4):
                        b = 2 * (u % 2)
                        act.wait_ge(to_act[b], 1)
                        act.sem_inc(to_act[b], -1)
                        nc.scalar.copy(qT[:, u, :].rearrange("p (a n) -> p a n", a=2), halves(b)
                                       ).then_inc(bank_free[b], 1)
                        act.drain().then_inc(qt_ready, 1)
                phase_barrier(act, "act")
                for c in range(2):
                    act.wait_ge(to_act[2 * c], 1)
                    act.sem_inc(to_act[2 * c], -1)
                    nc.scalar.copy(bca[:, c], pair(2 * c, D)).then_inc(bank_free[2 * c], 1)
                nc.scalar.copy(stage, arena[:, 0:2048]).then_inc(stage_ready, 1)

                def peer_act(t, more, norm):
                    act.wait_ge(dots_ready, 1)
                    act.sem_inc(dots_ready, -1)
                    nc.scalar.activation(gate, gate, ACT.Exp).then_inc(softexp_ready, 1)
                    nc.scalar.activation(av, av, ACT.Gelu).then_inc(gelu_ready, 1)
                    if more:
                        act.wait_ge(stage_free, 1)
                        act.sem_inc(stage_free, -1)
                        nc.scalar.copy(stage, arena[:, bass.ds((t + 1) * 2048, 2048)]).then_inc(stage_ready, 1)
                    act.wait_ge(wv_ready, 1)
                    act.sem_inc(wv_ready, -1)
                    for first, last, mine in ((0, TURNS_A, ALL_ROWS), (TURNS_A, TURNS_B, PE_ROWS),
                                              (TURNS_B, TURNS, PE_ROWS)):
                        if first == TURNS_B and norm:
                            square_root(1)
                        with act.Fori(first, last) as i:
                            for n, j in enumerate(mine):
                                act.wait_ge(diag_used, 1)
                                act.sem_inc(diag_used, -1)
                                nc.scalar.activation(diag[n % DIAGS], ident[:], ACT.Copy,
                                                     scale=wv[:, bass.ds(i * ROWS + j, 1)]
                                                     ).then_inc(diag_ready, 1)
                    act.wait_ge(to_act[4], 1)
                    act.sem_inc(to_act[4], -1)
                    nc.scalar.copy(h2[:, bass.ds(t, 1), :].rearrange("p a n -> p (a n)"), pair(4, D)
                                   ).then_inc(bank_free[4], 1)
                    act.drain().then_inc(tile_summed, 1)

                peer_act(0, True, False)
                with act.Fori(1, NT - 1) as t:
                    peer_act(t, True, True)
                peer_act(NT - 1, False, True)
                square_root(1)
                phase_barrier(act, "act")

        @block.tensor
        def _(pe):
            def project(b, s, c, rhs):
                pe.wait_ge(bank_free[b], 1)
                pe.sem_inc(bank_free[b], -1)
                for f in range(2):
                    for k in range(KD):
                        last = nc.tensor.matmul(banks[:, b + f, 0:HALF], ring[:, s, k, c:c + P],
                                                rhs[:, k, f * HALF:(f + 1) * HALF], start=k == 0, stop=k == KD - 1)
                return last

            def tokenwise(b, s, lhs, t):
                pe.wait_ge(bank_free[b], 1)
                pe.sem_inc(bank_free[b], -1)
                for k in range(KD):
                    last = nc.tensor.matmul(banks[:, b, :], lhs[:, k, t * P:(t + 1) * P], ring[:, s, k, :],
                                            start=k == 0, stop=k == KD - 1)
                return last

            def at(b, t):
                return banks[:, b + t // 4, t % 4 * P:(t % 4 + 1) * P]

            def spread(b, part, c):
                pe.wait_ge(bank_free[b], 1)
                pe.sem_inc(bank_free[b], -1)
                for k in range(KD):
                    last = nc.tensor.matmul(at(b, k), modv[:, part * 8 + k, c:c + 1].to_broadcast([P, P]),
                                            ident[:], start=True, stop=True)
                last.then_inc(to_act[b], 1)

            pe.wait_ge(init, INIT)
            pe.wait_ge(cond_ready, 1)
            with pe.Fori(0, DEPTH) as l:
                with pe.Fori(0, B_GATE // 2):
                    for s in range(2):
                        pe.wait_ge(w_full[s], 16)
                        pe.sem_inc(w_full[s], -16)
                        pe.wait_ge(bank_free[s], 1)
                        pe.sem_inc(bank_free[s], -1)
                        for k in range(KD):
                            last = nc.tensor.matmul(banks[0:2, s, :], cond[:, k, :], ring[:, s, k, :],
                                                    start=k == 0, stop=k == KD - 1)
                        last.then_inc(to_dve[s], 1)
                        pe.drain().then_inc(w_free[s], 1)
                pe.wait_ge(modrows_ready, 1)
                pe.sem_inc(modrows_ready, -1)
                pe.wait_ge(bank_free[2], 1)
                pe.sem_inc(bank_free[2], -1)
                for m in range(48):
                    last = nc.tensor.transpose(banks[:, 2, 2 * m:2 * m + 2], modrows[:, m * P:(m + 1) * P],
                                               ident[0:2, 0:2])
                last.then_inc(to_dve[2], 1)
                phase_barrier(pe, "pe")
                for k in range(KD):
                    b = k % 4
                    pe.wait_ge(bank_free[4 + b], 1)
                    pe.sem_inc(bank_free[4 + b], -1)
                    nc.tensor.transpose(banks[:, 4 + b, 0:P], x[:, 0, k * P:(k + 1) * P], ident[:]
                                        ).then_inc(to_act[4 + b], 1)
                    pe.wait_ge(bank_free[b], 1)
                    pe.sem_inc(bank_free[b], -1)
                    for t in range(1, NT):
                        last = nc.tensor.transpose(banks[:, b, (t - 1) * P:t * P], x[:, t, k * P:(k + 1) * P], ident[:])
                    last.then_inc(to_dve[b], 1)
                phase_barrier(pe, "pe")
                for g in range(2 * NT):
                    s = (B_GATE + g // NT) % 2
                    if g % NT == 0:
                        pe.wait_ge(w_full[s], 16)
                        pe.sem_inc(w_full[s], -16)
                    tokenwise(g % 8, s, hT, g % NT).then_inc(to_act[g % 8], 1)
                    if g % NT == NT - 1:
                        pe.drain().then_inc(w_free[s], 1)
                phase_barrier(pe, "pe")

                def projection(b, n):
                    if n == 0:
                        pe.wait_ge(w_full[b], 16)
                        pe.sem_inc(w_full[b], -16)
                    if n < 24:
                        c, q = divmod(n, 8)
                        f, k0 = divmod(q, 4)
                        bank = (4, 6, 4)[c]
                        if q == 0:
                            pe.wait_ge(bank_free[bank], 1)
                            pe.sem_inc(bank_free[bank], -1)
                        tok = slice(f * HALF, (f + 1) * HALF)
                        for k in range(2 * k0, 2 * k0 + 2):
                            last = nc.tensor.matmul(banks[:, bank + f, 0:HALF], ring[:, b, k, c * P:(c + 1) * P],
                                                    hT[:, k, tok], start=k == 0, stop=k == KD - 1)
                        if q == 7:
                            last.then_inc(to_act[bank], 1)
                    else:
                        t = n - 24
                        if t == 0:
                            pe.wait_ge(bank_free[6], 1)
                            pe.sem_inc(bank_free[6], -1)
                        for k in range(KD):
                            last = nc.tensor.matmul(at(6, t), hT[:, k, t * P:(t + 1) * P], ring[:, b, k, 3 * P:4 * P],
                                                    start=k == 0, stop=k == KD - 1)
                        if t == NT - 1:
                            last.then_inc(to_act[6], 1)
                            pe.drain().then_inc(w_free[b], 1)

                def turn_output():
                    pe.wait_ge(o1_ready, 1)
                    pe.sem_inc(o1_ready, -1)
                    pe.wait_ge(bank_free[6], 1)
                    pe.sem_inc(bank_free[6], -1)
                    for t in range(NT):
                        last = nc.tensor.transpose(at(6, t), o1[:, t * P:(t + 1) * P], ident[:])
                    last.then_inc(to_act[6], 1)

                def head(b, first, more):
                    pe.wait_ge(ksum_ready, 1)
                    pe.sem_inc(ksum_ready, -1)
                    pe.wait_ge(bank_free[0], 1)
                    pe.sem_inc(bank_free[0], -1)
                    for t in range(NT):
                        last = nc.tensor.matmul(at(0, t), ksum[:, t * P:(t + 1) * P], hq[b][:, t * P:(t + 1) * P],
                                                start=True, stop=True)
                    last.then_inc(to_dve[0], 1)
                    if more:
                        for part in range(3):
                            projection(1 - b, part)
                    for n in range(2 * NL):
                        bank = 2 - 2 * (n % 2)
                        pe.wait_ge(x_ready[n % 2], 1)
                        pe.sem_inc(x_ready[n % 2], -1)
                        pe.wait_ge(bank_free[bank], 1)
                        pe.sem_inc(bank_free[bank], -1)
                        for t in range(NT):
                            xt = X[n % 2][:, t * P:(t + 1) * P]
                            last = nc.tensor.matmul(at(bank, t), xt, xt, start=True, stop=True)
                        last.then_inc(to_dve[bank], 1)
                        if n == 1 and not first:
                            turn_output()
                        if more:
                            for part in range(3 + 3 * n // 2, 3 + 3 * (n + 1) // 2):
                                projection(1 - b, part)
                    if more:
                        projection(1 - b, 24)
                    for d in range(2):
                        pe.wait_ge(x_ready[d], 1)
                        pe.sem_inc(x_ready[d], -1)
                        pe.wait_ge(bank_free[2 - 2 * d], 1)
                        pe.sem_inc(bank_free[2 - 2 * d], -1)
                        for t in range(NT):
                            last = nc.tensor.transpose(at(2 - 2 * d, t), X[d][:, t * P:(t + 1) * P], ident[:])
                        last.then_inc(to_act[2 - 2 * d], 1)
                    if more:
                        projection(1 - b, 25)
                    pe.wait_ge(v_ready, 1)
                    pe.sem_inc(v_ready, -1)
                    for d in range(2):
                        pe.wait_ge(kdt_ready, 1)
                        pe.sem_inc(kdt_ready, -1)
                        pe.wait_ge(bank_free[2 - 2 * d], 1)
                        pe.sem_inc(bank_free[2 - 2 * d], -1)
                        for t in range(NT):
                            last = nc.tensor.matmul(at(2 - 2 * d, t), kdT[d][:, t * P:(t + 1) * P],
                                                    hv[b][:, t * P:(t + 1) * P], start=True, stop=True)
                        last.then_inc(to_dve[2 - 2 * d], 1)
                    if more:
                        projection(1 - b, 26)
                        projection(1 - b, 27)
                    pe.wait_ge(sc_ready, 1)
                    pe.sem_inc(sc_ready, -1)
                    pe.wait_ge(state_ready, 1)
                    pe.sem_inc(state_ready, -1)
                    pe.wait_ge(bank_free[2], 1)
                    pe.sem_inc(bank_free[2], -1)
                    for t in range(NT):
                        tt = slice(t * P, (t + 1) * P)
                        last = nc.tensor.matmul(at(2, t), sc[:, tt], hv[b][:, tt], start=True, stop=t == 0)
                        for d in range(2 * (t > 0)):
                            last = nc.tensor.matmul(at(2, t), qdec[d][:, tt], S[d][:, t - 1, :],
                                                    start=False, stop=d == 1)
                    last.then_inc(to_act[2], 1)
                    if more:
                        projection(1 - b, 28)

                for n in range(29):
                    projection(0, n)
                head(0, True, True)
                with pe.Fori(0, HEADS // 2 - 1):
                    head(1, False, True)
                    head(0, False, True)
                head(1, False, False)
                turn_output()
                phase_barrier(pe, "pe")
                for g in range(3 * NT):
                    s = (B_KV + g // NT) % 2
                    if g % NT == 0:
                        pe.wait_ge(w_full[s], 16)
                        pe.sem_inc(w_full[s], -16)
                    tokenwise(g % 8, s, hT, g % NT).then_inc(to_act[g % 8], 1)
                    if g % NT == NT - 1:
                        pe.drain().then_inc(w_free[s], 1)
                pe.wait_ge(past_full, 32)
                pe.sem_inc(past_full, -32)
                pe.wait_ge(kn_pe, 1)
                pe.sem_inc(kn_pe, -1)
                for b in (1, 3):
                    pe.wait_ge(bank_free[b], 1)
                    pe.sem_inc(bank_free[b], -1)
                    pe.sem_inc(bank_free[b], 1)
                for kp in range(2):
                    pe.wait_ge(bank_free[2 * kp], 1)
                    pe.sem_inc(bank_free[2 * kp], -1)
                    for t in range(NT + 1):
                        src = qkv[:, t, 1024 + kp * P:1024 + (kp + 1) * P] if t < NT else kpast[:, kp * P:(kp + 1) * P]
                        last = nc.tensor.transpose(at(2 * kp, t), src, ident[:])
                    last.then_inc(to_act[2 * kp], 1)
                pe.wait_ge(kt_ready, 2)
                pe.sem_inc(kt_ready, -2)

                def queries(b):
                    pe.wait_ge(qst_ready[b], 1)
                    pe.sem_inc(qst_ready[b], -1)
                    pe.wait_ge(bank_free[4], 1)
                    pe.sem_inc(bank_free[4], -1)
                    for t in range(NT):
                        last = nc.tensor.transpose(at(4, t), qstage[b][:, t, :], ident[:])
                    last.then_inc(to_act[4], 1)

                def score(b, u):
                    half, qt = divmod(u, NT)
                    rows = slice(64 * half, 64 * half + 64)
                    c = 2 * (u % 2)
                    lhs = qTs[b][rows, qt * P:(qt + 1) * P]
                    if qt == 0:
                        last = nc.tensor.matmul(banks[:, c, 0:P], lhs, KT[rows, b, 0:P], start=True, stop=True)
                    else:
                        nc.tensor.matmul(banks[:, c, :], lhs, KT[rows, b, P:T], start=True, stop=True)
                        last = nc.tensor.matmul(banks[:, c + 1, 0:P], lhs, KT[rows, b, T:T + P], start=True, stop=True)
                    last.then_inc(to_dve[c], 1)

                def turn(u):
                    pe.wait_ge(prob_ready[u % 2], 1)
                    pe.sem_inc(prob_ready[u % 2], -1)
                    pe.wait_ge(bank_free[4], 1)
                    pe.sem_inc(bank_free[4], -1)
                    for j in range(1 if u % NT == 0 else NT):
                        last = nc.tensor.transpose(at(4, j), pr[u % 2][:, j * P:(j + 1) * P], ident[:])
                    last.then_inc((to_act, to_dve)[u % 2][4], 1)

                def weigh(b, u):
                    half, qt = divmod(u, NT)
                    pe.wait_ge(pt_ready[u % 2], 1)
                    pe.sem_inc(pt_ready[u % 2], -1)
                    out = banks[:, 6 + half, qt * HD:(qt + 2) * HD].rearrange("p (a d) -> p a d", a=2)
                    c = 1280 + (2 * b + half) * HD

                    def twice(v):
                        return v.unsqueeze(1).to_broadcast([P, 2, HD])

                    if qt == 0:
                        last = nc.tensor.matmul(out, PT[u % 2][:, 0, :], twice(qkv[:, 0, c:c + HD]), start=True, stop=True)
                    for j in range(NT if qt else 0):
                        v = qkv[:, j + 1, c:c + HD] if j < NT - 1 else vpast[:, c - 1280:c - 1280 + HD]
                        last = nc.tensor.matmul(out, PT[u % 2][:, j, :], twice(v), start=j == 0, stop=j == NT - 1)
                    if u == 2 * NT - 1:
                        last.then_inc(to_dve[6], 1)

                def output():
                    pe.wait_ge(bank_free[4], 1)
                    pe.sem_inc(bank_free[4], -1)
                    for t in range(NT):
                        last = nc.tensor.transpose(at(4, t), onorm[:, t * P:(t + 1) * P], ident[:])
                    last.then_inc(to_act[4], 1)

                def att_pair(b, before, more):
                    for u in range(2 * NT):
                        turn(u)
                        if u + 2 < 2 * NT:
                            score(b, u + 2)
                        elif more:
                            score(1 - b, u + 2 - 2 * NT)
                        if u == 1 and before:
                            pe.wait_ge(onorm_ready, 1)
                            pe.sem_inc(onorm_ready, -1)
                            output()
                        if u == 5 and more:
                            queries(1 - b)
                        if u:
                            weigh(b, u - 1)
                        elif before:
                            weigh(1 - b, 2 * NT - 1)

                for b in (0, 2, 6):
                    pe.wait_ge(bank_free[b], 1)
                    pe.sem_inc(bank_free[b], -1)
                queries(0)
                pe.wait_ge(bank_free[4], 1)
                pe.sem_inc(bank_free[4], -1)
                pe.sem_inc(bank_free[4], 1)
                for u in range(2):
                    score(0, u)
                att_pair(0, False, True)
                with pe.Fori(0, QH // 4 - 1):
                    att_pair(1, True, True)
                    att_pair(0, True, True)
                att_pair(1, True, False)
                weigh(1, 2 * NT - 1)
                pe.wait_ge(onorm_ready, 1)
                pe.sem_inc(onorm_ready, -1)
                output()
                for b in (0, 2, 6):
                    pe.sem_inc(bank_free[b], 1)
                phase_barrier(pe, "pe")
                with pe.Fori(0, KD // 2):
                    for n in range(2):
                        s = (B_MIX + n) % 2
                        pe.wait_ge(w_full[s], 16)
                        pe.sem_inc(w_full[s], -16)
                        for f in range(2):
                            for c, rhs in enumerate([hT, hT, orecT, oattT]):
                                b = 4 * f + c
                                pe.wait_ge(bank_free[b], 1)
                                pe.sem_inc(bank_free[b], -1)
                                for k in range(KD):
                                    last = nc.tensor.matmul(banks[:, b, 0:HALF], ring[:, s, k, c * P:(c + 1) * P],
                                                            rhs[:, k, f * HALF:(f + 1) * HALF],
                                                            start=k == 0, stop=k == KD - 1)
                                last.then_inc((to_act if c < 2 else to_dve)[b], 1)
                        pe.drain().then_inc(w_free[s], 1)
                phase_barrier(pe, "pe")
                for v, (part, c) in enumerate([(G1, 0), (G1, 1), (SC2, 0), (SH2, 0), (SC2, 1), (SH2, 1)]):
                    spread(2 * (v % 4), part, c)
                for b in range(0, 8, 2):
                    pe.wait_ge(bank_free[b], 1)
                    pe.sem_inc(bank_free[b], -1)
                    pe.sem_inc(bank_free[b], 1)
                for g in range(2 * NT):
                    s = (B_OUT + g // NT) % 2
                    if g % NT == 0:
                        pe.wait_ge(w_full[s], 16)
                        pe.sem_inc(w_full[s], -16)
                    tokenwise(g % 8, s, yT, g % NT).then_inc(to_dve[g % 8], 1)
                    if g % NT == NT - 1:
                        pe.drain().then_inc(w_free[s], 1)
                phase_barrier(pe, "pe")
                pe.wait_ge(w_full[B_SK % 2], 16)
                pe.sem_inc(w_full[B_SK % 2], -16)
                pe.sem_inc(sk_arrived, 1)
                for t in range(NT):
                    b = 2 * (t % 4)
                    pe.wait_ge(h2_ready, 1)
                    pe.sem_inc(h2_ready, -1)
                    pe.wait_ge(bank_free[b], 1)
                    pe.sem_inc(bank_free[b], -1)
                    for k in range(KD):
                        last = nc.tensor.transpose(at(b, k), h2[:, t, k * P:(k + 1) * P], ident[:])
                    last.then_inc(to_act[b], 1)
                pe.wait_ge(h2T_ready, NT)
                pe.sem_inc(h2T_ready, -NT)
                pe.wait_ge(sk_ready, 1)
                pe.sem_inc(sk_ready, -1)
                with pe.Fori(0, 2) as i:
                    for s in range(2):
                        def match(u):
                            b = 4 + 2 * (u % 2)
                            pe.wait_ge(qt_ready, 1)
                            pe.sem_inc(qt_ready, -1)
                            pe.wait_ge(bank_free[b], 1)
                            pe.sem_inc(bank_free[b], -1)
                            for t in range(NT):
                                last = nc.tensor.matmul(
                                    at(b, t), qT[:, u, t * P:(t + 1) * P],
                                    skT[:, bass.ds((2 * i + s) * 4 + u, 1), :].rearrange("p a n -> p (a n)"),
                                    start=True, stop=True)
                            last.then_inc(to_dve[b], 1)

                        pe.wait_ge(w_full[s], 16)
                        pe.sem_inc(w_full[s], -16)
                        for u in range(4):
                            project(2 * (u % 2), s, u * P, hT).then_inc(to_act[2 * (u % 2)], 1)
                            if u:
                                match(u - 1)
                        match(3)
                        pe.drain().then_inc(w_free[s], 1)
                phase_barrier(pe, "pe")
                for c in range(2):
                    spread(2 * c, G2, c)
                with pe.Fori(0, NT) as t:
                    pe.wait_ge(acc_zero, 1)
                    pe.sem_inc(acc_zero, -1)
                    pe.wait_ge(bank_free[4], 1)
                    pe.sem_inc(bank_free[4], -1)
                    for c in range(2):
                        last = nc.tensor.matmul(banks[:, 4 + c, :], ident[:], acc[:, c * CB:(c + 1) * CB],
                                                start=True, stop=False, skip_group_check=True)
                    last.then_inc(acc_seen, 1)
                    for first, count, mine in ((0, TURNS_A, ALL_ROWS), (TURNS_A, TURNS - TURNS_A, PE_ROWS)):
                        with pe.Fori(0, count) as i:
                            for n, j in enumerate(mine):
                                pe.wait_ge(diag_ready, 1)
                                pe.sem_inc(diag_ready, -1)
                                pe.wait_ge(row_full[j], (((l * NT + t) * 2 + 1) * TURNS + first + i + 1) * 16)
                                nc.tensor.matmul(banks[:, 4, :], diag[n % DIAGS], grow[j][:, 0:CB], start=False,
                                                 stop=False, skip_group_check=True
                                                 ).then_inc(diag_used, 1)
                                nc.tensor.matmul(banks[:, 5, :], diag[n % DIAGS], grow[j][:, CB:D], start=False,
                                                 stop=False, skip_group_check=True).then_inc(row_free[j], 1)
                    pe.wait_ge(acc_done, 1)
                    pe.sem_inc(acc_done, -1)
                    for c in range(2):
                        last = nc.tensor.matmul(banks[:, 4 + c, :], ident[:], acc[:, c * CB:(c + 1) * CB],
                                                start=False, stop=True, skip_group_check=True)
                    last.then_inc(to_act[4], 1)
                    pe.drain().then_inc(acc_free, 1)
                phase_barrier(pe, "pe")

        @block.vector
        def _(dve):
            V = nc.vector
            dve.wait_ge(init, INIT)
            z = [lbz[:, :, j, :] for j in range(DEPTH)]
            m = r3(small[:, 0:16], 8)
            V.tensor_tensor(m, z[0], z[1], ALU.max)
            dve.drain()
            for j in range(DEPTH):
                V.tensor_tensor(z[j], z[j], m, ALU.subtract).then_inc(lb_shifted, j)                    if j else V.tensor_tensor(z[j], z[j], m, ALU.subtract)
            V.tensor_scalar(rows_g[:, :, P:P + HD], rows_g[:, :, P:P + HD], -SCALE, None, ALU.mult)
            dve.wait_ge(lb_exped, 1)
            V.tensor_tensor(m, z[0], z[1], ALU.add)
            V.memset(lbf[:, 0:16], LOG_FLOOR)
            V.tensor_copy(masks[:].rearrange("p n i -> p (n i)"), arena[:, 0:(2 * NL + 1) * P])
            V.memset(omlb[:, 0:16], 1.0)
            dve.drain()
            V.reciprocal(small[:, 0:16], small[:, 0:16])
            dve.drain()
            V.tensor_tensor(r3(lbf[:, 16:32], 8), z[1], m, ALU.mult)
            dve.drain()
            V.tensor_scalar(omlb[:, 16:32], lbf[:, 16:32], -1.0, 1.0, ALU.mult, ALU.add)
            dve.drain()
            V.tensor_scalar(lbf[:, 16:32], lbf[:, 16:32], LOG_FLOOR, None, ALU.add).then_inc(lb_ready, 1)
            dve.drain()

            def inverse_root(n):
                dve.drain().then_inc(var_ready, 1)
                dve.wait_ge(std_ready, 1)
                dve.sem_inc(std_ready, -1)
                V.reciprocal(small[:, 0:n], small[:, 0:n])
                dve.drain()

            def first_norm():
                stats = small[:, 64:64 + NT * 12].rearrange("p (t c s) -> p t c s", t=NT, c=2)
                mv = r3(small[:, 128:128 + 2 * NT], 2)
                for t in range(NT):
                    for c in range(2):
                        V.bn_stats(stats[:, t, c, :], x[:, t, c * 512:(c + 1) * 512])
                dve.drain()
                for t in range(NT):
                    V.bn_aggr(mv[:, t, :], stats[:, t, :, :])
                dve.drain()
                V.tensor_scalar(small[:, 0:NT], mv[:, :, 1:2].rearrange("p t a -> p (t a)"), EPS, None, ALU.add)
                inverse_root(NT)
                for t in range(NT):
                    V.tensor_scalar(x[:, t, :], x[:, t, :], mv[:, t, 0:1], small[:, t:t + 1], ALU.subtract, ALU.mult)
                dve.drain()
                for t in range(NT):
                    V.tensor_tensor(x[:, t, :], x[:, t, :], lnrows[:, 0, :], ALU.mult)
                dve.drain()
                for t in range(NT):
                    V.tensor_tensor(x[:, t, :], x[:, t, :], lnrows[:, 1, :], ALU.add)
                dve.drain()

            def top16(values, indices, source, spare, n, count):
                src, alt = r3(source, n), r3(spare, n)
                for u in range(count):
                    V.max(values[:, u, 0:8], src[:, u, :])
                dve.drain()
                for u in range(count):
                    V.max_index(indices[:, u, 0:8], values[:, u, 0:8], src[:, u, :])
                for u in range(count):
                    V.match_replace(alt[:, u, :], values[:, u, 0:8], src[:, u, :], -3.0e38)
                dve.drain()
                for u in range(count):
                    V.max(values[:, u, 8:16], alt[:, u, :])
                dve.drain()
                for u in range(count):
                    V.max_index(indices[:, u, 8:16], values[:, u, 8:16], alt[:, u, :])
                dve.drain()

            with dve.Fori(0, DEPTH) as l:
                with dve.Fori(0, B_GATE // 2) as i:
                    for s in range(2):
                        dve.wait_ge(to_dve[s], 1)
                        dve.sem_inc(to_dve[s], -1)
                        V.tensor_copy(modrows[:, bass.ds((2 * i + s) * CB, CB)], banks[0:2, s, :]
                                      ).then_inc(bank_free[s], 1)
                dve.drain().then_inc(modrows_ready, 1)
                dve.wait_ge(to_dve[2], 1)
                dve.sem_inc(to_dve[2], -1)
                V.tensor_tensor(modv[:], r3(banks[:, 2, 0:96], 2),
                                bmod[:, bass.ds(l, 1), :].rearrange("p a m -> p (a m)").unsqueeze(2)
                                .to_broadcast([P, 48, 2]), ALU.add).then_inc(bank_free[2], 1)
                dve.drain()
                for part in (SC1, SC2):
                    V.tensor_scalar(modv[:, part * 8:part * 8 + 8, :], modv[:, part * 8:part * 8 + 8, :],
                                    1.0, None, ALU.add)
                phase_barrier(dve, "dve")
                for k in range(KD):
                    b = k % 4
                    dve.wait_ge(to_dve[b], 1)
                    dve.sem_inc(to_dve[b], -1)
                    V.tensor_scalar(hT[:, k, P:T], banks[:, b, :], modv[:, SC1 * 8 + k, 1:2],
                                    modv[:, SH1 * 8 + k, 1:2], ALU.mult, ALU.add).then_inc(bank_free[b], 1)
                phase_barrier(dve, "dve")
                phase_barrier(dve, "dve")

                def decays(b, h):
                    for d in range(2):
                        dve.wait_ge(kneg_ready, 1)
                        dve.sem_inc(kneg_ready, -1)
                        V.tensor_scalar(hk[b][d], hk[b][d], omlb[:, bass.ds((l * 2 + d) * HEADS + h, 1)], None,
                                        ALU.mult)
                    dve.drain()
                    V.tensor_tensor(ksum, hk[b][0], hk[b][1], ALU.add).then_inc(ksum_ready, 1)
                    for d in range(2):
                        dve.wait_ge(log_ready, 1)
                        dve.sem_inc(log_ready, -1)
                        V.tensor_tensor_scan(pre[d].rearrange("p t n -> p (t n)"), reset[:],
                                             gl[d].rearrange("p t n -> p (t n)"), 0.0, ALU.mult, ALU.add
                                             ).then_inc(pre_ready, 1)

                def place(n, bank):
                    dve.wait_ge(to_dve[bank], 1)
                    dve.sem_inc(to_dve[bank], -1)
                    V.copy_predicated(r3(sc, P), masks[:, n:n + 1, :].to_broadcast([P, NT, P]),
                                      r3(pair(bank), P)).then_inc(bank_free[bank], 1)

                def head(b, h, more):
                    q, (kf, kb) = hq[b], hk[b]
                    for n, (d, s) in enumerate(units):
                        lo, up = (kf, q) if d == 0 else (q, kb)
                        v = [y.rearrange("p (b s) -> p b s", s=2 * s) for y in (X[n % 2], E[n % 2], lo, up)]
                        dve.wait_ge(exp_ready[n % 2], 1)
                        dve.sem_inc(exp_ready[n % 2], -1)
                        V.tensor_tensor(v[0][:, :, 0:s], v[1][:, :, 0:s], v[2][:, :, 0:s], ALU.mult)
                        V.tensor_tensor(v[0][:, :, s:2 * s], v[1][:, :, s:2 * s], v[3][:, :, s:2 * s], ALU.mult
                                        ).then_inc(x_ready[n % 2], 1)
                        if n:
                            place(n - 1, 2 - 2 * ((n - 1) % 2))
                        else:
                            place(2 * NL, 0)
                        dve.drain().then_inc(e_free[n % 2], 1)
                    for n, (src, dst) in enumerate([(q, qdec[0]), (kf, X[0]), (q, qdec[1]), (kb, X[1])]):
                        dve.wait_ge(exp_ready[n % 2], 1)
                        dve.sem_inc(exp_ready[n % 2], -1)
                        V.tensor_tensor(dst, E[n % 2], src, ALU.mult).then_inc(e_free[n % 2], 1)
                        if n % 2:
                            dve.drain().then_inc(x_ready[n // 2], 1)
                        if n == 0:
                            place(2 * NL - 1, 0)
                    dve.drain().then_inc(sc_ready, 1)
                    dve.wait_ge(tot_ready, 2)
                    dve.sem_inc(tot_ready, -2)
                    dve.wait_ge(s0_full, 32)
                    dve.sem_inc(s0_full, -32)
                    dve.wait_ge(hnew_sent, 32)
                    dve.sem_inc(hnew_sent, -32)
                    for d in range(2):
                        dve.wait_ge(to_dve[2 - 2 * d], 1)
                        dve.sem_inc(to_dve[2 - 2 * d], -1)
                        added = r3(pair(2 - 2 * d), P)
                        V.tensor_copy(hnew[:, d, :], added[:, 0, :])
                        for n in ([0, 1, 2], [3, 2, 1])[d]:
                            to = n + 1 - 2 * d
                            V.scalar_tensor_tensor(S[d][:, to, :], S[d][:, n, :], tot[:, d, n + 1:n + 2],
                                                   added[:, n + 1, :], ALU.mult, ALU.add)
                            dve.drain()
                        dve.drain().then_inc(bank_free[2 - 2 * d], 1)
                    dve.drain().then_inc(state_ready, 1)
                    dve.drain().then_inc(hnew_ready, 1)
                    if more:
                        decays(1 - b, h + 1)
                    dve.wait_ge(osq_ready, 1)
                    dve.sem_inc(osq_ready, -1)
                    V.tensor_reduce(small[:, 0:NT], r3(osq, P), AX.X, ALU.add)
                    dve.drain()
                    V.tensor_scalar(small[:, 0:NT], small[:, 0:NT], 1.0 / P, EPS, ALU.mult, ALU.add)
                    inverse_root(NT)
                    V.tensor_tensor(r3(o1, P), r3(pair(2), P), small[:, 0:NT].unsqueeze(2).to_broadcast([P, NT, P]),
                                    ALU.mult).then_inc(bank_free[2], 1)
                    dve.drain()
                    V.tensor_tensor(r3(o1, P), r3(o1, P), rows_g[:, bass.ds(l, 1), 0:P].to_broadcast([P, NT, P]),
                                    ALU.mult)
                    dve.drain()
                    V.tensor_tensor(r3(o1, P), r3(o1, P), sgate[:, :, bass.ds(h * P, P)], ALU.mult
                                    ).then_inc(o1_ready, 1)

                decays(0, 0)
                head(0, 0, True)
                with dve.Fori(0, HEADS // 2 - 1) as i:
                    head(1, 2 * i + 1, True)
                    head(0, 2 * i + 2, True)
                head(1, HEADS - 1, False)
                phase_barrier(dve, "dve")
                for c, heads, gain in ((1024, KV, P + HD), (0, 8, P), (512, 8, P)):
                    n = heads * HD
                    dve.wait_ge(qkv_ready, 1)
                    dve.sem_inc(qkv_ready, -1)
                    v = qkv[:, :, c:c + n].rearrange("p t (h d) -> p t h d", d=HD)
                    a, b = (y[:, 0:NT * n].rearrange("p (t h d) -> p t h d", t=NT, d=HD) for y in (nt1, nt2))
                    V.tensor_tensor(a, v, v, ALU.mult)
                    dve.drain()
                    V.tensor_reduce(small[:, 0:NT * heads], r3(nt1[:, 0:NT * n], HD), AX.X, ALU.add)
                    dve.drain()
                    V.tensor_scalar(small[:, 0:NT * heads], small[:, 0:NT * heads], 1.0 / HD, EPS, ALU.mult, ALU.add)
                    inverse_root(NT * heads)
                    V.tensor_tensor(v, v, r3(small[:, 0:NT * heads], heads).unsqueeze(3)
                                    .to_broadcast([P, NT, heads, HD]), ALU.mult)
                    dve.drain()
                    V.tensor_tensor(v, v, rows_g[:, bass.ds(l, 1), gain:gain + HD].unsqueeze(2)
                                    .to_broadcast([P, NT, heads, HD]), ALU.mult)
                    dve.drain()
                    lat = v[:, 1:NT]
                    cs, sn = (y[:].unsqueeze(2).to_broadcast([P, NT - 1, heads, 32]) for y in (cos, sin))
                    V.tensor_tensor(a[:, 1:NT, :, 0:32], lat[:, :, :, 0:32], cs, ALU.mult)
                    V.tensor_tensor(a[:, 1:NT, :, 32:64], lat[:, :, :, 0:32], sn, ALU.mult)
                    V.tensor_tensor(b[:, 1:NT, :, 0:32], lat[:, :, :, 32:64], sn, ALU.mult)
                    V.tensor_tensor(b[:, 1:NT, :, 32:64], lat[:, :, :, 32:64], cs, ALU.mult)
                    dve.drain()
                    V.tensor_tensor(lat[:, :, :, 0:32], a[:, 1:NT, :, 0:32], b[:, 1:NT, :, 0:32], ALU.subtract)
                    V.tensor_tensor(lat[:, :, :, 32:64], a[:, 1:NT, :, 32:64], b[:, 1:NT, :, 32:64], ALU.add)
                    dve.drain()
                    if c == 1024:
                        dve.drain().then_inc(kn_pe, 1)
                        dve.drain().then_inc(kn_act, 1)
                dve.drain().then_inc(qkn_pool, 1)

                def lowest(b, u):
                    c = 2 * (u % 2)
                    dve.wait_ge(to_dve[c], 1)
                    dve.sem_inc(to_dve[c], -1)
                    V.tensor_reduce(low[b][:, u:u + 1], pair(c, P if u % NT == 0 else T), AX.X, ALU.min
                                    ).then_inc(low_ready[u % 2], 1)

                def normalise(b):
                    dve.wait_ge(to_dve[6], 1)
                    dve.sem_inc(to_dve[6], -1)
                    V.reciprocal(psum[b], psum[b])
                    dve.drain()
                    for half in range(2):
                        op = V.tensor_tensor(r3(onorm, P)[:, :, half * HD:(half + 1) * HD],
                                             r3(banks[:, 6 + half, 0:NT * HD], HD),
                                             psum[b][:, half * NT:(half + 1) * NT].unsqueeze(2)
                                             .to_broadcast([P, NT, HD]), ALU.mult)
                    op.then_inc(onorm_ready, 1)

                def att_pair(b, before, more):
                    for u in range(2 * NT):
                        if u % 2:
                            dve.wait_ge(to_dve[4], 1)
                            dve.sem_inc(to_dve[4], -1)
                            n = 1 if u % NT == 0 else NT
                            V.tensor_copy(PT[1][:, 0:n, :], r3(pair(4, n * P), P)).then_inc(bank_free[4], 1)
                            dve.drain().then_inc(pt_ready[1], 1)
                        if u + 2 < 2 * NT:
                            lowest(b, u + 2)
                        elif more:
                            lowest(1 - b, u + 2 - 2 * NT)
                        if u == 0 and before:
                            normalise(1 - b)

                for u in range(2):
                    lowest(0, u)
                att_pair(0, False, True)
                with dve.Fori(0, QH // 4 - 1):
                    att_pair(1, True, True)
                    att_pair(0, True, True)
                att_pair(1, True, False)
                normalise(1)
                phase_barrier(dve, "dve")
                with dve.Fori(0, KD) as n:
                    for f in range(2):
                        dve.wait_ge(sg_ready[f], 1)
                        dve.sem_inc(sg_ready[f], -1)
                        dve.wait_ge(to_dve[4 * f + 2], 1)
                        dve.sem_inc(to_dve[4 * f + 2], -1)
                        V.tensor_tensor(y1, banks[:, 4 * f + 2, 0:HALF], sgA[f], ALU.mult
                                        ).then_inc(bank_free[4 * f + 2], 1)
                        dve.wait_ge(to_dve[4 * f + 3], 1)
                        dve.sem_inc(to_dve[4 * f + 3], -1)
                        V.tensor_tensor(y2, banks[:, 4 * f + 3, 0:HALF], sgB[f], ALU.mult
                                        ).then_inc(bank_free[4 * f + 3], 1)
                        dve.drain().then_inc(sg_free[f], 1)
                        V.tensor_tensor(yT[:, bass.ds(n, 1), f * HALF:(f + 1) * HALF].rearrange("p a n -> p (a n)"),
                                        y1, y2, ALU.add)
                        dve.drain()
                phase_barrier(dve, "dve")
                dve.wait_ge(bc_ready, 1)
                dve.sem_inc(bc_ready, -1)
                for g in range(2 * NT):
                    t, c = g % NT, slice(g // NT * CB, (g // NT + 1) * CB)
                    dve.wait_ge(to_dve[g % 8], 1)
                    dve.sem_inc(to_dve[g % 8], -1)
                    V.tensor_tensor(outtmp, banks[:, g % 8, :], bca[:, min(t, 1), c], ALU.mult
                                    ).then_inc(bank_free[g % 8], 1)
                    dve.drain()
                    V.scalar_tensor_tensor(x[:, t, c], x[:, t, c], ALPHA, outtmp, ALU.mult, ALU.add)
                    dve.drain()
                dve.wait_ge(ln_full, 16)
                dve.sem_inc(ln_full, -16)
                first_norm()
                phase_barrier(dve, "dve")
                for t in range(NT):
                    c = 2 * min(t, 1)
                    V.tensor_tensor(h2[:, t, :], x[:, t, :], bcb[:, c, :], ALU.mult)
                    dve.drain()
                    V.tensor_tensor(h2[:, t, :], h2[:, t, :], bcb[:, c + 1, :], ALU.add).then_inc(h2_ready, 1)
                with dve.Fori(0, 4) as i:
                    for u in range(4):
                        b = 4 + 2 * (u % 2)
                        dve.wait_ge(to_dve[b], 1)
                        dve.sem_inc(to_dve[b], -1)
                        V.tensor_copy(r3(arena[:, 0:10240], 2048)[:, :, bass.ds((i * 4 + u) * NKEYS, NKEYS)],
                                      r3(pair(b), P)).then_inc(bank_free[b], 1)
                phase_barrier(dve, "dve")
                def choose_experts(t):
                    dve.wait_ge(stage_ready, 1)
                    dve.sem_inc(stage_ready, -1)
                    top16(tv, ti.bitcast(U32), stage, work, NKEYS, 2 * PEER_H)
                    V.tensor_copy(tif, ti.bitcast(U32))
                    halves_v = tv.rearrange("p (h a) k -> p h a k", a=2)
                    V.tensor_tensor(stage.rearrange("p (h a b) -> p h a b", h=PEER_H, a=TOPK),
                                    halves_v[:, :, 0, :].unsqueeze(3).to_broadcast([P, PEER_H, TOPK, TOPK]),
                                    halves_v[:, :, 1, :].unsqueeze(2).to_broadcast([P, PEER_H, TOPK, TOPK]), ALU.add)
                    dve.drain()
                    top16(r3(bs, TOPK), r3(bp, TOPK).bitcast(U32), stage, work, TOPK * TOPK, PEER_H)
                    V.tensor_tensor(r3(gate, TOPK), r3(bs, TOPK), r3(bs, TOPK)[:, :, 0:1]
                                    .to_broadcast([P, PEER_H, TOPK]), ALU.subtract)
                    V.tensor_scalar(bq.bitcast(U32), bp.bitcast(U32), 4, None, ALU.logical_shift_right)
                    V.tensor_scalar(bp.bitcast(U32), bp.bitcast(U32), 15, None, ALU.bitwise_and)
                    dve.drain()
                    V.tensor_copy(paf, bq.bitcast(U32))
                    V.tensor_copy(pbf, bp.bitcast(U32))
                    dve.drain()
                    halves_i = tif.rearrange("p (h a) k -> p h a k", a=2)
                    for a, (pos, found) in enumerate([(paf, e1), (pbf, e2)]):
                        V.tensor_tensor(r3(stage, TOPK), pos.unsqueeze(2).to_broadcast([P, SLOTS, TOPK]),
                                        iota[:].unsqueeze(1).to_broadcast([P, SLOTS, TOPK]), ALU.is_equal)
                        dve.drain()
                        one = stage.rearrange("p (h s k) -> p h s k", h=PEER_H, s=TOPK)
                        V.tensor_tensor(one, one, halves_i[:, :, a, :].unsqueeze(2)
                                        .to_broadcast([P, PEER_H, TOPK, TOPK]), ALU.mult)
                        dve.drain()
                        V.tensor_reduce(found, r3(stage, TOPK), AX.X, ALU.add)
                        dve.drain()
                    dve.drain().then_inc(stage_free, 1)
                    V.scalar_tensor_tensor(e1, e1, float(NKEYS), e2, ALU.mult, ALU.add)
                    dve.drain()
                    V.tensor_scalar(arena[:, bass.ds(t * 2048, SLOTS)].bitcast(U32), e1, layer_base[:], None,
                                    ALU.add).then_inc(idx_ready, 1)

                def peer_dve(t, more, c):
                    ht = h2[:, bass.ds(t, 1), :].rearrange("p a n -> p (a n)")
                    with dve.Fori(0, TURNS) as i:
                        for j in range(ROWS):
                            dve.wait_ge(row_full[j], (((l * NT + t) * 2) * TURNS + i + 1) * 16)
                            V.scalar_tensor_tensor(grow[j], grow[j], 1.0, ht, ALU.mult, ALU.mult,
                                                   accum_out=av[:, bass.ds(i * ROWS + j, 1)]
                                                   ).then_inc(row_free[j], 1)
                    dve.drain().then_inc(dots_ready, 1)
                    dve.wait_ge(acc_free, 1)
                    dve.sem_inc(acc_free, -1)
                    V.memset(acc, 0.0).then_inc(acc_zero, 1)
                    dve.wait_ge(softexp_ready, 1)
                    dve.sem_inc(softexp_ready, -1)
                    V.tensor_reduce(gsum, r3(gate, TOPK), AX.X, ALU.add)
                    dve.drain()
                    V.reciprocal(gsum, gsum)
                    dve.drain()
                    V.tensor_tensor(r3(gate, TOPK), r3(gate, TOPK), gsum.unsqueeze(2)
                                    .to_broadcast([P, PEER_H, TOPK]), ALU.mult)
                    dve.drain()
                    dve.wait_ge(gelu_ready, 1)
                    dve.sem_inc(gelu_ready, -1)
                    V.tensor_tensor(wv, av, gate, ALU.mult).then_inc(wv_ready, 1)
                    dve.drain()
                    if more:
                        choose_experts(t + 1)
                    dve.wait_ge(acc_seen, 1)
                    dve.sem_inc(acc_seen, -1)
                    for first, last in ((TURNS_A, TURNS_B), (TURNS_B, TURNS)):
                        with dve.Fori(first, last) as i:
                            for j in sorted(set(ALL_ROWS) - set(PE_ROWS)):
                                dve.wait_ge(row_full[j], (((l * NT + t) * 2 + 1) * TURNS + i + 1) * 16)
                                V.scalar_tensor_tensor(acc, grow[j], wv[:, bass.ds(i * ROWS + j, 1)], acc,
                                                       ALU.mult, ALU.add).then_inc(row_free[j], 1)
                                dve.drain()
                        if first == TURNS_A and c is not None:
                            second_norm(t - 1, c)
                    dve.drain().then_inc(acc_done, 1)

                def second_norm(t, c):
                    xt, yt = (y[:, bass.ds(t, 1), :].rearrange("p a n -> p (a n)") for y in (x, h2))
                    stats, mv = small[:, 64:76], small[:, 128:130]
                    dve.wait_ge(tile_summed, 1)
                    dve.sem_inc(tile_summed, -1)
                    V.tensor_tensor(yt, yt, bca[:, c, :], ALU.mult)
                    dve.drain()
                    V.scalar_tensor_tensor(xt, xt, ALPHA, yt, ALU.mult, ALU.add)
                    dve.drain()
                    for f in range(2):
                        V.bn_stats(stats[:, 6 * f:6 * f + 6], xt[:, f * 512:(f + 1) * 512])
                    dve.drain()
                    V.bn_aggr(mv, r3(stats, 6))
                    dve.drain()
                    V.tensor_scalar(small[:, 0:1], mv[:, 1:2], EPS, None, ALU.add)
                    inverse_root(1)
                    V.tensor_scalar(xt, xt, mv[:, 0:1], small[:, 0:1], ALU.subtract, ALU.mult)
                    dve.drain()
                    V.tensor_tensor(xt, xt, lnrows[:, 2, :], ALU.mult)
                    dve.drain()
                    V.tensor_tensor(xt, xt, lnrows[:, 3, :], ALU.add)

                choose_experts(0)
                peer_dve(0, True, None)
                peer_dve(1, True, 0)
                with dve.Fori(2, NT - 1) as t:
                    peer_dve(t, True, 1)
                peer_dve(NT - 1, False, 1)
                second_norm(NT - 1, 1)
                V.tensor_scalar(layer_base[:], layer_base[:], float(N_EXPERTS), None, ALU.add)
                phase_barrier(dve, "dve")
            dve.wait_ge(hnew_sent, 32)
            dve.drain().then_inc(done, 1)


def level_masks():
    j, i = np.meshgrid(np.arange(P), np.arange(P), indexing="ij")
    out = np.zeros((P, 2 * NL + 1, P), np.float32)
    for n, s in enumerate(LEVELS):
        same = (i // (2 * s)) == (j // (2 * s))
        out[:, 2 * n] = same & (i // s % 2 == 1) & (j // s % 2 == 0)
        out[:, 2 * n + 1] = same & (i // s % 2 == 0) & (j // s % 2 == 1)
    out[:, 2 * NL] = i == j
    return out.reshape(P, (2 * NL + 1) * P)


def rotary_tables():
    t = np.arange(LAT, dtype=np.float32)
    inv = (np.float32(10000.0) ** (-np.arange(HD // 4, dtype=np.float32) / np.float32(HD // 4))).astype(np.float32)
    ang = np.concatenate([np.floor(t / GRID_W)[:, None] * inv, (t % GRID_W)[:, None] * inv], axis=1).astype(np.float32)
    return [np.ascontiguousarray(f(ang).astype(np.float32).reshape(NT - 1, P, 32).transpose(1, 0, 2))
            for f in (np.cos, np.sin)]


def layout(inputs):
    a = {k: np.asarray(v) for k, v in inputs.items()}
    w_in = a["w_in"]
    off = np.cumsum([0, 1024, 1024, 1024, 1024, 1024, 1024, 256, 256, 1024, 1024])
    hq, hff, hfb, hi, hg, aq, ak, av, ga, gb = (w_in[:, :, off[n]:off[n + 1]] for n in range(10))
    order = [h for i in range(4) for kp in range(2) for h in (8 * kp + i, 8 * kp + 4 + i)]
    aq = aq.reshape(DEPTH, D, QH, HD)[:, :, order].reshape(DEPTH, D, D)
    watt = a["w_branch_att"].reshape(DEPTH, QH, HD, D)[:, order].reshape(DEPTH, D, D)
    sk = a["peer_sub_keys"].transpose(0, 4, 1, 2, 3).reshape(DEPTH, P, 2048)

    def block(w):
        return w.reshape(KD, P, CB).transpose(1, 0, 2).reshape(P, KD * CB)

    wblk = np.zeros((DEPTH * NB, P, KD * CB), np.float32)
    for l in range(DEPTH):
        blocks = [a["w_mod"][l][:, j * CB:(j + 1) * CB] for j in range(12)]
        blocks += [hg[l][:, j * CB:(j + 1) * CB] for j in range(2)]
        blocks += [np.concatenate([w[l][:, h * P:(h + 1) * P] for w in (hq, hff, hfb, hi)], 1) for h in range(HEADS)]
        blocks += [np.concatenate([ak[l], av[l]], 1), aq[l][:, 0:CB], aq[l][:, CB:]]
        blocks += [np.concatenate([w[l][:, n * P:(n + 1) * P] for w in (ga, gb, a["w_branch_rec"], watt)], 1)
                   for n in range(KD)]
        blocks += [a["w_out"][l][:, j * CB:(j + 1) * CB] for j in range(2)]
        blocks += [None] + [a["peer_w_query"][l][:, j * CB:(j + 1) * CB] for j in range(4)]
        for n, w in enumerate(blocks):
            if w is None:
                wblk[l * NB + n, :, 0:2048] = sk[l]
            else:
                wblk[l * NB + n] = block(w)
    cos, sin = rotary_tables()
    reset = np.ones((P, NT, 129), np.float32)
    reset[:, :, 0] = 0.0
    return {
        "x_prompt": a["x_prompt"][0], "x_sample": a["x_sample"][0],
        "cond": np.stack([a["c_ctx"], a["c"][0]]).reshape(2, KD, P).transpose(2, 1, 0),
        "bmod": a["b_mod"].reshape(DEPTH, 48, P).transpose(2, 0, 1),
        "lbz": a["hgrn_lb_logits"].reshape(2, DEPTH, HEADS, P).transpose(3, 0, 1, 2),
        "ident": np.eye(P, dtype=np.float32), "cos": cos, "sin": sin,
        "iota": np.tile(np.arange(TOPK, dtype=np.float32), (P, 1)),
        "masks": level_masks(), "reset": reset.reshape(P, NT * 129),
        "hgrn_norm_g": a["hgrn_norm_g"], "q_norm_g": a["q_norm_g"], "k_norm_g": a["k_norm_g"],
        "state": a["state_hgrn"].reshape(DEPTH * 2 * HEADS, P, P),
        "cache_k": a["cache_attn_k"].reshape(DEPTH, P, KV * HD),
        "cache_v": a["cache_attn_v"].reshape(DEPTH, P, KV * HD),
        "lnrows": np.stack([a[n] for n in ("ln1_g", "ln1_b", "ln2_g", "ln2_b")], axis=1),
        "peer_u": a["peer_u"].reshape(DEPTH * N_EXPERTS, D), "peer_v": a["peer_v"].reshape(DEPTH * N_EXPERTS, D),
        "wblk": wblk,
    }


def kernel(**inputs):
    import concourse.bacc as bacc
    from concourse.bass_utils import run_bass_kernel_spmd

    nc = bacc.Bacc("TRN2", target_bir_lowering=False, num_devices=1)
    arrays, ins = {}, {}
    for name, a in layout(inputs).items():
        a = np.ascontiguousarray(a)
        arrays[f"in_{name}"] = a
        ins[name] = nc.dram_tensor(f"in_{name}", a.shape, mybir.dt.from_np(a.dtype), kind="ExternalInput").ap()
    shapes = [(1, P, D), (1, LAT, D), (DEPTH, P, KV * HD), (DEPTH, P, KV * HD), (DEPTH * 2 * HEADS, P, P)]
    outs = [nc.dram_tensor(f"out_{i}", s, F32, kind="ExternalOutput").ap() for i, s in enumerate(shapes)]
    build(nc, ins, outs)
    r = run_bass_kernel_spmd(nc, [arrays], core_ids=[0])
    got = [r.results[0][f"out_{i}"] for i in range(len(shapes))]
    return (got[0], got[1], got[2].reshape(1, DEPTH, P, KV, HD), got[3].reshape(1, DEPTH, P, KV, HD),
            got[4].reshape(1, DEPTH, 2, HEADS, P, P))
```
